# Optimizing a Trainium2 kernel written in Bass

```python
import jax, jax.numpy as jnp
from jax import lax
import numpy as np
import math

D_MODEL = 1024
BATCH = 1
SEQ = 256
DEPTH = 1

GRID_W = 64
N_MEM = 256
EPS = 1e-6

ATT_HEADS = 8
ATT_KV_HEADS = 2
ATT_HEAD_DIM = 64
ATT_WIDTH = ATT_HEADS * ATT_HEAD_DIM
KV_WIDTH = ATT_KV_HEADS * ATT_HEAD_DIM
ROPE_THETA = 10000.0
Q_BLOCK = 128

SGU_GROUPS = 4
SGU_WIDTH = 512
SGU_GROUP_CH = SGU_WIDTH // SGU_GROUPS
SGU_CHUNK = 128

IN_COLS = ATT_WIDTH + 2 * KV_WIDTH + 2 * SGU_WIDTH + 2 * D_MODEL

X_HEADS = 4
X_HEAD_DIM = 128
X_WIDTH = X_HEADS * X_HEAD_DIM

N_GROUPS = 4
EXPERTS_PER_GROUP = 4
N_EXPERTS = N_GROUPS * EXPERTS_PER_GROUP
TOP_K = 2
D_EXPERT = 512


def rms_norm(x, g):
    xf = x.astype(jnp.float32)
    y = xf * lax.rsqrt(jnp.mean(xf * xf, axis=-1, keepdims=True) + EPS)
    return y.astype(x.dtype) * g

def layer_norm(x, g, b):
    xf = x.astype(jnp.float32)
    mu = jnp.mean(xf, axis=-1, keepdims=True)
    xc = xf - mu
    var = jnp.mean(xc * xc, axis=-1, keepdims=True)
    return (xc * lax.rsqrt(var + EPS)).astype(x.dtype) * g + b

def axial_rope_tables(seq_len):
    rows = seq_len // GRID_W
    row_ids = jnp.repeat(jnp.arange(rows), GRID_W).astype(jnp.float32)
    col_ids = jnp.tile(jnp.arange(GRID_W), rows).astype(jnp.float32)
    pairs_per_axis = ATT_HEAD_DIM // 4
    inv_freq = ROPE_THETA ** (-jnp.arange(pairs_per_axis, dtype=jnp.float32) / pairs_per_axis)
    ang = jnp.concatenate([row_ids[:, None] * inv_freq[None, :],
                           col_ids[:, None] * inv_freq[None, :]], axis=-1)
    return jnp.cos(ang), jnp.sin(ang)

def apply_rope(x, cos, sin):
    xf = x.astype(jnp.float32).reshape(*x.shape[:-1], x.shape[-1] // 2, 2)
    x0, x1 = xf[..., 0], xf[..., 1]
    c = cos[None, :, None, :]
    s = sin[None, :, None, :]
    out = jnp.stack([x0 * c - x1 * s, x0 * s + x1 * c], axis=-1).reshape(x.shape)
    return out.astype(x.dtype)

def gqa_attention(q, k, v):
    B, S, _, HD = q.shape
    G = ATT_HEADS // ATT_KV_HEADS
    nb = S // Q_BLOCK
    qb = q.reshape(B, nb, Q_BLOCK, ATT_KV_HEADS, G, HD).transpose(1, 0, 2, 3, 4, 5)
    scale = HD ** -0.5

    def block(q_blk):
        s = jnp.einsum('bqhgd,bkhd->bhgqk', q_blk, k, preferred_element_type=jnp.float32) * scale
        p = jax.nn.softmax(s, axis=-1).astype(v.dtype)
        return jnp.einsum('bhgqk,bkhd->bqhgd', p, v)

    o = lax.map(block, qb)
    return o.transpose(1, 0, 2, 3, 4, 5).reshape(B, S, ATT_WIDTH)

def spatial_gating(u, v, w_s, b_s, ln_g, ln_b):
    B, S, _ = v.shape
    nc = S // SGU_CHUNK
    vn = layer_norm(v, ln_g, ln_b).reshape(B, nc, SGU_CHUNK, SGU_GROUPS, SGU_GROUP_CH)
    vm = jnp.einsum('gpq,bnqgc->bnpgc', w_s, vn) + b_s.T[:, :, None]
    return u * vm.reshape(B, S, SGU_WIDTH)

def memory_cross_attention(h, mem_n, w_cq, w_ckv, w_co):
    B, S, _ = h.shape
    M = mem_n.shape[1]
    q = (h @ w_cq).reshape(B, S, X_HEADS, X_HEAD_DIM)
    kv = mem_n @ w_ckv
    k = kv[..., :X_WIDTH].reshape(B, M, X_HEADS, X_HEAD_DIM)
    v = kv[..., X_WIDTH:].reshape(B, M, X_HEADS, X_HEAD_DIM)
    s = jnp.einsum('bshd,bmhd->bhsm', q, k, preferred_element_type=jnp.float32) * (X_HEAD_DIM ** -0.5)
    p = jax.nn.softmax(s, axis=-1).astype(v.dtype)
    o = jnp.einsum('bhsm,bmhd->bshd', p, v).reshape(B, S, X_WIDTH)
    return o @ w_co

def hierarchical_moe(h, w_rg, b_rg, w_re, b_re, w_gate, w_up, w_down):
    B, S, D = h.shape
    t = h.reshape(B * S, D)
    glog = (t @ w_rg + b_rg).astype(jnp.float32)
    gprob = jax.nn.softmax(glog, axis=-1)
    gval, gidx = lax.top_k(gprob, 1)
    elog = (t @ w_re + b_re).astype(jnp.float32).reshape(-1, N_GROUPS, EXPERTS_PER_GROUP)
    elog_sel = jnp.take_along_axis(elog, gidx[:, :, None], axis=1)[:, 0]
    evals, eidx = lax.top_k(elog_sel, TOP_K)
    ew = jax.nn.softmax(evals, axis=-1) * gval
    expert_id = gidx * EXPERTS_PER_GROUP + eidx
    combine = jnp.sum(jax.nn.one_hot(expert_id, N_EXPERTS, dtype=jnp.float32) * ew[..., None], axis=1)
    combine = combine.astype(t.dtype)
    y = jnp.zeros_like(t)
    for e in range(N_EXPERTS):
        he = jax.nn.silu(t @ w_gate[e]) * (t @ w_up[e])
        y = y + combine[:, e:e + 1] * (he @ w_down[e])
    return y.reshape(B, S, D)

def first_inputs(seed: int = 0) -> dict:
    key = jax.random.key(seed)
    ks = iter(jax.random.split(key, 40))
    L = DEPTH
    f32 = jnp.float32

    def nrm(shape, scale):
        return jax.random.normal(next(ks), shape, f32) * scale

    def gain(shape):
        return 1.0 + 0.1 * jax.random.normal(next(ks), shape, f32)

    return {
        'x': nrm((BATCH, SEQ, D_MODEL), 1.0),
        'mem': nrm((BATCH, N_MEM, D_MODEL), 1.0),
        'g_mix': gain((L, D_MODEL)),
        'w_in': nrm((L, D_MODEL, IN_COLS), D_MODEL ** -0.5),
        'g_q': gain((L, ATT_HEAD_DIM)),
        'g_k': gain((L, ATT_HEAD_DIM)),
        'w_att_out': nrm((L, ATT_WIDTH, D_MODEL), ATT_WIDTH ** -0.5),
        'sgu_ln_g': gain((L, SGU_WIDTH)),
        'sgu_ln_b': nrm((L, SGU_WIDTH), 0.02),
        'w_s': nrm((L, SGU_GROUPS, SGU_CHUNK, SGU_CHUNK), 0.5 * SGU_CHUNK ** -0.5),
        'b_s': 1.0 + nrm((L, SGU_GROUPS, SGU_CHUNK), 0.1),
        'w_sgu_out': nrm((L, SGU_WIDTH, D_MODEL), SGU_WIDTH ** -0.5),
        'w_out': nrm((L, D_MODEL, D_MODEL), D_MODEL ** -0.5),
        'g_cross': gain((L, D_MODEL)),
        'g_mem': gain((L, D_MODEL)),
        'w_cq': nrm((L, D_MODEL, X_WIDTH), D_MODEL ** -0.5),
        'w_ckv': nrm((L, D_MODEL, 2 * X_WIDTH), D_MODEL ** -0.5),
        'w_co': nrm((L, X_WIDTH, D_MODEL), X_WIDTH ** -0.5),
        'g_moe': gain((L, D_MODEL)),
        'w_rg': nrm((L, D_MODEL, N_GROUPS), D_MODEL ** -0.5),
        'b_rg': nrm((L, N_GROUPS), 0.01),
        'w_re': nrm((L, D_MODEL, N_EXPERTS), D_MODEL ** -0.5),
        'b_re': nrm((L, N_EXPERTS), 0.01),
        'w_gate': nrm((L, N_EXPERTS, D_MODEL, D_EXPERT), D_MODEL ** -0.5),
        'w_up': nrm((L, N_EXPERTS, D_MODEL, D_EXPERT), D_MODEL ** -0.5),
        'w_down': nrm((L, N_EXPERTS, D_EXPERT, D_MODEL), D_EXPERT ** -0.5),
        'g_final': gain((D_MODEL,)),
    }

def first_block(x, mem, g_mix, w_in, g_q, g_k, w_att_out, sgu_ln_g, sgu_ln_b, w_s, b_s,
              w_sgu_out, w_out, g_cross, g_mem, w_cq, w_ckv, w_co, g_moe, w_rg, b_rg,
              w_re, b_re, w_gate, w_up, w_down, g_final):
    B, S, _ = x.shape
    cos, sin = axial_rope_tables(S)
    splits = [ATT_WIDTH,
              ATT_WIDTH + KV_WIDTH,
              ATT_WIDTH + 2 * KV_WIDTH,
              ATT_WIDTH + 2 * KV_WIDTH + SGU_WIDTH,
              ATT_WIDTH + 2 * KV_WIDTH + 2 * SGU_WIDTH,
              ATT_WIDTH + 2 * KV_WIDTH + 2 * SGU_WIDTH + D_MODEL]
    for l in range(DEPTH):
        h = rms_norm(x, g_mix[l])
        z = h @ w_in[l]
        q, k, v, su, sv, ga, gb = jnp.split(z, splits, axis=-1)
        q = rms_norm(q.reshape(B, S, ATT_HEADS, ATT_HEAD_DIM), g_q[l])
        k = rms_norm(k.reshape(B, S, ATT_KV_HEADS, ATT_HEAD_DIM), g_k[l])
        q = apply_rope(q, cos, sin)
        k = apply_rope(k, cos, sin)
        v = v.reshape(B, S, ATT_KV_HEADS, ATT_HEAD_DIM)
        y_att = gqa_attention(q, k, v) @ w_att_out[l]
        y_sgu = spatial_gating(jax.nn.gelu(su), jax.nn.gelu(sv), w_s[l], b_s[l],
                               sgu_ln_g[l], sgu_ln_b[l]) @ w_sgu_out[l]
        merged = jax.nn.sigmoid(ga) * y_att + jax.nn.sigmoid(gb) * y_sgu
        x = x + merged @ w_out[l]
        x = x + memory_cross_attention(rms_norm(x, g_cross[l]), rms_norm(mem, g_mem[l]),
                                       w_cq[l], w_ckv[l], w_co[l])
        x = x + hierarchical_moe(rms_norm(x, g_moe[l]), w_rg[l], b_rg[l], w_re[l], b_re[l],
                                 w_gate[l], w_up[l], w_down[l])
    return rms_norm(x, g_final)


DEPTH_2 = 2

N_MIXERS = 4
HEADS_PER_GROUP = 4
GROUP_WIDTH = D_MODEL // N_MIXERS
HD = GROUP_WIDTH // HEADS_PER_GROUP
MIX_WIDTH = N_MIXERS * GROUP_WIDTH

NSA_HEADS = HEADS_PER_GROUP
NSA_CMP_LEN = 32
NSA_CMP_STRIDE = 16
NSA_CMP_HIDDEN = 4 * HD
NSA_SEL_LEN = 64
NSA_TOPK = 16
NSA_WINDOW = 512

DIFF_HEADS = HEADS_PER_GROUP
DIFF_QK_DIM = HD // 2
DIFF_V_DIM = HD

GLA_HEADS = HEADS_PER_GROUP
GLA_DK = HD // 2
GLA_DV = HD
GLA_GATE_RANK = 16
GLA_TAU = 16.0

HG_HEADS = HEADS_PER_GROUP
HG_DK = HD
HG_DV = HD

CHUNK = 64

D_FF = 7 * D_MODEL // 2
N_EXPERTS_2 = 8
D_FF_EXPERT = 7 * D_MODEL // 2
PLE_DIM = 256
NEG = -1e30
BIG = 1e30

IN_SPLITS = (
    NSA_HEADS * HD, HD, HD, HD, HD, HD, HD, NSA_HEADS * 3,
    DIFF_HEADS * 2 * DIFF_QK_DIM, DIFF_HEADS * 2 * DIFF_QK_DIM, DIFF_HEADS * DIFF_V_DIM,
    GLA_HEADS * GLA_DK, GLA_HEADS * GLA_DK, GLA_HEADS * GLA_DV, GLA_GATE_RANK, GLA_HEADS * GLA_DV,
    HG_HEADS * HG_DK, HG_HEADS * HG_DK, HG_HEADS * HG_DV, HG_HEADS * HG_DV,
)
IN_COLS_2 = sum(IN_SPLITS)


def rms_norm_2(x, gain):
    xf = x.astype(jnp.float32)
    y = xf * lax.rsqrt(jnp.mean(xf * xf, axis=-1, keepdims=True) + EPS)
    return (y * gain.astype(jnp.float32)).astype(x.dtype)

def split_cols(u, sizes):
    offsets = np.cumsum(sizes)[:-1].tolist()
    return jnp.split(u, offsets, axis=-1)

def chunked_gated_linear_attention(q, k, v, log_g):
    B, S, H, DK = q.shape
    DV = v.shape[-1]
    n_chunks = S // CHUNK

    def to_chunks(t):
        return t.astype(jnp.float32).reshape(B, n_chunks, CHUNK, H, -1).transpose(1, 0, 3, 2, 4)

    qc, kc, vc = to_chunks(q), to_chunks(k), to_chunks(v)
    bc = jnp.cumsum(to_chunks(log_g), axis=3)
    causal = np.tril(np.ones((CHUNK, CHUNK), dtype=bool))[None, None, :, :, None]

    def step(state, inp):
        q_, k_, v_, b_ = inp
        o_inter = jnp.einsum('bhik,bhkv->bhiv', q_ * jnp.exp(b_), state)
        rel = jnp.where(causal, b_[:, :, :, None, :] - b_[:, :, None, :, :], NEG)
        attn = jnp.einsum('bhik,bhjk,bhijk->bhij', q_, k_, jnp.exp(rel))
        o_intra = jnp.einsum('bhij,bhjv->bhiv', attn, v_)
        b_last = b_[:, :, -1:, :]
        new_state = (jnp.exp(b_last[:, :, 0, :, None]) * state
                     + jnp.einsum('bhjk,bhjv->bhkv', k_ * jnp.exp(b_last - b_), v_))
        return new_state, o_inter + o_intra

    state0 = jnp.zeros((B, H, DK, DV), jnp.float32)
    _, o = lax.scan(step, state0, (qc, kc, vc, bc))
    return o.transpose(1, 0, 3, 2, 4).reshape(B, S, H, DV).astype(v.dtype)

def nsa_attention(q, k_cmp, v_cmp, k_slc, v_slc, k_win, v_win, gate_logits,
                  cmp_pos, cmp_w1, cmp_w2, qk_gain):
    B, S, H, _ = q.shape
    scale = HD ** -0.5
    q = rms_norm_2(q, qk_gain[0])
    t_pos = np.arange(S)

    n_cmp = (S - NSA_CMP_LEN) // NSA_CMP_STRIDE + 1
    cmp_idx = np.arange(n_cmp)[:, None] * NSA_CMP_STRIDE + np.arange(NSA_CMP_LEN)[None, :]

    def compress(t, j):
        blocks = t[:, cmp_idx] + cmp_pos[j]
        hidden = jax.nn.silu(blocks.reshape(B, n_cmp, NSA_CMP_LEN * HD) @ cmp_w1[j])
        return hidden @ cmp_w2[j]

    kc = rms_norm_2(compress(k_cmp, 0), qk_gain[1])
    vc = compress(v_cmp, 1)
    cmp_ok = cmp_idx[:, -1][None, :] <= t_pos[:, None]
    s_c = jnp.einsum('bthd,bnd->bhtn', q, kc).astype(jnp.float32) * scale
    p_c = jax.nn.softmax(jnp.where(cmp_ok, s_c, NEG), axis=-1) * cmp_ok
    o_c = jnp.einsum('bhtn,bnd->bthd', p_c.astype(vc.dtype), vc)

    n_sel = S // NSA_SEL_LEN
    k_sel = min(NSA_TOPK, n_sel)
    sel_start = np.arange(n_sel) * NSA_SEL_LEN
    cmp_start = cmp_idx[:, 0]
    overlap = ((cmp_start[:, None] <= sel_start[None, :] + NSA_SEL_LEN - 1)
               & (cmp_start[:, None] + NSA_CMP_LEN - 1 >= sel_start[None, :])).astype(np.float32)
    importance = jnp.einsum('bhtn,nm->btm', p_c, overlap)
    blk = np.arange(n_sel)[None, :]
    cur = (t_pos // NSA_SEL_LEN)[:, None]
    forced = (blk == 0) | (blk == cur) | (blk == cur - 1)
    importance = jnp.where(forced, BIG,
                           jnp.where(sel_start[None, :] <= t_pos[:, None], importance, NEG))
    _, sel = lax.top_k(lax.stop_gradient(importance), k_sel)

    kb = rms_norm_2(k_slc, qk_gain[2]).reshape(B, n_sel, NSA_SEL_LEN, HD)
    vb = v_slc.reshape(B, n_sel, NSA_SEL_LEN, HD)
    kw_pad = jnp.pad(rms_norm_2(k_win, qk_gain[3]), ((0, 0), (NSA_WINDOW, 0), (0, 0)))
    vw_pad = jnp.pad(v_win, ((0, 0), (NSA_WINDOW, 0), (0, 0)))
    band = NSA_WINDOW + Q_BLOCK
    gather_blocks = jax.vmap(lambda t, i: t[i])

    def block_body(args):
        qb, selb, t0 = args
        tq = t0 + jnp.arange(Q_BLOCK)
        kg = gather_blocks(kb, selb)
        vg = gather_blocks(vb, selb)
        s = jnp.einsum('bqhd,bqnld->bhqnl', qb, kg).astype(jnp.float32) * scale
        kpos = selb[..., None] * NSA_SEL_LEN + jnp.arange(NSA_SEL_LEN)
        s = jnp.where((kpos <= tq[None, :, None, None])[:, None], s, NEG)
        p = jax.nn.softmax(s.reshape(B, H, Q_BLOCK, k_sel * NSA_SEL_LEN), axis=-1).reshape(s.shape)
        o_s = jnp.einsum('bhqnl,bqnld->bqhd', p.astype(vg.dtype), vg)
        kwb = lax.dynamic_slice_in_dim(kw_pad, t0, band, axis=1)
        vwb = lax.dynamic_slice_in_dim(vw_pad, t0, band, axis=1)
        s = jnp.einsum('bqhd,bkd->bhqk', qb, kwb).astype(jnp.float32) * scale
        kp = t0 - NSA_WINDOW + jnp.arange(band)
        m = ((kp[None, :] <= tq[:, None]) & (kp[None, :] > tq[:, None] - NSA_WINDOW)
             & (kp[None, :] >= 0))
        p = jax.nn.softmax(jnp.where(m, s, NEG), axis=-1)
        o_w = jnp.einsum('bhqk,bkd->bqhd', p.astype(vwb.dtype), vwb)
        return o_s, o_w

    nq = S // Q_BLOCK
    qs = q.reshape(B, nq, Q_BLOCK, H, HD).transpose(1, 0, 2, 3, 4)
    sels = sel.reshape(B, nq, Q_BLOCK, k_sel).transpose(1, 0, 2, 3)
    t0s = jnp.arange(nq, dtype=jnp.int32) * Q_BLOCK
    o_s, o_w = lax.map(block_body, (qs, sels, t0s))
    o_s = o_s.transpose(1, 0, 2, 3, 4).reshape(B, S, H, HD)
    o_w = o_w.transpose(1, 0, 2, 3, 4).reshape(B, S, H, HD)

    g = jax.nn.sigmoid(gate_logits.astype(jnp.float32)).reshape(B, S, H, 3).astype(q.dtype)
    o = g[..., 0:1] * o_c + g[..., 1:2] * o_s + g[..., 2:3] * o_w
    return o.reshape(B, S, H * HD)

def diff_attention(q, k, v, qk_gain, lam, sub_gain, layer_idx):
    B, S, H = q.shape[:3]
    q = rms_norm_2(q, qk_gain[0])
    k = rms_norm_2(k, qk_gain[1])
    lam_init = 0.8 - 0.6 * math.exp(-0.3 * layer_idx)
    lam32 = lam.astype(jnp.float32)
    lam_full = (jnp.exp(jnp.sum(lam32[0] * lam32[1])) - jnp.exp(jnp.sum(lam32[2] * lam32[3]))
                + lam_init)
    scale = DIFF_QK_DIM ** -0.5
    outs = []
    for blk in range(S // Q_BLOCK):
        t0, t1 = blk * Q_BLOCK, (blk + 1) * Q_BLOCK
        s = jnp.einsum('bqhcd,bkhcd->bhcqk', q[:, t0:t1], k[:, :t1]).astype(jnp.float32) * scale
        mask = np.arange(t1)[None, :] <= np.arange(t0, t1)[:, None]
        p = jax.nn.softmax(jnp.where(mask, s, NEG), axis=-1)
        w = p[:, :, 0] - lam_full * p[:, :, 1]
        outs.append(jnp.einsum('bhqk,bkhd->bqhd', w.astype(v.dtype), v[:, :t1]))
    o = jnp.concatenate(outs, axis=1)
    o = rms_norm_2(o, sub_gain) * (1.0 - lam_init)
    return o.reshape(B, S, H * DIFF_V_DIM)

def gla_mixer(q, k, v, g_lr, og, w_gate2, b_gate, norm_gain):
    B, S = q.shape[:2]
    log_a = jax.nn.log_sigmoid((g_lr @ w_gate2 + b_gate).astype(jnp.float32)) / GLA_TAU
    shp = (B, S, GLA_HEADS, GLA_DK)
    o = chunked_gated_linear_attention(q.reshape(shp) * (GLA_DK ** -0.5), k.reshape(shp),
                                       v.reshape(B, S, GLA_HEADS, GLA_DV), log_a.reshape(shp))
    o = rms_norm_2(o, norm_gain) * jax.nn.silu(og.reshape(B, S, GLA_HEADS, GLA_DV))
    return o.reshape(B, S, GLA_HEADS * GLA_DV)

def hgrn2_mixer(q, f_pre, i_in, og, lb, norm_gain):
    B, S = q.shape[:2]
    z = f_pre.astype(jnp.float32)
    lb = lb.astype(jnp.float32)
    f = lb + (1.0 - lb) * jax.nn.sigmoid(z)
    log_f = jnp.log(f)
    one_minus_f = (1.0 - lb) * jax.nn.sigmoid(-z)
    shp = (B, S, HG_HEADS, HG_DK)
    o = chunked_gated_linear_attention(q.reshape(shp), one_minus_f.reshape(shp).astype(q.dtype),
                                       i_in.reshape(B, S, HG_HEADS, HG_DV), log_f.reshape(shp))
    o = rms_norm_2(o, norm_gain) * jax.nn.silu(og.reshape(B, S, HG_HEADS, HG_DV))
    return o.reshape(B, S, HG_HEADS * HG_DV)

def swiglu(x, w_gate, w_up, w_down):
    return (jax.nn.silu(x @ w_gate) * (x @ w_up)) @ w_down

def moe_swiglu(x, router, w_gate, w_up, w_down):
    logits = (x @ router).astype(jnp.float32)
    top_val, top_idx = lax.top_k(logits, TOP_K)
    top_w = jax.nn.softmax(top_val, axis=-1)
    combine = jnp.sum(jax.nn.one_hot(top_idx, N_EXPERTS_2, dtype=jnp.float32) * top_w[..., None], axis=-2)
    out = jnp.zeros_like(x)
    for e in range(N_EXPERTS_2):
        out = out + combine[..., e:e + 1].astype(x.dtype) * swiglu(x, w_gate[e], w_up[e], w_down[e])
    return out

def second_inputs(seed: int = 0) -> dict:
    key = jax.random.key(seed)
    keys = iter(jax.random.split(key, 32))

    def nrm(shape, scale):
        return scale * jax.random.normal(next(keys), shape, jnp.float32)

    def gain(shape):
        return 1.0 + 0.02 * jax.random.normal(next(keys), shape, jnp.float32)

    n_dense = (DEPTH_2 + 1) // 2
    n_moe = DEPTH_2 // 2
    return {
        'x': nrm((BATCH, SEQ, D_MODEL), 1.0),
        'p': nrm((DEPTH_2, BATCH, SEQ, PLE_DIM), 1.0),
        'norm_attn': gain((DEPTH_2, D_MODEL)),
        'w_in': nrm((DEPTH_2, D_MODEL, IN_COLS_2), D_MODEL ** -0.5),
        'w_out': nrm((DEPTH_2, MIX_WIDTH, D_MODEL), MIX_WIDTH ** -0.5),
        'nsa_cmp_pos': nrm((DEPTH_2, 2, NSA_CMP_LEN, HD), 0.1),
        'nsa_cmp_w1': nrm((DEPTH_2, 2, NSA_CMP_LEN * HD, NSA_CMP_HIDDEN), (NSA_CMP_LEN * HD) ** -0.5),
        'nsa_cmp_w2': nrm((DEPTH_2, 2, NSA_CMP_HIDDEN, HD), NSA_CMP_HIDDEN ** -0.5),
        'nsa_qk_gain': gain((DEPTH_2, 4, HD)),
        'diff_qk_gain': gain((DEPTH_2, 2, DIFF_QK_DIM)),
        'diff_lambda': nrm((DEPTH_2, 4, DIFF_QK_DIM), 0.1),
        'diff_norm': gain((DEPTH_2, DIFF_V_DIM)),
        'gla_w_gate2': nrm((DEPTH_2, GLA_GATE_RANK, GLA_HEADS * GLA_DK), GLA_GATE_RANK ** -0.5),
        'gla_b_gate': nrm((DEPTH_2, GLA_HEADS * GLA_DK), 0.1),
        'gla_norm': gain((DEPTH_2, GLA_DV)),
        'hgrn_lb_logits': nrm((DEPTH_2, HG_HEADS * HG_DK), 1.0),
        'hgrn_norm': gain((DEPTH_2, HG_DV)),
        'norm_ffn': gain((DEPTH_2, D_MODEL)),
        'ffn_w_gate': nrm((n_dense, D_MODEL, D_FF), D_MODEL ** -0.5),
        'ffn_w_up': nrm((n_dense, D_MODEL, D_FF), D_MODEL ** -0.5),
        'ffn_w_down': nrm((n_dense, D_FF, D_MODEL), D_FF ** -0.5),
        'moe_router': nrm((n_moe, D_MODEL, N_EXPERTS_2), D_MODEL ** -0.5),
        'moe_w_gate': nrm((n_moe, N_EXPERTS_2, D_MODEL, D_FF_EXPERT), D_MODEL ** -0.5),
        'moe_w_up': nrm((n_moe, N_EXPERTS_2, D_MODEL, D_FF_EXPERT), D_MODEL ** -0.5),
        'moe_w_down': nrm((n_moe, N_EXPERTS_2, D_FF_EXPERT, D_MODEL), D_FF_EXPERT ** -0.5),
        'ple_norm': gain((DEPTH_2, D_MODEL)),
        'ple_w_gate': nrm((DEPTH_2, D_MODEL, D_MODEL), D_MODEL ** -0.5),
        'ple_w_proj': nrm((DEPTH_2, PLE_DIM, D_MODEL), PLE_DIM ** -0.5),
    }

def second_block(x, p, norm_attn, w_in, w_out, nsa_cmp_pos, nsa_cmp_w1, nsa_cmp_w2, nsa_qk_gain,
              diff_qk_gain, diff_lambda, diff_norm, gla_w_gate2, gla_b_gate, gla_norm,
              hgrn_lb_logits, hgrn_norm, norm_ffn, ffn_w_gate, ffn_w_up, ffn_w_down,
              moe_router, moe_w_gate, moe_w_up, moe_w_down, ple_norm, ple_w_gate, ple_w_proj):
    B, S, _ = x.shape
    lb_p = jax.nn.softmax(hgrn_lb_logits.astype(jnp.float32), axis=0)
    lower_bounds = jnp.cumsum(lb_p, axis=0) - lb_p[0]
    h = x
    for i in range(DEPTH_2):
        a = rms_norm_2(h, norm_attn[i])
        u = a @ w_in[i]
        (nsa_q, k_cmp, v_cmp, k_slc, v_slc, k_win, v_win, nsa_g,
         d_q, d_k, d_v,
         g_q, g_k, g_v, g_lr, g_og,
         r_q, r_f, r_i, r_og) = split_cols(u, IN_SPLITS)
        o_a = nsa_attention(nsa_q.reshape(B, S, NSA_HEADS, HD), k_cmp, v_cmp, k_slc, v_slc,
                            k_win, v_win, nsa_g, nsa_cmp_pos[i], nsa_cmp_w1[i], nsa_cmp_w2[i],
                            nsa_qk_gain[i])
        o_b = diff_attention(d_q.reshape(B, S, DIFF_HEADS, 2, DIFF_QK_DIM),
                             d_k.reshape(B, S, DIFF_HEADS, 2, DIFF_QK_DIM),
                             d_v.reshape(B, S, DIFF_HEADS, DIFF_V_DIM),
                             diff_qk_gain[i], diff_lambda[i], diff_norm[i], i)
        o_c = gla_mixer(g_q, g_k, g_v, g_lr, g_og, gla_w_gate2[i], gla_b_gate[i], gla_norm[i])
        o_d = hgrn2_mixer(r_q, r_f, r_i, r_og, lower_bounds[i], hgrn_norm[i])
        mix = jnp.concatenate([o_a, o_b, o_c, o_d], axis=-1)
        h = h + mix @ w_out[i]
        c = rms_norm_2(h, norm_ffn[i])
        if i % 2 == 0:
            h = h + swiglu(c, ffn_w_gate[i // 2], ffn_w_up[i // 2], ffn_w_down[i // 2])
        else:
            h = h + moe_swiglu(c, moe_router[i // 2], moe_w_gate[i // 2], moe_w_up[i // 2],
                               moe_w_down[i // 2])
        gate = jax.nn.sigmoid(rms_norm_2(h, ple_norm[i]) @ ple_w_gate[i])
        h = h + (p[i] @ ple_w_proj[i]) * gate
    return h


def setup_inputs(seed=0):
    out = dict(first_inputs(seed))
    for name, value in second_inputs(seed + 1).items():
        if name != "x":
            out[name + "_2"] = value
    return out


def reference(
    x, mem, g_mix, w_in, g_q, g_k, w_att_out, sgu_ln_g, sgu_ln_b, w_s, b_s, w_sgu_out, w_out,
    g_cross, g_mem, w_cq, w_ckv, w_co, g_moe, w_rg, b_rg, w_re, b_re, w_gate, w_up, w_down,
    g_final, p_2, norm_attn_2, w_in_2, w_out_2, nsa_cmp_pos_2, nsa_cmp_w1_2, nsa_cmp_w2_2,
    nsa_qk_gain_2, diff_qk_gain_2, diff_lambda_2, diff_norm_2, gla_w_gate2_2, gla_b_gate_2,
    gla_norm_2, hgrn_lb_logits_2, hgrn_norm_2, norm_ffn_2, ffn_w_gate_2, ffn_w_up_2,
    ffn_w_down_2, moe_router_2, moe_w_gate_2, moe_w_up_2, moe_w_down_2, ple_norm_2,
    ple_w_gate_2, ple_w_proj_2,
):
    x = first_block(
        x, mem, g_mix, w_in, g_q, g_k, w_att_out, sgu_ln_g, sgu_ln_b, w_s, b_s, w_sgu_out,
        w_out, g_cross, g_mem, w_cq, w_ckv, w_co, g_moe, w_rg, b_rg, w_re, b_re, w_gate, w_up,
        w_down, g_final,
    )
    return second_block(
        x, p_2, norm_attn_2, w_in_2, w_out_2, nsa_cmp_pos_2, nsa_cmp_w1_2, nsa_cmp_w2_2,
        nsa_qk_gain_2, diff_qk_gain_2, diff_lambda_2, diff_norm_2, gla_w_gate2_2, gla_b_gate_2,
        gla_norm_2, hgrn_lb_logits_2, hgrn_norm_2, norm_ffn_2, ffn_w_gate_2, ffn_w_up_2,
        ffn_w_down_2, moe_router_2, moe_w_gate_2, moe_w_up_2, moe_w_down_2, ple_norm_2,
        ple_w_gate_2, ple_w_proj_2,
    )


_drawn_inputs = setup_inputs


def setup_inputs(seed=0):
    import zlib

    import numpy as np

    out = dict(_drawn_inputs(seed))
    spreads = {}
    factors = {'nsa_qk_gain_2': 3.591,
     'diff_qk_gain_2': 3.562,
     'gla_norm_2': 2.947,
     'hgrn_norm_2': 3.634,
     'ple_norm_2': 19.249,
     'diff_lambda_2': 2.776,
     'diff_norm_2': 4.055}
    for name, (base, spread) in spreads.items():
        noise = np.random.default_rng([zlib.crc32(name.encode()), seed]).standard_normal(out[name].shape)
        drawn = base * np.exp(spread * noise) if base else spread * noise
        out[name] = __import__('jax').numpy.asarray(drawn.astype(out[name].dtype))
    for name, factor in factors.items():
        out[name] = (out[name] * factor).astype(out[name].dtype)
    return out
```

```python
from contextlib import ExitStack, contextmanager
import math

import numpy as np

import concourse.bass as bass
from concourse import mybir

F32 = mybir.dt.float32
ALU = mybir.AluOpType
ACT = mybir.ActivationFunctionType
AXX = mybir.AxisListType.X

P = 128
SEQ = 256
HALVES = SEQ // P
D = 1024
KT = D // P
EPS = 1e-6
BANK = 512
GRID_W = 64
ATT_HEADS, ATT_KV, HD = 8, 2, 64
SGU_W, SGU_G = 512, 4
X_HEADS, X_HD = 4, 128
N_GROUPS, PER_GROUP = 4, 4
N_EXP1, N_EXP2 = 16, 8
D_FF = 3584
FF = 512
FF_STEPS = D_FF // FF
LAYERS = 2
MH = 4
DIFF_QK = 32
GLA_DK = 32
GLA_RANK = 16
GLA_TAU = 16.0
PLE = 256
CMP_LEN, CMP_STRIDE = 32, 16
N_CMP = (SEQ - CMP_LEN) // CMP_STRIDE + 1
CMP_HID = 4 * HD
NEG = -1e30
LEVELS = [64, 32, 16, 8, 4, 2, 1]
N_LEVELS = len(LEVELS)

IN1 = dict(q=(0, 512), k=(512, 128), v=(640, 128), su=(768, 512), sv=(1280, 512),
           ga=(1792, 1024), gb=(2816, 1024))
IN1_COLS = 3840
IN2_SIZES = dict(nq=256, kc=64, vc=64, ks=64, vs=64, kw=64, vw=64, ng=12, dq=256, dk=256, dv=256,
                 gq=128, gk=128, gv=256, glr=16, gog=256, rq=256, rf=256, ri=256, rog=256)
IN2, _at = {}, 0
for _n, _w in IN2_SIZES.items():
    IN2[_n] = (_at, _w)
    _at += _w
IN2_COLS = _at


def shape_constants():
    cols, parts = {}, []

    def put(name, a):
        a = np.asarray(a, np.float32).reshape(P, -1)
        cols[name] = (sum(x.shape[1] for x in parts), a.shape[1])
        parts.append(a)

    tok = np.arange(SEQ)
    halves = lambda a: np.ascontiguousarray(a.reshape(HALVES, P, -1).transpose(1, 0, 2))
    put("ident", np.eye(P))
    pairs = HD // 4
    inv = (np.float32(10000.0) ** (-np.arange(pairs, dtype=np.float32) / np.float32(pairs))).astype(np.float32)
    ang = np.concatenate([(tok // GRID_W).astype(np.float32)[:, None] * inv,
                          (tok % GRID_W).astype(np.float32)[:, None] * inv], axis=1)
    put("cos", halves(np.cos(ang)))
    put("sin", halves(np.sin(ang)))
    put("causal", halves(np.where(tok[None, :] <= tok[:, None], 0.0, NEG)))
    ok = (np.arange(N_CMP) * CMP_STRIDE + CMP_LEN - 1)[None, :] <= tok[:, None]
    put("cmp_add", halves(np.where(ok, 0.0, NEG)))
    put("cmp_mul", halves(ok.astype(np.float32)))
    t, i = np.arange(P)[:, None], np.arange(P)[None, :]
    sums = []
    for size in LEVELS:
        b = (i // (2 * size)) * 2 * size + size
        sums.append(np.where(i >= b, (t >= b) & (t <= i), (t > i) & (t < b)))
    put("gate_sums", np.stack(sums, 1))
    put("gate_cross", np.stack([t > i, t <= i], 1))
    j = t
    pairs_of = [((j // (2 * s)) == (i // (2 * s))) & ((j % (2 * s)) < s) & ((i % (2 * s)) >= s) for s in LEVELS]
    put("level_mask", np.stack([*pairs_of, i == j], 1))
    put("iota", np.tile(np.arange(16, dtype=np.float32), (P, 1)))
    put("eps", np.full((P, 1), EPS))
    put("ones", np.ones((P, 16)))
    return cols, np.ascontiguousarray(np.concatenate(parts, 1))


class Signal:

    def __init__(self, sem):
        self.sem, self.total, self.base = sem, 0, 0

    def inc(self, ins, by=1):
        ins.then_inc(self.sem, by)
        self.total += by
        return ins

    def at(self, k):
        return self.base + k


class WeightStream:

    SLOTS = 12

    def __init__(self):
        self.slot = 0
        self.loads = []
        self.arrived = [0] * self.SLOTS
        self.freed_at = [0] * self.SLOTS
        self.n_used = 0
        self.taken = 0

    def add(self, parts_of):
        s = self.slot % self.SLOTS
        parts = parts_of(s)
        self.arrived[s] += 16 * len(parts)
        self.loads.append((s, parts, self.freed_at[s], self.arrived[s]))
        self.n_used += 1
        self.freed_at[s] = self.n_used
        self.slot += 1

    def align(self):
        while self.slot % self.SLOTS:
            self.slot += 1


def fused_layers(nc, A, consts_dram, const_cols, out):
    ctx = ExitStack()
    with ctx:
        build(nc, ctx, A, consts_dram, const_cols, out)


def build(nc, ctx, A, consts_dram, const_cols, out):
    def sb(name, shape, stack=ctx):
        return stack.enter_context(nc.sbuf_tensor(name, shape, F32))

    serial = [0]

    def tmp(stack, name, shape):
        serial[0] += 1
        return sb(f"{name}_{serial[0]}", shape, stack)

    signals = {}

    def S(name):
        if name not in signals:
            signals[name] = Signal(ctx.enter_context(nc.semaphore(name)))
        return signals[name]

    @contextmanager
    def stage():
        for s in signals.values():
            s.base = s.total
        with nc.Block() as block:
            yield block

    v, sc, pe = nc.vector, nc.scalar, nc.tensor

    ring = sb("ring", [P, WeightStream.SLOTS, 1024])
    x = sb("x", [P, HALVES, D])
    xT = sb("xT", [P, KT, SEQ])
    consts = sb("consts", [P, consts_dram.shape[1]])

    def const(name):
        a, w = const_cols[name]
        return consts[:, a:a + w]

    ident = const("ident")
    eps = const("eps")
    psum = ctx.enter_context(nc.psum_tensor("psum", [P, 8 * BANK], F32))

    def bank(b, n=1):
        return psum[:, b * BANK:(b + n) * BANK]

    small = []

    def row_param(name, ap):
        t = sb(name, [P, ap.shape[-1]])
        small.append((t[:], ap.partition_broadcast(P)))
        return t

    def col_param(name, ap):
        t = sb(name, [P, KT])
        small.append((t[:], ap))
        return t

    def tile_param(name, shape, ap):
        t = sb(name, shape)
        small.append((t[:], ap))
        return t

    small.append((consts[:], consts_dram))
    small.append((x[:], A["x"][0].rearrange("(h p) d -> p h d", p=P)))
    g_mix, g_cross, g_mem, g_moe = (col_param("c_" + n, A[n][0]) for n in ("g_mix", "g_cross", "g_mem", "g_moe"))
    g_attn2 = [col_param(f"g_attn2_{i}", A["norm_attn_2"][i]) for i in range(LAYERS)]
    g_ffn2 = [col_param(f"g_ffn2_{i}", A["norm_ffn_2"][i]) for i in range(LAYERS)]
    g_ple2 = [col_param(f"g_ple2_{i}", A["ple_norm_2"][i]) for i in range(LAYERS)]
    g_q, g_k = row_param("r_g_q", A["g_q"][0]), row_param("r_g_k", A["g_k"][0])
    b_s = tile_param("b_s", [P, SGU_G], A["b_s"][0])
    w_rg = tile_param("w_rg", [P, KT, N_GROUPS], A["w_rg"][0].rearrange("(k p) n -> p k n", p=P))
    w_re = tile_param("w_re", [P, KT, N_EXP1], A["w_re"][0].rearrange("(k p) n -> p k n", p=P))
    b_rg, b_re = row_param("r_b_rg", A["b_rg"][0]), row_param("r_b_re", A["b_re"][0])
    router2 = tile_param("router2", [P, KT, N_EXP2], A["moe_router_2"][0].rearrange("(k p) n -> p k n", p=P))
    hg_logits = tile_param("hg_logits", [P, LAYERS, 256],
                           A["hgrn_lb_logits_2"].rearrange("l c -> (l c)").partition_broadcast(P)
                           .rearrange("p (l c) -> p l c", l=LAYERS))

    ws = WeightStream()

    def stream_matrix(w):
        k, n = w.shape
        for c in range(0, n, FF):
            width = min(FF, n - c)
            for q in range(k // (2 * P)):
                src = w[q * 2 * P:(q + 1) * 2 * P, c:c + width].rearrange("(a p) n -> p a n", p=P)
                ws.add(lambda s, src=src, width=width: [(slot_tile(s, 2)[:, :, 0:width], src)])

    def slot_tile(s, a):
        return ring[:, s, :].rearrange("p (a n) -> p a n", a=a)

    CMP_PIECES = CMP_LEN // 4

    def stream_cmp(w1):
        for q in range(CMP_PIECES):
            def parts(s, q=q):
                return [(slot_tile(s, 4)[j * HD:(j + 1) * HD],
                         w1[j].rearrange("(l d) h -> d l h", d=HD)[:, 4 * q:4 * q + 4, :]) for j in range(2)]
            ws.add(parts)

    stream_matrix(A["w_in"][0])
    stream_matrix(A["w_att_out"][0])
    stream_matrix(A["w_sgu_out"][0])
    stream_matrix(A["w_out"][0])
    stream_matrix(A["w_cq"][0])
    stream_matrix(A["w_ckv"][0])
    stream_matrix(A["w_co"][0])
    ws.align()

    def stream_experts(gate, up, down, counts):
        assert ws.slot % ws.SLOTS == 0
        n = math.prod(counts)
        first = len(ws.loads)
        ws.loads.append(("experts", gate, up, down, counts, list(ws.freed_at), list(ws.arrived), ws.n_used))
        for s in range(ws.SLOTS):
            ws.arrived[s] += 16 * n
            ws.freed_at[s] = ws.n_used + (n - 1) * ws.SLOTS + s + 1
        ws.n_used += n * ws.SLOTS
        return first

    stream_experts(lambda e: A["w_gate"][0, e], lambda e: A["w_up"][0, e], lambda e: A["w_down"][0, e], [N_EXP1])
    for i in range(LAYERS):
        stream_matrix(A["w_in_2"][i])
        stream_cmp(A["nsa_cmp_w1_2"][i])
        stream_matrix(A["w_out_2"][i])
        ws.align()
        if i % 2 == 0:
            wg = A["ffn_w_gate_2"][0].rearrange("k (c f) -> c k f", f=FF)
            wu = A["ffn_w_up_2"][0].rearrange("k (c f) -> c k f", f=FF)
            wd = A["ffn_w_down_2"][0].rearrange("(c f) d -> c f d", f=FF)
            stream_experts(lambda c, w=wg: w[c], lambda c, w=wu: w[c], lambda c, w=wd: w[c], [FF_STEPS])
        else:
            wg = A["moe_w_gate_2"][0].rearrange("e k (c f) -> e c k f", f=FF)
            wu = A["moe_w_up_2"][0].rearrange("e k (c f) -> e c k f", f=FF)
            wd = A["moe_w_down_2"][0].rearrange("e (c f) d -> e c f d", f=FF)
            stream_experts(lambda e, c, w=wg: w[e, c], lambda e, c, w=wu: w[e, c],
                           lambda e, c, w=wd: w[e, c], [N_EXP2, FF_STEPS])
        stream_matrix(A["ple_w_proj_2"][i])
        stream_matrix(A["ple_w_gate_2"][i])
        ws.align()

    arrived = [ctx.enter_context(nc.semaphore(f"weights_in_slot{s}")) for s in range(ws.SLOTS)]
    used = S("weights_used")
    params_loaded = S("params_loaded")
    flow = {"issued": 0, "load": 0, "took": 0}

    def issue_loads(sp, ahead=WeightStream.SLOTS):
        while flow["load"] < len(ws.loads):
            item = ws.loads[flow["load"]]
            if item[0] == "experts":
                break
            s, parts, freed, _ = item
            if freed > flow["took_end"]:
                break
            if freed:
                sp.wait_ge(used.sem, freed)
            for dst, src in parts:
                sp.dma_start(dst, src).then_inc(arrived[s], 16)
            flow["load"] += 1

    def issue_expert_step(sp, item, index, i):
        _, gate, up, down, _, freed, _, n_used = item
        wg = gate(*index).rearrange("(q a p) f -> q p a f", p=P, a=2)
        wu = up(*index).rearrange("(q a p) f -> q p a f", p=P, a=2)
        wd = down(*index).rearrange("(q p) d -> q p d", p=P)
        for s in range(ws.SLOTS):
            first = isinstance(i, int) and i == 0
            sp.wait_ge(used.sem, freed[s] if first else n_used + (i - 1) * ws.SLOTS + s + 1)
            if s < 8:
                sp.dma_start(slot_tile(s, 2), (wg if s < 4 else wu)[s % 4]).then_inc(arrived[s], 16)
            else:
                sp.dma_start(ring[:, s, :], wd[s - 8]).then_inc(arrived[s], 16)

    def first_expert_step(sp):
        item = ws.loads[flow["load"]] if flow["load"] < len(ws.loads) else (None,)
        if item[0] == "experts" and not flow.get("begun") and max(item[5]) <= flow["took_end"]:
            issue_expert_step(sp, item, [0] * len(item[4]), 0)
            flow["begun"] = True

    pieces = [l for l in ws.loads]

    def take(n):
        got = []
        while len(got) < n:
            item = pieces.pop(0)
            assert item[0] != "experts"
            got.append((item[0], item[3]))
        flow["took"] += n
        flow["took_end"] = flow["took"]
        return got

    flow["took_end"] = 0

    def sync_stage(block):
        @block.sync
        def _(sp):
            issue_loads(sp)
            first_expert_step(sp)

    def transposes(jobs, width, dst, scale=None):
        done, free_v, free_s = S("transposed"), S("bank_copied_dve"), S("bank_copied_act")
        groups = [list(range(i, min(i + 4, len(jobs)))) for i in range(0, len(jobs), 4)]
        with stage() as block:
            sync_stage(block)

            @block.tensor
            def _(e):
                for g, group in enumerate(groups):
                    if g >= 8:
                        f = free_s if g % 2 else free_v
                        e.wait_ge(f.sem, f.at((g - 8) // 2 + 1))
                    for m, n in enumerate(group):
                        last = pe.transpose(psum[0:width, (g % 8) * BANK + m * P:(g % 8) * BANK + (m + 1) * P],
                                            jobs[n], ident)
                    done.inc(last)

            def copy(e, parity, free):
                for g, group in enumerate(groups):
                    if g % 2 != parity:
                        continue
                    e.wait_ge(done.sem, done.at(g + 1))
                    n0, n1 = group[0] * P, (group[-1] + 1) * P
                    b0 = (g % 8) * BANK
                    steps = [(n0, n1)] if scale is None else [(a, a + 2 * P) for a in range(n0, n1, 2 * P)]
                    for a, b in steps:
                        src = psum[0:width, b0 + a - n0:b0 + b - n0]
                        if parity == 0:
                            if scale is None:
                                last = v.tensor_copy(dst[:, a:b], src)
                            else:
                                last = v.tensor_scalar(dst[:, a:b], src, scale[:, a // (2 * P):a // (2 * P) + 1],
                                                       None, ALU.mult)
                        else:
                            k = 1.0 if scale is None else scale[:, a // (2 * P):a // (2 * P) + 1]
                            last = sc.activation(dst[:, a:b], src, ACT.Copy, scale=k)
                    free.inc(last)

            @block.vector
            def _(e):
                copy(e, 0, free_v)

            @block.scalar
            def _(e):
                copy(e, 1, free_s)

    def row_rms(block, src, rinv, junk, ss, rms):
        sq, rms_done = S("squares_summed"), S("rms_done")

        @block.scalar
        def _(e):
            for h in range(HALVES):
                sq.inc(sc.activation(junk[:, h, :], src[:, h, :], ACT.Square, accum_out=ss[:, h:h + 1]))
            e.wait_ge(sq.sem, sq.at(HALVES))
            rms_done.inc(sc.activation(rms, ss, ACT.Sqrt, scale=1.0 / D, bias=eps))

    def normed_T(src, gain, dst):
        with ExitStack() as st:
            xn = tmp(st, "xn", [P, HALVES, D])
            ss, rms, rinv = (tmp(st, n, [P, HALVES]) for n in ("ss", "rms", "rinv"))
            dve = S("dve_chain")
            with stage() as block:
                sync_stage(block)
                row_rms(block, src, rinv, xn, ss[:], rms[:])
                rms_done = S("rms_done")

                @block.vector
                def _(e):
                    e.wait_ge(rms_done.sem, rms_done.at(1))
                    dve.inc(v.reciprocal(rinv[:], rms[:]))
                    e.wait_ge(dve.sem, dve.total)
                    for h in range(HALVES):
                        dve.inc(v.tensor_scalar(xn[:, h, :], src[:, h, :], rinv[:, h:h + 1], None, ALU.mult))
            transposes([xn[:, h, k * P:(k + 1) * P] for k in range(KT) for h in range(HALVES)], P,
                       dst[:].rearrange("p k n -> p (k n)"), scale=gain[:])

    def product(lhsT, kt, cols, copy_to=None, add_to=None):
        chunks = [(c, min(FF, cols - c)) for c in range(0, cols, FF)]
        per = kt // 2
        got = take(per * len(chunks))
        free_v, free_s = S("bank_copied_dve"), S("bank_copied_act")
        with stage() as block:
            sync_stage(block)

            @block.tensor
            def _(e):
                for n, (c, width) in enumerate(chunks):
                    if n >= 4:
                        e.wait_ge(free_v.sem, free_v.at(n - 3))
                        if add_to is None:
                            e.wait_ge(free_s.sem, free_s.at(n - 3))
                    for q in range(per):
                        s, value = got[n * per + q]
                        e.wait_ge(arrived[s], value)
                        w = slot_tile(s, 2)
                        for a in range(2):
                            k = 2 * q + a
                            for h in range(HALVES):
                                last = pe.matmul(bank((2 * n + h) % 8)[:, 0:width], lhsT[:, k, h * P:(h + 1) * P],
                                                 w[:, a, 0:width], start=(k == 0), stop=(k == kt - 1))
                        used.inc(last)

            @block.vector
            def _(e):
                for n, (c, width) in enumerate(chunks):
                    e.wait_ge(used.sem, used.at(per * (n + 1)))
                    if add_to is None:
                        free_v.inc(v.tensor_copy(copy_to[:, 0, c:c + width], bank(2 * n % 8)[:, 0:width]))
                    else:
                        for h in range(HALVES):
                            to = add_to[:, h, c:c + width]
                            last = v.tensor_tensor(to, to, bank((2 * n + h) % 8)[:, 0:width], ALU.add)
                        free_v.inc(last)

            if add_to is None:
                @block.scalar
                def _(e):
                    for n, (c, width) in enumerate(chunks):
                        e.wait_ge(used.sem, used.at(per * (n + 1)))
                        free_s.inc(sc.activation(copy_to[:, 1, c:c + width], bank((2 * n + 1) % 8)[:, 0:width], ACT.Copy))

    def product_T(rhsT, dst):
        got = take(KT // 2)
        copied = S("bank_copied_dve")
        with stage() as block:
            sync_stage(block)

            @block.tensor
            def _(e):
                for q, (s, value) in enumerate(got):
                    e.wait_ge(arrived[s], value)
                    w = slot_tile(s, 2)
                    for a in range(2):
                        k = 2 * q + a
                        for j in range(4):
                            last = pe.matmul(bank(j)[:, 0:SEQ], w[:, a, j * P:(j + 1) * P], rhsT[:, k, :],
                                             start=(k == 0), stop=(k == KT - 1))
                    used.inc(last)

            @block.vector
            def _(e):
                e.wait_ge(used.sem, used.at(KT // 2))
                copied.inc(v.tensor_copy(dst[:], psum[:, 0:4 * BANK].rearrange("p (j n) -> p j n", j=4)[:, :, 0:SEQ]))

    def last_bc(ap, n):
        return ap.unsqueeze(len(ap.shape)).to_broadcast([*ap.shape, n])

    def row_bc(ap, groups):
        for _ in groups:
            ap = ap.unsqueeze(1)
        return ap.to_broadcast([P, *groups, ap.shape[-1]])

    def group_norms(items):
        dve, act, sums, roots = S("dve_chain"), S("act_chain"), S("group_sums"), S("group_roots")
        with ExitStack() as st:
            n = [i[0].shape[2] for i in items]
            sq = [tmp(st, "sq", [P, HALVES, a, i[3]]) for a, i in zip(n, items)]
            ss = [tmp(st, "gss", [P, HALVES, a]) for a in n]
            rt = [tmp(st, "grt", [P, HALVES, a]) for a in n]
            with stage() as block:
                sync_stage(block)

                @block.vector
                def _(e):
                    for (src, _, _, _), q in zip(items, sq):
                        dve.inc(v.tensor_tensor(q[:], src, src, ALU.mult))
                    e.wait_ge(dve.sem, dve.total)
                    for q, s_ in zip(sq, ss):
                        sums.inc(v.tensor_reduce(s_[:], q[:], AXX, ALU.add))
                    for i, (src, dst, gain, d) in enumerate(items):
                        e.wait_ge(roots.sem, roots.at(i + 1))
                        dve.inc(v.reciprocal(ss[i][:], rt[i][:]))
                        e.wait_ge(dve.sem, dve.total)
                        dve.inc(v.tensor_tensor(dst, src, last_bc(ss[i][:], d), ALU.mult))
                        e.wait_ge(dve.sem, dve.total)
                        dve.inc(v.tensor_tensor(dst, dst, row_bc(gain, [HALVES, n[i]]), ALU.mult))

                @block.scalar
                def _(e):
                    for i, (_, _, _, d) in enumerate(items):
                        e.wait_ge(sums.sem, sums.at(i + 1))
                        roots.inc(sc.activation(rt[i][:], ss[i][:], ACT.Sqrt, scale=1.0 / d, bias=eps))

    def attend(heads, n_keys, dv, scale, weight, dst, mask=None, keep=None, accumulate=False):
        nh = len(heads)
        tiles = (n_keys + P - 1) // P
        rows = min(P, n_keys)
        scores, shifted, exped, pT, pT_v, pT_s, o = (S(n) for n in (
            "scores_ready", "scores_shifted", "exp_ready", "probs_transposed", "probsT_dve", "probsT_act", "attended"))
        dve, ready = S("dve_chain"), S("exp_kept")
        kw = n_keys if n_keys < P else SEQ
        with ExitStack() as st:
            E = tmp(st, "E", [P, nh, n_keys])
            PT = tmp(st, "PT", [P, nh * tiles, P])
            mx, rs, ri = (tmp(st, n, [P, nh]) for n in ("mx", "rs", "ri"))
            O = tmp(st, "O", [P, nh, dv])
            sp_ = psum[:, 0:nh * kw].rearrange("p (h k) -> p h k", h=nh)
            tp = psum[:, 4 * BANK:4 * BANK + nh * tiles * P].rearrange("p (h k) -> p h k", k=P)
            op = psum[:, 0:nh * dv].rearrange("p (h k) -> p h k", h=nh)
            groups = [(a, min(a + 4, nh * tiles)) for a in range(0, nh * tiles, 4)]
            with stage() as block:
                sync_stage(block)

                @block.tensor
                def _(e):
                    for h, (qT, kT, _) in enumerate(heads):
                        last = pe.matmul(sp_[:, h, :], qT, kT, start=True, stop=True)
                    scores.inc(last)
                    e.wait_ge(ready.sem, ready.at(1))
                    for a, b in groups:
                        for n in range(a, b):
                            h, k = divmod(n, tiles)
                            last = pe.transpose(tp[0:rows, n, :], E[:, h, k * P:k * P + rows], ident)
                        pT.inc(last)
                    e.wait_ge(pT_v.sem, pT_v.at((len(groups) + 1) // 2))
                    if len(groups) > 1:
                        e.wait_ge(pT_s.sem, pT_s.at(len(groups) // 2))
                    for h, (_, _, vals) in enumerate(heads):
                        for k in range(tiles):
                            last = pe.matmul(op[:, h, :], PT[0:rows, h * tiles + k, :], vals[k],
                                             start=(k == 0), stop=(k == tiles - 1))
                    o.inc(last)

                @block.vector
                def _(e):
                    def step(ins, sig=dve):
                        sig.inc(ins)
                        e.wait_ge(sig.sem, sig.total)
                    e.wait_ge(scores.sem, scores.at(1))
                    if mask is None:
                        step(v.tensor_scalar(E[:], sp_, scale, None, ALU.mult))
                    else:
                        step(v.scalar_tensor_tensor(out=E[:], in0=sp_, scalar=scale, in1=row_bc(mask, [nh]),
                                                    op0=ALU.mult, op1=ALU.add))
                    step(v.tensor_reduce(mx[:], E[:], AXX, ALU.max))
                    step(v.tensor_tensor(E[:], E[:], last_bc(mx[:], n_keys), ALU.subtract), shifted)
                    e.wait_ge(exped.sem, exped.at(1))
                    step(v.tensor_reduce(rs[:], E[:], AXX, ALU.add))
                    if keep is not None:
                        step(v.tensor_tensor(E[:], E[:], row_bc(keep, [nh]), ALU.mult), ready)
                    step(v.reciprocal(ri[:], rs[:]))
                    if weight is not None:
                        weight(step, ri[:])
                    for g, (a, b) in enumerate(groups):
                        if g % 2 == 0:
                            e.wait_ge(pT.sem, pT.at(g + 1))
                            pT_v.inc(v.tensor_copy(PT[0:rows, a:b, :], tp[0:rows, a:b, :]))
                    e.wait_ge(o.sem, o.at(1))
                    if accumulate:
                        step(v.tensor_tensor(O[:], op, last_bc(ri[:], dv), ALU.mult))
                        step(v.tensor_tensor(dst, dst, O[:], ALU.add))
                    else:
                        step(v.tensor_tensor(dst, op, last_bc(ri[:], dv), ALU.mult))

                @block.scalar
                def _(e):
                    e.wait_ge(shifted.sem, shifted.at(1))
                    exped.inc(sc.activation(E[:], E[:], ACT.Exp))
                    if keep is None:
                        e.wait_ge(exped.sem, exped.total)
                        ready.total += 1
                        e.sem_inc(ready.sem, 1)
                    for g, (a, b) in enumerate(groups):
                        if g % 2 == 1:
                            e.wait_ge(pT.sem, pT.at(g + 1))
                            pT_s.inc(sc.activation(PT[0:rows, a:b, :], tp[0:rows, a:b, :], ACT.Copy))

    def expert_steps(combine):
        item = pieces.pop(0)
        assert item[0] == "experts" and ws.loads[flow["load"]] is item and flow["begun"]
        _, _, _, _, counts, _, arr0, used0 = item
        n = math.prod(counts)
        G, U = psum[:, 0:2 * BANK], psum[:, 2 * BANK:4 * BANK]
        silu, hid, y_out = S("silu_ready"), S("hidden_ready"), S("expert_output_added")
        used.base = used.total = used0
        with ExitStack() as st:
            s_g, hT = tmp(st, "silu_g", [P, 4, SEQ]), tmp(st, "hiddenT", [P, 4, SEQ])

            def loop(e, body, ranges, index=(), base=0):
                if not ranges:
                    body(index, base)
                    return
                with e.Fori(0, ranges[0]) as i:
                    loop(e, body, ranges[1:], (*index, i), (base * ranges[0] + i) if index else i)

            for s in signals.values():
                s.base = s.total
            with stage() as block:
                @block.sync
                def _(sp):
                    if len(counts) == 1:
                        with sp.Fori(1, counts[0]) as i:
                            issue_expert_step(sp, item, [i], i)
                    else:
                        with sp.Fori(1, counts[1]) as c:
                            issue_expert_step(sp, item, [0, c], c)
                        with sp.Fori(1, counts[0]) as i:
                            with sp.Fori(0, counts[1]) as c:
                                issue_expert_step(sp, item, [i, c], i * counts[1] + c)
                    flow["load"] += 1
                    flow["begun"] = False
                    flow["took"] = flow["took_end"] = used0 + n * ws.SLOTS
                    issue_loads(sp)
                    first_expert_step(sp)

                @block.tensor
                def _(e):
                    def body(index, i):
                        for part, psum_part in enumerate((G, U)):
                            for q in range(4):
                                s = 4 * part + q
                                e.wait_ge(arrived[s], i * 16 + (arr0[s] + 16))
                                w = slot_tile(s, 2)
                                for a in range(2):
                                    k = 2 * q + a
                                    for j in range(4):
                                        last = pe.matmul(psum_part[:, j * SEQ:(j + 1) * SEQ], w[:, a, j * P:(j + 1) * P],
                                                         xT[:, k, :], start=(k == 0 and j % 2 == 0),
                                                         stop=(k == KT - 1 and j % 2 == 1))
                                last.then_inc(used.sem, 1)
                        for j in range(4):
                            s = 8 + j
                            e.wait_ge(hid.sem, i * 4 + hid.at(j + 1))
                            e.wait_ge(arrived[s], i * 16 + (arr0[s] + 16))
                            if j == 0:
                                e.wait_ge(y_out.sem, i + y_out.at(0))
                            for h in range(HALVES):
                                for c in range(2):
                                    last = pe.matmul(bank(4 + 2 * h + c), hT[:, j, h * P:(h + 1) * P],
                                                     ring[:, s, c * BANK:(c + 1) * BANK], start=(j == 0), stop=(j == 3))
                            last.then_inc(used.sem, 1)
                    loop(e, body, counts)

                @block.scalar
                def _(e):
                    def body(index, i):
                        e.wait_ge(used.sem, i * ws.SLOTS + (used0 + 4))
                        sc.activation(s_g[:].rearrange("p j n -> p (j n)"), G, ACT.Silu).then_inc(silu.sem, 1)
                    loop(e, body, counts)

                @block.vector
                def _(e):
                    def body(index, i):
                        e.wait_ge(used.sem, i * ws.SLOTS + (used0 + 8))
                        e.wait_ge(silu.sem, i + silu.at(1))
                        for j in range(4):
                            v.tensor_tensor(hT[:, j, :], s_g[:, j, :], U[:, j * SEQ:(j + 1) * SEQ], ALU.mult) \
                                .then_inc(hid.sem, 1)
                        e.wait_ge(used.sem, i * ws.SLOTS + (used0 + 12))
                        for h in range(HALVES):
                            last = v.scalar_tensor_tensor(
                                out=x[:, h, :], in0=psum[:, (4 + 2 * h) * BANK:(6 + 2 * h) * BANK],
                                scalar=combine(h, index), in1=x[:, h, :], op0=ALU.mult, op1=ALU.add)
                        last.then_inc(y_out.sem, 1)
                        e.wait_ge(y_out.sem, i + y_out.at(1))
                    loop(e, body, counts)
        used.total += n * ws.SLOTS
        silu.total += n
        hid.total += 4 * n
        y_out.total += n

    def route(jobs, finish):
        done = S("router_ready")
        with stage() as block:
            sync_stage(block)

            @block.tensor
            def _(e):
                for w, c, n in jobs:
                    for h in range(HALVES):
                        for k in range(KT):
                            last = pe.matmul(bank(h)[:, c:c + n], xT[:, k, h * P:(h + 1) * P], w[:, k, :],
                                             start=(k == 0), stop=(k == KT - 1))
                done.inc(last)

            finish(block, done)

    logits_psum = psum[:, 0:HALVES * BANK].rearrange("p (h c) -> p h c", h=HALVES)

    def make_step(e):
        dve = S("dve_chain")

        def step(ins, sig=dve):
            sig.inc(ins)
            e.wait_ge(sig.sem, sig.total)
        return step

    def pick(step, scores, n, best, cand, idx, onehot):
        step(v.tensor_reduce(best, scores, AXX, ALU.max))
        step(v.tensor_tensor(cand, scores, last_bc(best, n), ALU.is_equal))
        step(v.scalar_tensor_tensor(out=cand, in0=cand, scalar=-64.0, in1=row_bc(const("iota")[:, 0:n], [HALVES]),
                                    op0=ALU.mult, op1=ALU.add))
        step(v.tensor_reduce(idx, cand, AXX, ALU.min))
        step(v.tensor_tensor(onehot, cand, last_bc(idx, n), ALU.is_equal))

    def top_two_weights(e, step, scores, n, out_w, t, other=None):
        best1, best2, idx, cand, one1, one2, left = t
        diff_ready, diff_exp = S("top_two_difference"), S("top_two_exp")
        pick(step, scores, n, best1, cand, idx, one1)
        step(v.scalar_tensor_tensor(out=left, in0=one1, scalar=-3e38, in1=scores, op0=ALU.mult, op1=ALU.add))
        pick(step, left, n, best2, cand, idx, one2)
        step(v.tensor_tensor(best2, best2, best1, ALU.subtract), diff_ready)
        e.wait_ge(diff_exp.sem, diff_exp.at(1))
        step(v.tensor_scalar(best1, best2, 1.0, None, ALU.add))
        step(v.reciprocal(best1, best1))
        step(v.tensor_tensor(best2, best2, best1, ALU.mult))
        if other is not None:
            step(v.tensor_tensor(best1, best1, other, ALU.mult))
            step(v.tensor_tensor(best2, best2, other, ALU.mult))
        step(v.tensor_tensor(one1, one1, last_bc(best1, n), ALU.mult))
        step(v.tensor_tensor(one2, one2, last_bc(best2, n), ALU.mult))
        step(v.tensor_tensor(out_w, one1, one2, ALU.add))

    def hybrid_mixers(layer, L2):
        loads = []

        def par(name, shape, src):
            t = tmp(L2, name, shape)
            loads.append((t, src))
            return t

        qk_gain = par("nsa_gain", [P, 4, HD], A["nsa_qk_gain_2"][layer].rearrange("a d -> (a d)").partition_broadcast(P)
                      .rearrange("p (a d) -> p a d", a=4))
        d_gain = par("diff_gain", [P, 2, DIFF_QK], A["diff_qk_gain_2"][layer].rearrange("a d -> (a d)").partition_broadcast(P)
                     .rearrange("p (a d) -> p a d", a=2))
        lam_p = par("diff_lambda", [P, 4, DIFF_QK], A["diff_lambda_2"][layer].rearrange("a d -> (a d)").partition_broadcast(P)
                    .rearrange("p (a d) -> p a d", a=4))
        d_norm = par("diff_norm", [P, HD], A["diff_norm_2"][layer].partition_broadcast(P))
        w_gate2 = par("gla_w_gate2", [GLA_RANK, MH * GLA_DK], A["gla_w_gate2_2"][layer])
        b_gate = par("gla_b_gate", [P, MH * GLA_DK], A["gla_b_gate_2"][layer].partition_broadcast(P))
        gla_gain = par("gla_gain", [P, HD], A["gla_norm_2"][layer].partition_broadcast(P))
        hg_gain = par("hgrn_gain", [P, HD], A["hgrn_norm_2"][layer].partition_broadcast(P))
        cmp_w2 = par("cmp_w2", [P, 2, 2, HD], A["nsa_cmp_w2_2"][layer].rearrange("j (c p) d -> p j c d", p=P))
        pos = tmp(L2, "cmp_pos", [P, CMP_LEN])
        u = tmp(L2, "u2", [P, HALVES, IN2_COLS])
        mix = tmp(L2, "mix", [P, HALVES, D])
        lam = tmp(L2, "lam", [P, 2])
        lam_init = 0.8 - 0.6 * math.exp(-0.3 * layer)
        with stage() as block:
            @block.sync
            def _(sp):
                for dst, src in loads:
                    params_loaded.inc(sp.dma_start(dst[:], src), 16)
                for j in range(2):
                    params_loaded.inc(sp.dma_start(pos[j * HD:(j + 1) * HD, :],
                                                   A["nsa_cmp_pos_2"][layer, j]), 16)
                issue_loads(sp)
                sp.wait_ge(params_loaded.sem, params_loaded.total)
        normed_T(x, g_attn2[layer], xT)
        product(xT, KT, IN2_COLS, copy_to=u)

        def uc(name, lo=0, width=None):
            a, w = IN2[name]
            return u[:, :, a + lo:a + (w if width is None else lo + width)]

        def heads_of(ap, d):
            return ap.rearrange("p h (n d) -> p h n d", d=d)

        with ExitStack() as st:
            nq = tmp(st, "nq", [P, HALVES, MH, HD])
            nks = tmp(st, "nks", [P, HALVES, 1, HD])
            nkw = tmp(st, "nkw", [P, HALVES, 1, HD])
            group_norms([(heads_of(uc("nq"), HD), nq[:], qk_gain[:, 0, :], HD),
                         (heads_of(uc("ks"), HD), nks[:], qk_gain[:, 2, :], HD),
                         (heads_of(uc("kw"), HD), nkw[:], qk_gain[:, 3, :], HD)])
            qT = tmp(st, "nqT", [HD, MH + 2, SEQ])
            transposes([nq[:, h, n, :] for n in range(MH) for h in range(HALVES)]
                       + [k[:, h, 0, :] for k in (nks, nkw) for h in range(HALVES)], HD,
                       qT[:].rearrange("p n t -> p (n t)"))
            kvT = tmp(st, "kvT", [P, SEQ])
            a0 = IN2["kc"][0]
            transposes([u[:, h, a0:a0 + 2 * HD] for h in range(HALVES)], P, kvT[:])
            blocks = tmp(st, "cmp_blocks", [P, CMP_LEN, N_CMP])
            hid, hid_e = (tmp(st, n, [N_CMP, 2, CMP_HID]) for n in ("cmp_hid", "cmp_sig"))
            hidT = tmp(st, "cmp_hidT", [P, 4, N_CMP])
            ckv = tmp(st, "ckv", [N_CMP, 2, HD])
            csq, css, crt = tmp(st, "csq", [N_CMP, HD]), tmp(st, "css", [N_CMP, 1]), tmp(st, "crt", [N_CMP, 1])
            ckT = tmp(st, "ckT", [HD, N_CMP])
            got = take(CMP_PIECES)
            ready, sig, act_hid, hT, hTc, out2, ssr, root, kn, knT = (S(n) for n in (
                "blocks_ready", "hidden_sigmoid", "hidden_active", "hidden_transposed", "hiddenT_copied",
                "compressed_ready", "group_sums", "group_roots", "key_normed", "key_transposed"))
            with stage() as block:
                sync_stage(block)

                @block.vector
                def _(e):
                    step = make_step(e)
                    for l in range(CMP_LEN):
                        last = v.tensor_scalar(blocks[:, l, :], kvT[:, l:l + CMP_STRIDE * (N_CMP - 1) + 1:CMP_STRIDE],
                                               pos[:, l:l + 1], None, ALU.add)
                    ready.inc(last)
                    e.wait_ge(sig.sem, sig.at(2))
                    for j in range(2):
                        last = v.tensor_tensor(hid[:, j, :], bank(j)[0:N_CMP, 0:CMP_HID], hid_e[:, j, :], ALU.mult)
                    act_hid.inc(last)
                    e.wait_ge(hT.sem, hT.at(1))
                    hTc.inc(v.tensor_copy(hidT[:], bank(2)[:, 0:4 * P].rearrange("p (n k) -> p n k", n=4)[:, :, 0:N_CMP]))
                    e.wait_ge(out2.sem, out2.at(1))
                    step(v.tensor_copy(ckv[:], bank(3)[0:N_CMP, 0:2 * HD].rearrange("p (j d) -> p j d", j=2)))
                    step(v.tensor_tensor(csq[:], ckv[:, 0, :], ckv[:, 0, :], ALU.mult))
                    step(v.tensor_reduce(css[:], csq[:], AXX, ALU.add), ssr)
                    e.wait_ge(root.sem, root.at(1))
                    step(v.reciprocal(css[:], crt[:]))
                    step(v.tensor_scalar(csq[:], ckv[:, 0, :], css[:], None, ALU.mult))
                    step(v.tensor_tensor(csq[:], csq[:], qk_gain[0:N_CMP, 1, :], ALU.mult), kn)
                    e.wait_ge(knT.sem, knT.at(1))
                    step(v.tensor_copy(ckT[:], bank(4)[0:HD, 0:N_CMP]))

                @block.scalar
                def _(e):
                    e.wait_ge(used.sem, used.at(CMP_PIECES))
                    for j in range(2):
                        sig.inc(sc.activation(hid_e[:, j, :], bank(j)[0:N_CMP, 0:CMP_HID], ACT.Sigmoid))
                    e.wait_ge(ssr.sem, ssr.at(1))
                    root.inc(sc.activation(crt[:], css[:], ACT.Sqrt, scale=1.0 / HD, bias=eps[0:N_CMP, :]))

                @block.tensor
                def _(e):
                    e.wait_ge(ready.sem, ready.at(1))
                    for q, (s, value) in enumerate(got):
                        e.wait_ge(arrived[s], value)
                        for a in range(4):
                            l = 4 * q + a
                            for j in range(2):
                                rows = slice(j * HD, (j + 1) * HD)
                                last = pe.matmul(bank(j)[0:N_CMP, 0:CMP_HID], blocks[rows, l, :], slot_tile(s, 4)[rows, a, :],
                                                 start=(l == 0), stop=(l == CMP_LEN - 1))
                        used.inc(last)
                    e.wait_ge(act_hid.sem, act_hid.at(1))
                    for n in range(4):
                        last = pe.transpose(bank(2)[:, n * P:n * P + N_CMP], hid[:, n // 2, (n % 2) * P:(n % 2 + 1) * P],
                                            ident[0:N_CMP, 0:N_CMP])
                    hT.inc(last)
                    e.wait_ge(hTc.sem, hTc.at(1))
                    for j in range(2):
                        for c in range(2):
                            last = pe.matmul(bank(3)[0:N_CMP, j * HD:(j + 1) * HD], hidT[:, 2 * j + c, :], cmp_w2[:, j, c, :],
                                             start=(c == 0), stop=(c == 1))
                    out2.inc(last)
                    e.wait_ge(kn.sem, kn.at(1))
                    knT.inc(pe.transpose(bank(4)[0:HD, 0:N_CMP], csq[:], ident[0:N_CMP, 0:N_CMP]))
            gate = tmp(st, "nsa_gate", [P, HALVES, MH, 3])
            gates = S("gates_ready")
            with stage() as block:
                sync_stage(block)

                @block.scalar
                def _(e):
                    gates.inc(sc.activation(gate[:], uc("ng").rearrange("p h (n b) -> p h n b", b=3), ACT.Sigmoid))
            for h in range(HALVES):
                dst = mix[:, h, 0:MH * HD].rearrange("p (n d) -> p n d", d=HD)

                def weight(b, h=h):
                    return lambda step, r: step(v.tensor_tensor(r, r, gate[:, h, :, b], ALU.mult))
                qs = [qT[:, n, h * P:(h + 1) * P] for n in range(MH)]
                attend([(q, ckT[:], [ckv[:, 1, :]]) for q in qs], N_CMP, HD, HD ** -0.5, weight(0), dst,
                       mask=const("cmp_add")[:, h * N_CMP:(h + 1) * N_CMP],
                       keep=const("cmp_mul")[:, h * N_CMP:(h + 1) * N_CMP])
                for b, keys, vals in ((1, MH, "vs"), (2, MH + 1, "vw")):
                    attend([(q, qT[:, keys, :], [uc(vals)[:, k, :] for k in range(HALVES)]) for q in qs], SEQ, HD,
                           HD ** -0.5, weight(b), dst, mask=const("causal")[:, h * SEQ:(h + 1) * SEQ], accumulate=True)

        with ExitStack() as st:
            n2 = 2 * MH
            dq, dk = (tmp(st, n, [P, HALVES, n2, DIFF_QK]) for n in ("dq", "dk"))
            group_norms([(heads_of(uc("dq"), DIFF_QK), dq[:], d_gain[:, 0, :], DIFF_QK),
                         (heads_of(uc("dk"), DIFF_QK), dk[:], d_gain[:, 1, :], DIFF_QK)])
            dqT, dkT = (tmp(st, n, [DIFF_QK, n2, SEQ]) for n in ("dqT", "dkT"))
            for src, dst in ((dq, dqT), (dk, dkT)):
                transposes([src[:, h, n, :] for n in range(n2) for h in range(HALVES)], DIFF_QK,
                           dst[:].rearrange("p n t -> p (n t)"))
            prod, dots = tmp(st, "lam_prod", [P, 2, DIFF_QK]), tmp(st, "lam_dots", [P, 2])
            dots_ready, exp_ready = S("group_sums"), S("exp_ready")
            with stage() as block:
                sync_stage(block)

                @block.vector
                def _(e):
                    step = make_step(e)
                    pairs = lam_p[:].rearrange("p (a two) d -> p a two d", two=2)
                    step(v.tensor_tensor(prod[:], pairs[:, :, 0, :], pairs[:, :, 1, :], ALU.mult))
                    step(v.tensor_reduce(dots[:], prod[:], AXX, ALU.add), dots_ready)
                    e.wait_ge(exp_ready.sem, exp_ready.at(1))
                    step(v.tensor_tensor(lam[:, 0:1], dots[:, 1:2], dots[:, 0:1], ALU.subtract))
                    step(v.tensor_scalar(lam[:, 0:1], lam[:, 0:1], -lam_init, None, ALU.add))

                @block.scalar
                def _(e):
                    e.wait_ge(dots_ready.sem, dots_ready.at(1))
                    exp_ready.inc(sc.activation(dots[:], dots[:], ACT.Exp))
            o8 = tmp(st, "o8", [P, HALVES, n2, HD])
            for h in range(HALVES):
                def weight(step, r):
                    second = r.rearrange("p (n c) -> p n c", c=2)[:, :, 1]
                    step(v.tensor_scalar(second, second, lam[:, 0:1], None, ALU.mult))
                attend([(dqT[:, n, h * P:(h + 1) * P], dkT[:, n, :],
                         [uc("dv", (n // 2) * HD, HD)[:, k, :] for k in range(HALVES)]) for n in range(n2)],
                       SEQ, HD, DIFF_QK ** -0.5, weight, o8[:, h, :, :],
                       mask=const("causal")[:, h * SEQ:(h + 1) * SEQ])
            od = tmp(st, "od", [P, HALVES, MH, HD])
            dve = S("dve_chain")
            with stage() as block:
                sync_stage(block)

                @block.vector
                def _(e):
                    for h in range(HALVES):
                        both = o8[:, h, :, :].rearrange("p (n c) d -> p n c d", c=2)
                        dve.inc(v.tensor_tensor(od[:, h, :, :], both[:, :, 0, :], both[:, :, 1, :], ALU.add))
                    dve.inc(v.tensor_scalar(d_norm[:], d_norm[:], 1.0 - lam_init, None, ALU.mult))
            group_norms([(od[:], heads_of(mix[:, :, 256:512], HD), d_norm[:], HD)])

        def linear_attention(q, k, log_g, vals, groups, dk, dst):
            nh = P // dk
            with ExitStack() as st:
                qkT = tmp(st, "qkT", [P, 2, SEQ])
                decay = tmp(st, "decay", [P, N_LEVELS + 1, P])
                QD = tmp(st, "QD", [P, HALVES, N_LEVELS + 2, P])
                KD = tmp(st, "KD", [P, HALVES, N_LEVELS + 2, P])
                pairs = tmp(st, "pairs", [P, 2, N_LEVELS + 1, P])
                cross = tmp(st, "cross", [P, 2, P])
                for g in range(groups):
                    cols = slice(g * P, (g + 1) * P)
                    transposes([a[:, h, cols] for a in (q, k) for h in range(HALVES)], P,
                               qkT[:].rearrange("p a t -> p (a t)"))
                    exps, exped, dve, decayed = S("exponents_ready"), S("exp_ready"), S("dve_chain"), S("decayed")
                    with stage() as block:
                        sync_stage(block)

                        @block.tensor
                        def _(e):
                            for h in range(HALVES):
                                if h:
                                    e.wait_ge(exped.sem, exped.at(h))
                                pe.matmul(bank(0), log_g[:, h, cols], const("gate_sums")[:, 0:4 * P], start=True, stop=True)
                                pe.matmul(bank(1)[:, 0:3 * P], log_g[:, h, cols], const("gate_sums")[:, 4 * P:7 * P],
                                          start=True, stop=True)
                                exps.inc(pe.matmul(bank(1)[:, 3 * P:4 * P], log_g[:, h, cols],
                                                   const("gate_cross")[:, h * P:(h + 1) * P], start=True, stop=True))

                        @block.scalar
                        def _(e):
                            for h in range(HALVES):
                                e.wait_ge(exps.sem, exps.at(h + 1))
                                if h:
                                    e.wait_ge(decayed.sem, decayed.at(h))
                                exped.inc(sc.activation(decay[:].rearrange("p l t -> p (l t)"), bank(0, 2), ACT.Exp))

                        @block.vector
                        def _(e):
                            for h in range(HALVES):
                                tok = slice(h * P, (h + 1) * P)
                                v.tensor_copy(QD[:, h, N_LEVELS + 1, :], qkT[:, 0, tok])
                                dve.inc(v.tensor_copy(KD[:, h, N_LEVELS + 1, :], qkT[:, 1, tok]))
                                e.wait_ge(exped.sem, exped.at(h + 1))
                                for a, to in ((0, QD), (1, KD)):
                                    last = v.tensor_tensor(to[:, h, 0:N_LEVELS + 1, :], decay[:],
                                                           row_bc(qkT[:, a, tok], [N_LEVELS + 1]), ALU.mult)
                                decayed.inc(last)
                    in_half = [*range(N_LEVELS), N_LEVELS + 1]
                    ready, masked, masked_a, o, taken_o = (S(n) for n in (
                        "pairs_ready", "pairs_masked", "cross_copied", "attended", "output_copied"))
                    jobs = [(h, n) for h in range(HALVES) for n in range(nh)]
                    with stage() as block:
                        sync_stage(block)

                        @block.tensor
                        def _(e):
                            def pv(m):
                                h, n = jobs[m]
                                e.wait_ge(masked.sem, masked.at(m + 1))
                                if h:
                                    e.wait_ge(masked_a.sem, masked_a.at(m - nh + 1))
                                if m >= 2:
                                    e.wait_ge(taken_o.sem, taken_o.at(m - 1))
                                to = bank(6 + m % 2)[:, 0:HD]
                                va = [vals[:, hh, (g * nh + n) * HD:(g * nh + n + 1) * HD] for hh in range(HALVES)]
                                for l in range(N_LEVELS + 1):
                                    last = pe.matmul(to, pairs[:, m % 2, l, :], va[h], start=(l == 0),
                                                     stop=(l == N_LEVELS and h == 0))
                                if h:
                                    last = pe.matmul(to, cross[:, m % 2, :], va[0], start=False, stop=True)
                                o.inc(last)

                            for m, (h, n) in enumerate(jobs):
                                ch = slice(n * dk, (n + 1) * dk)
                                if m >= 2:
                                    e.wait_ge(masked.sem, masked.at(m - 1))
                                    if h and m - 2 >= nh:
                                        e.wait_ge(masked_a.sem, masked_a.at(m - 1 - nh))
                                for s, l in enumerate(in_half):
                                    last = pe.matmul(psum[:, (m % 2) * 2 * BANK + s * P:(m % 2) * 2 * BANK + (s + 1) * P],
                                                     KD[ch, h, l, :], QD[ch, h, l, :], start=True, stop=True)
                                if h:
                                    last = pe.matmul(bank(4 + m % 2)[:, 0:P], KD[ch, 0, N_LEVELS, :],
                                                     QD[ch, 1, N_LEVELS, :], start=True, stop=True)
                                ready.inc(last)
                                if m:
                                    pv(m - 1)
                            pv(len(jobs) - 1)

                        @block.vector
                        def _(e):
                            def take_out(m):
                                h, n = jobs[m]
                                e.wait_ge(o.sem, o.at(m + 1))
                                taken_o.inc(v.tensor_copy(dst[:, h, g * nh + n, :], bank(6 + m % 2)[:, 0:HD]))

                            for m, (h, n) in enumerate(jobs):
                                e.wait_ge(ready.sem, ready.at(m + 1))
                                if m >= 2:
                                    e.wait_ge(o.sem, o.at(m - 1))
                                masked.inc(v.tensor_tensor(
                                    pairs[:, m % 2, :, :].rearrange("p l t -> p (l t)"),
                                    psum[:, (m % 2) * 2 * BANK:(m % 2 + 1) * 2 * BANK], const("level_mask"), ALU.mult))
                                if m:
                                    take_out(m - 1)
                            take_out(len(jobs) - 1)

                        @block.scalar
                        def _(e):
                            for m, (h, n) in enumerate(jobs):
                                if h:
                                    e.wait_ge(ready.sem, ready.at(m + 1))
                                    if m >= 2:
                                        e.wait_ge(o.sem, o.at(m - 1))
                                    masked_a.inc(sc.activation(cross[:, m % 2, :], bank(4 + m % 2)[:, 0:P], ACT.Copy))

        def gated_output(o, gain, gate_name, dst):
            sig, dve = S("gates_ready"), S("dve_chain")
            with ExitStack() as st:
                sg = tmp(st, "sg", [P, HALVES, MH * HD])
                group_norms([(o[:], heads_of(dst, HD), gain[:], HD)])
                with stage() as block:
                    sync_stage(block)

                    @block.scalar
                    def _(e):
                        sig.inc(sc.activation(sg[:], uc(gate_name), ACT.Silu))

                    @block.vector
                    def _(e):
                        e.wait_ge(sig.sem, sig.at(1))
                        dve.inc(v.tensor_tensor(dst, dst, sg[:], ALU.mult))

        with ExitStack() as st:
            gT = tmp(st, "glrT", [GLA_RANK, SEQ])
            transposes([uc("glr")[:, h, :] for h in range(HALVES)], GLA_RANK, gT[:])
            lg, ab, mn = (tmp(st, n, [P, HALVES, MH * GLA_DK]) for n in ("lg", "gabs", "gmin"))
            pre, abs_ready, log_ready = S("router_ready"), S("gate_abs"), S("gate_log")
            with stage() as block:
                sync_stage(block)

                @block.tensor
                def _(e):
                    for h in range(HALVES):
                        last = pe.matmul(bank(h)[:, 0:P], gT[:, h * P:(h + 1) * P], w_gate2[:], start=True, stop=True)
                    pre.inc(last)

                @block.vector
                def _(e):
                    step = make_step(e)
                    e.wait_ge(pre.sem, pre.at(1))
                    step(v.tensor_tensor(lg[:], logits_psum[:, :, 0:P], row_bc(b_gate[:], [HALVES]), ALU.add))
                    step(v.tensor_scalar(mn[:], lg[:], 0.0, 1.0 / GLA_TAU, ALU.min, ALU.mult))
                    step(v.scalar_tensor_tensor(out=ab[:], in0=lg[:], scalar=-1.0, in1=lg[:], op0=ALU.mult, op1=ALU.max), abs_ready)
                    e.wait_ge(log_ready.sem, log_ready.at(1))
                    step(v.scalar_tensor_tensor(out=lg[:], in0=ab[:], scalar=-1.0 / GLA_TAU, in1=mn[:],
                                                op0=ALU.mult, op1=ALU.add))
                    step(v.tensor_scalar(uc("gq"), uc("gq"), GLA_DK ** -0.5, None, ALU.mult))

                @block.scalar
                def _(e):
                    act = S("act_chain")
                    e.wait_ge(abs_ready.sem, abs_ready.at(1))
                    act.inc(sc.activation(ab[:], ab[:], ACT.Exp, scale=-1.0))
                    e.wait_ge(act.sem, act.total)
                    log_ready.inc(sc.activation(ab[:], ab[:], ACT.Ln, scale=1.0, bias=const("ones")[:, 0:1]))
            o = tmp(st, "o_gla", [P, HALVES, MH, HD])
            linear_attention(uc("gq"), uc("gk"), lg, uc("gv"), 1, GLA_DK, o)
            gated_output(o, gla_gain, "gog", mix[:, :, 512:768])

        with ExitStack() as st:
            f, k1 = (tmp(st, n, [P, HALVES, MH * HD]) for n in ("forget", "hkeys"))
            lb, top = (tmp(st, n, [P, MH * HD]) for n in ("lower_bound", "lb_max"))
            ex = tmp(st, "lb_exp", [P, LAYERS, MH * HD])
            sig, lb_ready, lb_exp, f_ready, log_ready = (S(n) for n in (
                "gates_ready", "bounds_shifted", "bounds_exp", "forget_ready", "gate_log"))
            with stage() as block:
                sync_stage(block)

                @block.scalar
                def _(e):
                    if layer:
                        e.wait_ge(lb_ready.sem, lb_ready.at(1))
                        lb_exp.inc(sc.activation(ex[:], ex[:], ACT.Exp))
                    sc.activation(f[:], uc("rf"), ACT.Sigmoid)
                    sig.inc(sc.activation(k1[:], uc("rf"), ACT.Sigmoid, scale=-1.0))
                    e.wait_ge(f_ready.sem, f_ready.at(1))
                    log_ready.inc(sc.activation(f[:], f[:], ACT.Ln))

                @block.vector
                def _(e):
                    step = make_step(e)
                    if layer:
                        step(v.tensor_tensor(top[:], hg_logits[:, 0, :], hg_logits[:, 1, :], ALU.max))
                        step(v.tensor_tensor(ex[:], hg_logits[:], row_bc(top[:], [LAYERS]), ALU.subtract), lb_ready)
                        e.wait_ge(lb_exp.sem, lb_exp.at(1))
                        step(v.tensor_tensor(top[:], ex[:, 0, :], ex[:, 1, :], ALU.add))
                        step(v.reciprocal(top[:], top[:]))
                        step(v.tensor_tensor(lb[:], ex[:, 1, :], top[:], ALU.mult))
                        step(v.tensor_scalar(top[:], lb[:], -1.0, 1.0, ALU.mult, ALU.add))
                    e.wait_ge(sig.sem, sig.at(1))
                    if layer:
                        for a in (f, k1):
                            step(v.tensor_tensor(a[:], a[:], row_bc(top[:], [HALVES]), ALU.mult))
                        step(v.tensor_tensor(f[:], f[:], row_bc(lb[:], [HALVES]), ALU.add))
                    step(v.tensor_scalar(f[:], f[:], 2.0 ** -63, None, ALU.max), f_ready)
                    e.wait_ge(log_ready.sem, log_ready.at(1))
                    step(v.tensor_scalar(f[:], f[:], 0.0, None, ALU.min))
            o = tmp(st, "o_hgrn", [P, HALVES, MH, HD])
            linear_attention(uc("rq"), k1, f, uc("ri"), 2, HD, o)
            gated_output(o, hg_gain, "rog", mix[:, :, 768:1024])

        transposes([mix[:, h, k * P:(k + 1) * P] for k in range(KT) for h in range(HALVES)], P,
                   xT[:].rearrange("p k t -> p (k t)"))
        product(xT, KT, D, add_to=x)

    with stage() as block:
        @block.sync
        def _(sp):
            for dst, src in small:
                params_loaded.inc(sp.dma_start(dst, src), 16)
            issue_loads(sp)
            sp.wait_ge(params_loaded.sem, params_loaded.total)

    comb1 = sb("comb1", [P, HALVES, N_EXP1])

    with ExitStack() as L1:
        z = tmp(L1, "z", [P, HALVES, IN1_COLS])
        normed_T(x, g_mix, xT)
        product(xT, KT, IN1_COLS, copy_to=z)

        def zc(name, lo=0, width=None):
            a, w = IN1[name]
            return z[:, :, a + lo:a + (w if width is None else lo + width)]

        y_att = tmp(L1, "y_att", [P, HALVES, D])
        with ExitStack() as st:
            qn = tmp(st, "qn", [P, HALVES, ATT_HEADS, HD])
            kn = tmp(st, "kn", [P, HALVES, ATT_KV, HD])
            group_norms([(zc("q").rearrange("p h (n d) -> p h n d", d=HD), qn[:], g_q[:], HD),
                         (zc("k").rearrange("p h (n d) -> p h n d", d=HD), kn[:], g_k[:], HD)])
            qr = tmp(st, "qr", [P, HALVES, ATT_HEADS, HD])
            kr = tmp(st, "kr", [P, HALVES, ATT_KV, HD])
            t1 = tmp(st, "t1", [P, ATT_HEADS, HD // 2])
            t2 = tmp(st, "t2", [P, ATT_HEADS, HD // 2])
            with stage() as block:
                sync_stage(block)

                @block.vector
                def _(e):
                    step = make_step(e)
                    for src, dst, nh in ((qn, qr, ATT_HEADS), (kn, kr, ATT_KV)):
                        for h in range(HALVES):
                            x0, x1 = (src[:, h, :, :].rearrange("p n (d two) -> p n d two", two=2)[:, :, :, i] for i in range(2))
                            o0, o1 = (dst[:, h, :, :].rearrange("p n (d two) -> p n d two", two=2)[:, :, :, i] for i in range(2))
                            cos = row_bc(const("cos")[:, h * 32:(h + 1) * 32], [nh])
                            sin = row_bc(const("sin")[:, h * 32:(h + 1) * 32], [nh])
                            step(v.tensor_tensor(t1[:, 0:nh, :], x0, cos, ALU.mult))
                            step(v.tensor_tensor(t2[:, 0:nh, :], x1, sin, ALU.mult))
                            step(v.tensor_tensor(o0, t1[:, 0:nh, :], t2[:, 0:nh, :], ALU.subtract))
                            step(v.tensor_tensor(t1[:, 0:nh, :], x0, sin, ALU.mult))
                            step(v.tensor_tensor(t2[:, 0:nh, :], x1, cos, ALU.mult))
                            step(v.tensor_tensor(o1, t1[:, 0:nh, :], t2[:, 0:nh, :], ALU.add))
            qT = tmp(st, "qT", [HD, ATT_HEADS, SEQ])
            kT = tmp(st, "kT", [HD, ATT_KV, SEQ])
            transposes([qr[:, h, n, :] for n in range(ATT_HEADS) for h in range(HALVES)], HD,
                       qT[:].rearrange("p n t -> p (n t)"))
            transposes([kr[:, h, n, :] for n in range(ATT_KV) for h in range(HALVES)], HD,
                       kT[:].rearrange("p n t -> p (n t)"))
            att = tmp(st, "att", [P, HALVES, ATT_HEADS, HD])
            for h in range(HALVES):
                attend([(qT[:, n, h * P:(h + 1) * P], kT[:, n // 4, :],
                         [zc("v", (n // 4) * HD, HD)[:, k, :] for k in range(HALVES)]) for n in range(ATT_HEADS)],
                       SEQ, HD, HD ** -0.5, None, att[:, h, :, :])
            attT = tmp(st, "attT", [P, 4, SEQ])
            att_rows = att[:].rearrange("p h n d -> p h (n d)")
            transposes([att_rows[:, h, k * P:(k + 1) * P] for k in range(4) for h in range(HALVES)], P,
                       attT[:].rearrange("p k t -> p (k t)"))
            product(attT, 4, D, copy_to=y_att)

        y_sgu = tmp(L1, "y_sgu", [P, HALVES, D])
        with ExitStack() as st:
            sgu_ln_g = tmp(st, "sgu_g", [P, SGU_W])
            sgu_ln_b = tmp(st, "sgu_b", [P, SGU_W])
            w_sT = tmp(st, "w_sT", [P, SGU_G, P])
            u = tmp(st, "u", [P, HALVES, SGU_W])
            vn = tmp(st, "vn", [P, HALVES, SGU_W])
            sq = tmp(st, "sgu_sq", [P, HALVES, SGU_W])
            mean, var, rt = (tmp(st, n, [P, HALVES]) for n in ("mean", "var", "rt"))
            gelu, var_ready, root = S("gelu_ready"), S("group_sums"), S("group_roots")
            with stage() as block:
                @block.sync
                def _(sp):
                    for dst, src in ((sgu_ln_g[:], A["sgu_ln_g"][0].partition_broadcast(P)),
                                     (sgu_ln_b[:], A["sgu_ln_b"][0].partition_broadcast(P)),
                                     (w_sT[:], A["w_s"][0].rearrange("g q p -> q g p"))):
                        params_loaded.inc(sp.dma_start(dst, src), 16)
                    issue_loads(sp)

                @block.scalar
                def _(e):
                    gelu.inc(sc.activation(vn[:], zc("sv"), ACT.Gelu_apprx_tanh))
                    gelu.inc(sc.activation(u[:], zc("su"), ACT.Gelu_apprx_tanh))
                    e.wait_ge(var_ready.sem, var_ready.at(1))
                    root.inc(sc.activation(rt[:], var[:], ACT.Sqrt, scale=1.0 / SGU_W, bias=eps))

                @block.vector
                def _(e):
                    step = make_step(e)
                    e.wait_ge(gelu.sem, gelu.at(1))
                    step(v.tensor_reduce(mean[:], vn[:], AXX, ALU.add))
                    step(v.tensor_scalar(mean[:], mean[:], 1.0 / SGU_W, None, ALU.mult))
                    step(v.tensor_tensor(vn[:], vn[:], last_bc(mean[:], SGU_W), ALU.subtract))
                    step(v.tensor_tensor(sq[:], vn[:], vn[:], ALU.mult))
                    step(v.tensor_reduce(var[:], sq[:], AXX, ALU.add), var_ready)
                    e.wait_ge(root.sem, root.at(1))
                    step(v.reciprocal(var[:], rt[:]))
                    step(v.tensor_tensor(vn[:], vn[:], last_bc(var[:], SGU_W), ALU.mult))
                    e.wait_ge(params_loaded.sem, params_loaded.at(48))
                    step(v.tensor_tensor(vn[:], vn[:], row_bc(sgu_ln_g[:], [HALVES]), ALU.mult))
                    step(v.tensor_tensor(vn[:], vn[:], row_bc(sgu_ln_b[:], [HALVES]), ALU.add))
            mixed, dve = S("tokens_mixed"), S("dve_chain")
            with stage() as block:
                sync_stage(block)

                @block.tensor
                def _(e):
                    for h in range(HALVES):
                        for g in range(SGU_G):
                            last = pe.matmul(bank(h)[:, g * P:(g + 1) * P], w_sT[:, g, :], vn[:, h, g * P:(g + 1) * P],
                                             start=True, stop=True)
                        mixed.inc(last)

                @block.vector
                def _(e):
                    for h in range(HALVES):
                        e.wait_ge(mixed.sem, mixed.at(h + 1))
                        for g in range(SGU_G):
                            uu = u[:, h, g * P:(g + 1) * P]
                            last = v.scalar_tensor_tensor(out=uu, in0=bank(h)[:, g * P:(g + 1) * P], scalar=b_s[:, g:g + 1],
                                                          in1=uu, op0=ALU.add, op1=ALU.mult)
                        dve.inc(last)
            uT = tmp(st, "uT", [P, 4, SEQ])
            transposes([u[:, h, k * P:(k + 1) * P] for k in range(4) for h in range(HALVES)], P,
                       uT[:].rearrange("p k t -> p (k t)"))
            product(uT, 4, D, copy_to=y_sgu)

        gates, dve = S("gates_ready"), S("dve_chain")
        with stage() as block:
            sync_stage(block)

            @block.scalar
            def _(e):
                for n in ("ga", "gb"):
                    gates.inc(sc.activation(zc(n), zc(n), ACT.Sigmoid))

            @block.vector
            def _(e):
                step = make_step(e)
                e.wait_ge(gates.sem, gates.at(1))
                step(v.tensor_tensor(y_att[:], y_att[:], zc("ga"), ALU.mult))
                e.wait_ge(gates.sem, gates.at(2))
                step(v.tensor_tensor(y_sgu[:], y_sgu[:], zc("gb"), ALU.mult))
                step(v.tensor_tensor(y_att[:], y_att[:], y_sgu[:], ALU.add))
        transposes([y_att[:, h, k * P:(k + 1) * P] for k in range(KT) for h in range(HALVES)], P,
                   xT[:].rearrange("p k t -> p (k t)"))
        product(xT, KT, D, add_to=x)

    with ExitStack() as st:
        mem = tmp(st, "mem", [P, HALVES, D])
        memT = tmp(st, "memT", [P, KT, SEQ])
        with stage() as block:
            @block.sync
            def _(sp):
                params_loaded.inc(sp.dma_start(mem[:], A["mem"][0].rearrange("(h p) d -> p h d", p=P)), 16)
                issue_loads(sp)
                sp.wait_ge(params_loaded.sem, params_loaded.total)
        normed_T(mem, g_mem, memT)
        normed_T(x, g_cross, xT)
        cqT, ckT = tmp(st, "cqT", [P, X_HEADS, SEQ]), tmp(st, "ckT", [P, X_HEADS, SEQ])
        cv = tmp(st, "cv", [P, HALVES, X_HEADS * X_HD])
        product_T(xT, cqT)
        product_T(memT, ckT)
        product(memT, KT, X_HEADS * X_HD, copy_to=cv)
        catt = tmp(st, "catt", [P, HALVES, X_HEADS, X_HD])
        for h in range(HALVES):
            attend([(cqT[:, n, h * P:(h + 1) * P], ckT[:, n, :],
                     [cv[:, k, n * X_HD:(n + 1) * X_HD] for k in range(HALVES)]) for n in range(X_HEADS)],
                   SEQ, X_HD, X_HD ** -0.5, None, catt[:, h, :, :])
        cT = tmp(st, "cT", [P, 4, SEQ])
        transposes([catt[:, h, k, :] for k in range(4) for h in range(HALVES)], P, cT[:].rearrange("p k t -> p (k t)"))
        product(cT, 4, D, add_to=x)

    normed_T(x, g_moe, xT)
    with ExitStack() as st:
        gl, goh = tmp(st, "gl", [P, HALVES, N_GROUPS]), tmp(st, "goh", [P, HALVES, N_GROUPS])
        ge = tmp(st, "ge", [P, HALVES, N_GROUPS])
        el = tmp(st, "el", [P, HALVES, N_EXP1])
        sel, c4 = tmp(st, "sel", [P, HALVES, PER_GROUP]), tmp(st, "c4", [P, HALVES, PER_GROUP])
        gbest, gsum = tmp(st, "gbest", [P, HALVES]), tmp(st, "gsum", [P, HALVES])
        t = [tmp(st, n, [P, HALVES]) for n in ("best1", "best2", "idx")] + \
            [tmp(st, n, [P, HALVES, PER_GROUP]) for n in ("cand", "one1", "one2", "left")]
        t = [a[:] for a in t]

        def finish(block, done):
            gshift, gexp = S("group_logits_shifted"), S("group_exp_ready")
            diff_ready, diff_exp = S("top_two_difference"), S("top_two_exp")

            @block.vector
            def _(e):
                step = make_step(e)
                e.wait_ge(done.sem, done.at(1))
                step(v.tensor_tensor(gl[:], logits_psum[:, :, 0:N_GROUPS], row_bc(b_rg[:], [HALVES]), ALU.add))
                step(v.tensor_tensor(el[:], logits_psum[:, :, 16:16 + N_EXP1], row_bc(b_re[:], [HALVES]), ALU.add))
                pick(step, gl[:], N_GROUPS, gbest[:], t[3], t[2], goh[:])
                step(v.tensor_tensor(ge[:], gl[:], last_bc(gbest[:], N_GROUPS), ALU.subtract), gshift)
                for h in range(HALVES):
                    for g in range(N_GROUPS):
                        src = el[:, h, g * PER_GROUP:(g + 1) * PER_GROUP]
                        if g == 0:
                            step(v.tensor_scalar(sel[:, h, :], src, goh[:, h, g:g + 1], None, ALU.mult))
                        else:
                            step(v.scalar_tensor_tensor(out=sel[:, h, :], in0=src, scalar=goh[:, h, g:g + 1],
                                                        in1=sel[:, h, :], op0=ALU.mult, op1=ALU.add))
                e.wait_ge(gexp.sem, gexp.at(1))
                step(v.tensor_reduce(gsum[:], ge[:], AXX, ALU.add))
                step(v.reciprocal(gsum[:], gsum[:]))
                top_two_weights(e, step, sel[:], PER_GROUP, c4[:], t, other=gsum[:])
                for h in range(HALVES):
                    for g in range(N_GROUPS):
                        step(v.tensor_scalar(comb1[:, h, g * PER_GROUP:(g + 1) * PER_GROUP], c4[:, h, :],
                                             goh[:, h, g:g + 1], None, ALU.mult))

            @block.scalar
            def _(e):
                e.wait_ge(gshift.sem, gshift.at(1))
                gexp.inc(sc.activation(ge[:], ge[:], ACT.Exp))
                e.wait_ge(diff_ready.sem, diff_ready.at(1))
                diff_exp.inc(sc.activation(t[1], t[1], ACT.Exp))

        route([(w_rg, 0, N_GROUPS), (w_re, 16, N_EXP1)], finish)
    expert_steps(lambda h, index: comb1[:, h, bass.ds(index[0], 1)])

    with ExitStack() as st:
        g_final = tmp(st, "g_final", [P, D])
        junk = tmp(st, "junk", [P, HALVES, D])
        ss, rms, rinv = (tmp(st, n, [P, HALVES]) for n in ("ss", "rms", "rinv"))
        with stage() as block:
            @block.sync
            def _(sp):
                params_loaded.inc(sp.dma_start(g_final[:], A["g_final"].partition_broadcast(P)), 16)
                issue_loads(sp)
            row_rms(block, x, rinv, junk, ss[:], rms[:])
            rms_done = S("rms_done")

            @block.vector
            def _(e):
                step = make_step(e)
                e.wait_ge(rms_done.sem, rms_done.at(1))
                step(v.reciprocal(rinv[:], rms[:]))
                e.wait_ge(params_loaded.sem, params_loaded.at(16))
                for h in range(HALVES):
                    step(v.scalar_tensor_tensor(out=x[:, h, :], in0=x[:, h, :], scalar=rinv[:, h:h + 1],
                                                in1=g_final[:], op0=ALU.mult, op1=ALU.mult))

    for layer in range(LAYERS):
        with ExitStack() as L2:
            hybrid_mixers(layer, L2)

        normed_T(x, g_ffn2[layer], xT)
        if layer % 2 == 0:
            expert_steps(lambda h, index: const("ones")[:, 0:1])
        else:
            with ExitStack() as st:
                lg = tmp(st, "lg", [P, HALVES, N_EXP2])
                t = [tmp(st, n, [P, HALVES]) for n in ("best1", "best2", "idx")] + \
                    [tmp(st, n, [P, HALVES, N_EXP2]) for n in ("cand", "one1", "one2", "left")]
                t = [a[:] for a in t]

                def finish(block, done):
                    diff_ready, diff_exp = S("top_two_difference"), S("top_two_exp")

                    @block.vector
                    def _(e):
                        step = make_step(e)
                        e.wait_ge(done.sem, done.at(1))
                        step(v.tensor_copy(lg[:], logits_psum[:, :, 0:N_EXP2]))
                        top_two_weights(e, step, lg[:], N_EXP2, comb1[:, :, 0:N_EXP2], t)

                    @block.scalar
                    def _(e):
                        e.wait_ge(diff_ready.sem, diff_ready.at(1))
                        diff_exp.inc(sc.activation(t[1], t[1], ACT.Exp))

                route([(router2, 0, N_EXP2)], finish)
            expert_steps(lambda h, index: comb1[:, h, bass.ds(index[0], 1)])

        with ExitStack() as st:
            pr = tmp(st, "pr", [P, HALVES, PLE])
            with stage() as block:
                @block.sync
                def _(sp):
                    params_loaded.inc(sp.dma_start(pr[:], A["p_2"][layer, 0].rearrange("(h p) d -> p h d", p=P)), 16)
                    issue_loads(sp)
                    sp.wait_ge(params_loaded.sem, params_loaded.total)
            pT = tmp(st, "pT", [P, PLE // P, SEQ])
            transposes([pr[:, h, k * P:(k + 1) * P] for k in range(PLE // P) for h in range(HALVES)], P,
                       pT[:].rearrange("p k t -> p (k t)"))
            proj, gate = tmp(st, "proj", [P, HALVES, D]), tmp(st, "gate", [P, HALVES, D])
            product(pT, PLE // P, D, copy_to=proj)
            normed_T(x, g_ple2[layer], xT)
            product(xT, KT, D, copy_to=gate)
            gates = S("gates_ready")
            with stage() as block:
                sync_stage(block)

                @block.scalar
                def _(e):
                    gates.inc(sc.activation(gate[:], gate[:], ACT.Sigmoid))

                @block.vector
                def _(e):
                    step = make_step(e)
                    e.wait_ge(gates.sem, gates.at(1))
                    step(v.tensor_tensor(gate[:], gate[:], proj[:], ALU.mult))
                    step(v.tensor_tensor(x[:], x[:], gate[:], ALU.add))

    stored = S("output_stored")
    with stage() as block:
        @block.sync
        def _(sp):
            stored.inc(sp.dma_start(out[0].rearrange("(h p) d -> p h d", p=P), x[:]), 16)
            sp.wait_ge(stored.sem, stored.total)


_INS = ["x", "mem", "g_mix", "w_in", "g_q", "g_k", "w_att_out", "sgu_ln_g", "sgu_ln_b", "w_s", "b_s",
        "w_sgu_out", "w_out", "g_cross", "g_mem", "w_cq", "w_ckv", "w_co", "g_moe", "w_rg", "b_rg", "w_re",
        "b_re", "w_gate", "w_up", "w_down", "g_final", "p_2", "norm_attn_2", "w_in_2", "w_out_2",
        "nsa_cmp_pos_2", "nsa_cmp_w1_2", "nsa_cmp_w2_2", "nsa_qk_gain_2", "diff_qk_gain_2", "diff_lambda_2",
        "diff_norm_2", "gla_w_gate2_2", "gla_b_gate_2", "gla_norm_2", "hgrn_lb_logits_2", "hgrn_norm_2",
        "norm_ffn_2", "ffn_w_gate_2", "ffn_w_up_2", "ffn_w_down_2", "moe_router_2", "moe_w_gate_2",
        "moe_w_up_2", "moe_w_down_2", "ple_norm_2", "ple_w_gate_2", "ple_w_proj_2"]

_TILED_GAINS = ("g_mix", "g_cross", "g_mem", "g_moe", "norm_attn_2", "norm_ffn_2", "ple_norm_2")
_LAST_TWO_SWAPPED = ("b_s", "nsa_cmp_pos_2", "w_s")


def kernel(**inputs):
    import numpy as _np
    import concourse.bacc as _bacc
    from concourse import mybir as _mybir
    from concourse.bass_utils import run_bass_kernel_spmd as _run

    nc = _bacc.Bacc("TRN2", target_bir_lowering=False, num_devices=1)
    arrays, aps = {}, {}
    for name in _INS:
        a = _np.asarray(inputs[name])
        if name in _TILED_GAINS:
            a = a.reshape(a.shape[0], KT, P).transpose(0, 2, 1)
        elif name in _LAST_TWO_SWAPPED:
            a = a.swapaxes(-1, -2)
        a = _np.ascontiguousarray(a)
        arrays[f"in_{name}_dram"] = a
        aps[name] = nc.dram_tensor(f"in_{name}_dram", a.shape, _mybir.dt.from_np(a.dtype), kind="ExternalInput").ap()
    cols, values = shape_constants()
    arrays["shape_constants"] = values
    consts = nc.dram_tensor("shape_constants", values.shape, _mybir.dt.float32, kind="ExternalInput").ap()
    out = nc.dram_tensor("out_dram", (1, SEQ, D), _mybir.dt.float32, kind="ExternalOutput").ap()
    fused_layers(nc, aps, consts, cols, out)
    r = _run(nc, [arrays], core_ids=[0])
    return r.results[0]["out_dram"]
```

```python
from contextlib import ExitStack, contextmanager
import math

import numpy as np

import concourse.bass as bass
from concourse import mybir

F32 = mybir.dt.float32
F32R = mybir.dt.float32r
ALU = mybir.AluOpType
ACT = mybir.ActivationFunctionType
AXX = mybir.AxisListType.X

P = 128
SEQ = 256
HALVES = SEQ // P
D = 1024
KT = D // P
EPS = 1e-6
BANK = 512
GRID_W = 64
ATT_HEADS, ATT_KV, HD = 8, 2, 64
SGU_W, SGU_G = 512, 4
X_HEADS, X_HD = 4, 128
N_GROUPS, PER_GROUP = 4, 4
N_EXP1, N_EXP2 = 16, 8
D_FF = 3584
FF = 512
FF_STEPS = D_FF // FF
LAYERS = 2
MH = 4
DIFF_QK = 32
GLA_DK = 32
GLA_RANK = 16
GLA_TAU = 16.0
PLE = 256
CMP_LEN, CMP_STRIDE = 32, 16
N_CMP = (SEQ - CMP_LEN) // CMP_STRIDE + 1
CMP_HID = 4 * HD
NEG = -1e30
LEVELS = [64, 32, 16, 8, 4, 2, 1]
N_LEVELS = len(LEVELS)

IN1 = dict(q=(0, 512), k=(512, 128), v=(640, 128), su=(768, 512), sv=(1280, 512),
           ga=(1792, 1024), gb=(2816, 1024))
IN1_COLS = 3840
IN2_SIZES = dict(nq=256, kc=64, vc=64, ks=64, vs=64, kw=64, vw=64, ng=12, dq=256, dk=256, dv=256,
                 gq=128, gk=128, gv=256, glr=16, gog=256, rq=256, rf=256, ri=256, rog=256)
IN2, _at = {}, 0
for _n, _w in IN2_SIZES.items():
    IN2[_n] = (_at, _w)
    _at += _w
IN2_COLS = _at


def shape_constants():
    cols, parts = {}, []

    def put(name, a):
        a = np.asarray(a, np.float32).reshape(P, -1)
        cols[name] = (sum(x.shape[1] for x in parts), a.shape[1])
        parts.append(a)

    tok = np.arange(SEQ)
    halves = lambda a: np.ascontiguousarray(a.reshape(HALVES, P, -1).transpose(1, 0, 2))
    put("ident", np.eye(P))
    pairs = HD // 4
    inv = (np.float32(10000.0) ** (-np.arange(pairs, dtype=np.float32) / np.float32(pairs))).astype(np.float32)
    ang = np.concatenate([(tok // GRID_W).astype(np.float32)[:, None] * inv,
                          (tok % GRID_W).astype(np.float32)[:, None] * inv], axis=1)
    put("cos", halves(np.cos(ang)))
    put("sin", halves(np.sin(ang)))
    put("causal", halves(np.where(tok[None, :] <= tok[:, None], 0.0, NEG)))
    ok = (np.arange(N_CMP) * CMP_STRIDE + CMP_LEN - 1)[None, :] <= tok[:, None]
    put("cmp_add", halves(np.where(ok, 0.0, NEG)))
    put("cmp_mul", halves(ok.astype(np.float32)))
    t, i = np.arange(P)[:, None], np.arange(P)[None, :]
    sums = []
    for size in LEVELS:
        b = (i // (2 * size)) * 2 * size + size
        sums.append(np.where(i >= b, (t >= b) & (t <= i), (t > i) & (t < b)))
    put("gate_sums", np.stack(sums, 1))
    put("gate_cross", np.stack([t > i, t <= i], 1))
    j = t
    pairs_of = [((j // (2 * s)) == (i // (2 * s))) & ((j % (2 * s)) < s) & ((i % (2 * s)) >= s) for s in LEVELS]
    put("level_mask", np.stack([*pairs_of, i == j], 1))
    put("iota", np.tile(np.arange(P, dtype=np.float32), (P, 1)))
    put("before", t < i)
    put("all_ones", np.ones((P, P)))
    put("eps", np.full((P, 1), EPS))
    return cols, np.ascontiguousarray(np.concatenate(parts, 1))


class Signal:

    def __init__(self, sem):
        self.sem, self.total, self.base = sem, 0, 0

    def inc(self, ins, by=1):
        ins.then_inc(self.sem, by)
        self.total += by
        return ins

    def at(self, k):
        return self.base + k


class Piece:

    def __init__(self, n, src, a, width):
        self.n, self.src, self.a, self.width = n, src, a, width


class WeightStream:

    RAW, FINE = 12, 4

    def __init__(self):
        self.items, self.count = [], 0

    def add(self, src, a, width):
        self.items.append(Piece(self.count, src, a, width))
        self.count += 1


def fused_layers(nc, A, consts_dram, const_cols, out):
    ctx = ExitStack()
    with ctx:
        build(nc, ctx, A, consts_dram, const_cols, out)


def build(nc, ctx, A, consts_dram, const_cols, out):
    def sb(name, shape, stack=ctx, dtype=F32):
        return stack.enter_context(nc.sbuf_tensor(name, shape, dtype))

    serial = [0]

    def tmp(stack, name, shape, dtype=F32):
        serial[0] += 1
        return sb(f"{name}_{serial[0]}", shape, stack, dtype)

    def tmp_split(stack, name, shape):
        return tmp(stack, name + "_hi", shape, F32R), tmp(stack, name + "_lo", shape, F32R)

    signals = {}

    def S(name):
        if name not in signals:
            signals[name] = Signal(ctx.enter_context(nc.semaphore(name)))
        return signals[name]

    @contextmanager
    def stage():
        for s in signals.values():
            s.base = s.total
        with nc.Block() as block:
            yield block

    v, sc, pe = nc.vector, nc.scalar, nc.tensor

    ring = sb("ring", [P, WeightStream.RAW, 1024])
    ring_hi = sb("ring_hi", [P, WeightStream.FINE, 1024], dtype=F32R)
    ring_lo = sb("ring_lo", [P, WeightStream.FINE, 1024], dtype=F32R)
    x = sb("x", [P, HALVES, D])
    xT = (sb("xT_hi", [P, KT, SEQ], dtype=F32R),
          sb("xT_lo", [P, KT, SEQ], dtype=F32R))
    consts = sb("consts", [P, consts_dram.shape[1]])

    def const(name):
        a, w = const_cols[name]
        return consts[:, a:a + w]

    ident = const("ident")
    eps = const("eps")
    psum = ctx.enter_context(nc.psum_tensor("psum", [P, 8 * BANK], F32))

    def bank(b, n=1):
        return psum[:, b * BANK:(b + n) * BANK]

    small = []

    def row_param(name, ap):
        t = sb(name, [P, ap.shape[-1]])
        small.append((t[:], ap.partition_broadcast(P)))
        return t

    def col_param(name, ap):
        t = sb(name, [P, KT])
        small.append((t[:], ap))
        return t

    def tile_param(name, shape, ap):
        t = sb(name, shape)
        small.append((t[:], ap))
        return t

    small.append((consts[:], consts_dram))
    small.append((x[:], A["x"][0].rearrange("(h p) d -> p h d", p=P)))
    g_mix, g_cross, g_mem, g_moe = (col_param("c_" + n, A[n][0]) for n in ("g_mix", "g_cross", "g_mem", "g_moe"))
    g_attn2 = [col_param(f"g_attn2_{i}", A["norm_attn_2"][i]) for i in range(LAYERS)]
    g_ffn2 = [col_param(f"g_ffn2_{i}", A["norm_ffn_2"][i]) for i in range(LAYERS)]
    g_ple2 = [col_param(f"g_ple2_{i}", A["ple_norm_2"][i]) for i in range(LAYERS)]
    g_q, g_k = row_param("r_g_q", A["g_q"][0]), row_param("r_g_k", A["g_k"][0])
    b_s = tile_param("b_s", [P, SGU_G], A["b_s"][0])
    w_rg = tile_param("w_rg", [P, KT, N_GROUPS], A["w_rg"][0].rearrange("(k p) n -> p k n", p=P))
    w_re = tile_param("w_re", [P, KT, N_EXP1], A["w_re"][0].rearrange("(k p) n -> p k n", p=P))
    b_rg, b_re = row_param("r_b_rg", A["b_rg"][0]), row_param("r_b_re", A["b_re"][0])
    router2 = tile_param("router2", [P, KT, N_EXP2], A["moe_router_2"][0].rearrange("(k p) n -> p k n", p=P))
    hg_logits = tile_param("hg_logits", [P, LAYERS, 256],
                           A["hgrn_lb_logits_2"].rearrange("l c -> (l c)").partition_broadcast(P)
                           .rearrange("p (l c) -> p l c", l=LAYERS))

    ws = WeightStream()

    def stream_matrix(w):
        k, n = w.shape
        for c in range(0, n, FF):
            width = min(FF, n - c)
            for q in range(k // (2 * P)):
                ws.add(w[q * 2 * P:(q + 1) * 2 * P, c:c + width].rearrange("(a p) n -> p a n", p=P), 2, width)

    CMP_PIECES = CMP_LEN // 4

    def stream_cmp(w1):
        for q in range(CMP_PIECES):
            ws.add(w1[:, 4 * q:4 * q + 4, :], 4, CMP_HID)

    class Experts:

        def __init__(self, gate, up, down, n_experts, n_chunks):
            self.gate, self.up, self.down, self.E, self.C = gate, up, down, n_experts, n_chunks
            self.steps = n_experts * n_chunks
            self.n0 = ws.count
            for k in range(8):
                ws.add(self.src(k, (0, 0), None), 2, FF)
            ws.items.append(self)
            ws.count = self.n0 - 4 + 12 * self.steps
            for k in range(8, 12):
                ws.add(self.src(k, None, (n_experts - 1, n_chunks - 1)), 1, 1024)

        def src(self, k, cur, prev):
            if k < 8:
                w = (self.gate if k < 4 else self.up)(*cur)
                return w.rearrange("(q a p) f -> q p a f", p=P, a=2)[k % 4]
            return self.down(*prev).rearrange("(q a p) d -> q p a d", p=P, a=1)[k - 8]

        def number(self, k, i, cur=True):
            if not cur:
                k -= 8
            return (self.n0 + k, 0) if isinstance(i, int) and i == 0 else (self.n0 - 4 + k, i)

        def iterations(self, e, body):
            E, C = self.E, self.C

            def step(ex, c, last=False):
                return (ex, c, isinstance(c, int) and c == 0, last or (isinstance(c, int) and c == C - 1))

            def expert(ex, final):
                if C == 1:
                    body(ex + 1, None if final else step(ex + 1, 0), step(ex, 0), ex - 1)
                    return
                body(ex * C + 1, step(ex, 1), step(ex, 0), ex - 1)
                if C > 3:
                    with e.Fori(2, C - 1) as c:
                        body(ex * C + c, step(ex, c), step(ex, c - 1), None)
                body(ex * C + C - 1, step(ex, C - 1), step(ex, C - 2), None)
                body(ex * C + C, None if final else step(ex + 1, 0), step(ex, C - 1), None)

            body(0, step(0, 0), None, None)
            if E > 1:
                with e.Fori(0, E - 1) as ex:
                    expert(ex, False)
            expert(E - 1, True)
            body(None, None, None, E - 1)

    stream_matrix(A["w_in"][0])
    stream_matrix(A["w_att_out"][0])
    stream_matrix(A["w_sgu_out"][0])
    stream_matrix(A["w_out"][0])
    stream_matrix(A["w_cq"][0])
    stream_matrix(A["w_ckv"][0])
    stream_matrix(A["w_co"][0])
    Experts(lambda e, c: A["w_gate"][0, e], lambda e, c: A["w_up"][0, e], lambda e, c: A["w_down"][0, e], N_EXP1, 1)
    for i in range(LAYERS):
        stream_matrix(A["w_in_2"][i])
        stream_cmp(A["nsa_cmp_w1_2"][i])
        stream_matrix(A["w_out_2"][i])
        if i % 2 == 0:
            wg = A["ffn_w_gate_2"][0].rearrange("k (c f) -> c k f", f=FF)
            wu = A["ffn_w_up_2"][0].rearrange("k (c f) -> c k f", f=FF)
            wd = A["ffn_w_down_2"][0].rearrange("(c f) d -> c f d", f=FF)
            Experts(lambda e, c, w=wg: w[c], lambda e, c, w=wu: w[c], lambda e, c, w=wd: w[c], 1, FF_STEPS)
        else:
            wg = A["moe_w_gate_2"][0].rearrange("e k (c f) -> e c k f", f=FF)
            wu = A["moe_w_up_2"][0].rearrange("e k (c f) -> e c k f", f=FF)
            wd = A["moe_w_down_2"][0].rearrange("e (c f) d -> e c f d", f=FF)
            Experts(lambda e, c, w=wg: w[e, c], lambda e, c, w=wu: w[e, c], lambda e, c, w=wd: w[e, c],
                    N_EXP2, FF_STEPS)
        stream_matrix(A["ple_w_proj_2"][i])
        stream_matrix(A["ple_w_gate_2"][i])

    RAW, FINE = ws.RAW, ws.FINE
    params_loaded = S("params_loaded")
    arrived = [ctx.enter_context(nc.semaphore(f"piece_in_raw_slot{s}")) for s in range(RAW)]
    hi_ready, lo_ready, used = (ctx.enter_context(nc.semaphore(n)) for n in
                                ("piece_hi_ready", "piece_lo_ready", "pieces_used"))

    def count_after(num, off=1):
        return num[1] * 12 + (num[0] + off)

    def raw_view(buf, slots, num, a, width):
        w = buf[:, num[0] % slots, :].rearrange("p (a n) -> p a n", a=a)
        return w if width * a == 1024 else w[:, :, 0:width]

    def then_registers(e):
        e.sem_inc(passed_waits, 1)

    def load_piece(sp, num, src, a, width):
        if not (isinstance(num[1], int) and num[0] + 12 * num[1] < RAW):
            sp.wait_ge(lo_ready, count_after(num, 1 - RAW))
            if not isinstance(num[1], int):
                then_registers(sp)
        sp.dma_start(raw_view(ring, RAW, num, a, width), src).then_inc(arrived[num[0] % RAW], 16)

    def make_hi(e, num, a=2, width=FF):
        e.wait_ge(arrived[num[0] % RAW], num[1] * 16 + 16 * (num[0] // RAW + 1))
        if not (isinstance(num[1], int) and num[0] + 12 * num[1] < FINE):
            e.wait_ge(used, count_after(num, 1 - FINE))
        sc.activation(raw_view(ring_hi, FINE, num, a, width), raw_view(ring, RAW, num, a, width), ACT.Copy) \
            .then_inc(hi_ready, 1)

    def make_lo(e, num, a=2, width=FF):
        e.wait_ge(hi_ready, count_after(num))
        v.tensor_tensor(raw_view(ring_lo, FINE, num, a, width), raw_view(ring, RAW, num, a, width),
                        raw_view(ring_hi, FINE, num, a, width).bitcast(F32), ALU.subtract).then_inc(lo_ready, 1)

    def make_his(e, pcs):
        for p in pcs:
            make_hi(e, (p.n, 0), p.a, p.width)

    def make_los(e, pcs):
        for p in pcs:
            make_lo(e, (p.n, 0), p.a, p.width)

    def three_passes(out_, lhsT, rhs, start, stop):
        pe.matmul(out_, lhsT[0], rhs[0], start=start, stop=False)
        pe.matmul(out_, lhsT[0], rhs[1], start=False, stop=False)
        return pe.matmul(out_, lhsT[1], rhs[0], start=False, stop=stop)

    passed_waits = ctx.enter_context(nc.semaphore("passed_waits"))
    to_load, to_take = list(ws.items), list(ws.items)
    taken = [0]

    def take(n):
        got = [to_take.pop(0) for _ in range(n)]
        taken[0] = got[-1].n + 1
        return got

    def issue_loads(sp):
        while to_load and isinstance(to_load[0], Piece) and to_load[0].n + 1 - RAW <= taken[0]:
            p = to_load.pop(0)
            load_piece(sp, (p.n, 0), p.src, p.a, p.width)

    def sync_stage(block):
        @block.sync
        def _(sp):
            issue_loads(sp)

    def transposes(jobs, width, dst, scale=None):
        done, free_v, free_s = S("transposed"), S("bank_copied_dve"), S("bank_copied_act")
        split = isinstance(dst, tuple)
        groups = [list(range(i, min(i + 4, len(jobs)))) for i in range(0, len(jobs), 4)]
        assert len(groups) <= 8
        with stage() as block:
            sync_stage(block)

            @block.tensor
            def _(e):
                for g, group in enumerate(groups):
                    for m, n in enumerate(group):
                        last = pe.transpose(psum[0:width, g * BANK + m * P:g * BANK + (m + 1) * P], jobs[n], ident)
                    done.inc(last)

            def source(g, n0, a, b):
                return psum[0:width, g * BANK + a - n0:g * BANK + b - n0]

            def parts(group):
                n0, n1 = group[0] * P, (group[-1] + 1) * P
                return n0, [(n0, n1, None)] if scale is None else \
                    [(a, a + 2 * P, scale[:, a // (2 * P):a // (2 * P) + 1]) for a in range(n0, n1, 2 * P)]

            @block.vector
            def _(e):
                for g, group in enumerate(groups):
                    n0, todo = parts(group)
                    if split:
                        e.wait_ge(free_s.sem, free_s.at(g + 1))
                        for a, b, k in todo:
                            hi = dst[0][:, a:b].bitcast(F32)
                            if k is None:
                                last = v.tensor_tensor(dst[1][:, a:b], source(g, n0, a, b), hi, ALU.subtract)
                            else:
                                last = v.scalar_tensor_tensor(out=dst[1][:, a:b], in0=source(g, n0, a, b), scalar=k,
                                                              in1=hi, op0=ALU.mult, op1=ALU.subtract)
                        free_v.inc(last)
                    elif g % 2 == 0:
                        e.wait_ge(done.sem, done.at(g + 1))
                        free_v.inc(v.tensor_copy(dst[:, n0:todo[-1][1]], source(g, n0, n0, todo[-1][1])))

            @block.scalar
            def _(e):
                for g, group in enumerate(groups):
                    if not split and g % 2 == 0:
                        continue
                    n0, todo = parts(group)
                    e.wait_ge(done.sem, done.at(g + 1))
                    for a, b, k in todo:
                        to = dst[0] if split else dst
                        last = sc.activation(to[:, a:b], source(g, n0, a, b), ACT.Copy, scale=1.0 if k is None else k)
                    free_s.inc(last)

    def row_rms(block, src, rinv, junk, ss, rms):
        sq, rms_done = S("squares_summed"), S("rms_done")

        @block.scalar
        def _(e):
            for h in range(HALVES):
                sq.inc(sc.activation(junk[:, h, :], src[:, h, :], ACT.Square, accum_out=ss[:, h:h + 1]))
            e.wait_ge(sq.sem, sq.at(HALVES))
            rms_done.inc(sc.activation(rms, ss, ACT.Sqrt, scale=1.0 / D, bias=eps))

    def flat(pair):
        return tuple(t[:].rearrange("p k n -> p (k n)") for t in pair)

    def normed_T(src, gain, dst, xn=None):
        with ExitStack() as st:
            if xn is None:
                xn = tmp(st, "xn", [P, HALVES, D])
            ss, rms, rinv = (tmp(st, n, [P, HALVES]) for n in ("ss", "rms", "rinv"))
            dve = S("dve_chain")
            with stage() as block:
                sync_stage(block)
                row_rms(block, src, rinv, xn, ss[:], rms[:])
                rms_done = S("rms_done")

                @block.vector
                def _(e):
                    e.wait_ge(rms_done.sem, rms_done.at(1))
                    dve.inc(v.reciprocal(rinv[:], rms[:]))
                    e.wait_ge(dve.sem, dve.total)
                    for h in range(HALVES):
                        dve.inc(v.tensor_scalar(xn[:, h, :], src[:, h, :], rinv[:, h:h + 1], None, ALU.mult))
            transposes([xn[:, h, k * P:(k + 1) * P] for k in range(KT) for h in range(HALVES)], P,
                       flat(dst), scale=gain[:])

    def product(lhsT, kt, cols, copy_to=None, add_to=None):
        chunks = [(c, min(FF, cols - c)) for c in range(0, cols, FF)]
        per = kt // 2
        got = take(per * len(chunks))
        of_chunk = [got[n * per:(n + 1) * per] for n in range(len(chunks))]
        free_v, free_s = S("bank_copied_dve"), S("bank_copied_act")
        with stage() as block:
            sync_stage(block)

            @block.tensor
            def _(e):
                for n, (c, width) in enumerate(chunks):
                    if n >= 4:
                        e.wait_ge(free_v.sem, free_v.at(n - 3))
                        if add_to is None:
                            e.wait_ge(free_s.sem, free_s.at(n - 3))
                    for q, p in enumerate(of_chunk[n]):
                        e.wait_ge(lo_ready, p.n + 1)
                        w = [raw_view(r, FINE, (p.n, 0), 2, width) for r in (ring_hi, ring_lo)]
                        for a in range(2):
                            k = 2 * q + a
                            for h in range(HALVES):
                                last = three_passes(bank((2 * n + h) % 8)[:, 0:width],
                                                    [x_[:, k, h * P:(h + 1) * P] for x_ in lhsT], [w_[:, a, :] for w_ in w],
                                                    k == 0, k == kt - 1)
                        last.then_inc(used, 1)

            @block.vector
            def _(e):
                make_los(e, of_chunk[0])
                for n, (c, width) in enumerate(chunks):
                    if n + 1 < len(chunks):
                        make_los(e, of_chunk[n + 1])
                    e.wait_ge(used, of_chunk[n][-1].n + 1)
                    if add_to is None:
                        free_v.inc(v.tensor_copy(copy_to[:, 0, c:c + width], bank(2 * n % 8)[:, 0:width]))
                    else:
                        for h in range(HALVES):
                            to = add_to[:, h, c:c + width]
                            last = v.tensor_tensor(to, to, bank((2 * n + h) % 8)[:, 0:width], ALU.add)
                        free_v.inc(last)

            @block.scalar
            def _(e):
                make_his(e, of_chunk[0])
                for n, (c, width) in enumerate(chunks):
                    if n + 1 < len(chunks):
                        make_his(e, of_chunk[n + 1])
                    if add_to is None:
                        e.wait_ge(used, of_chunk[n][-1].n + 1)
                        free_s.inc(sc.activation(copy_to[:, 1, c:c + width], bank((2 * n + 1) % 8)[:, 0:width], ACT.Copy))

    def product_T(rhsT, dst):
        got = take(KT // 2)
        copied = S("bank_copied_dve")
        with stage() as block:
            sync_stage(block)

            @block.tensor
            def _(e):
                for q, p in enumerate(got):
                    e.wait_ge(lo_ready, p.n + 1)
                    w = [raw_view(r, FINE, (p.n, 0), 2, FF) for r in (ring_hi, ring_lo)]
                    for a in range(2):
                        k = 2 * q + a
                        for j in range(4):
                            last = three_passes(bank(j)[:, 0:SEQ], [w_[:, a, j * P:(j + 1) * P] for w_ in w],
                                                [x_[:, k, :] for x_ in rhsT], k == 0, k == KT - 1)
                    last.then_inc(used, 1)

            @block.scalar
            def _(e):
                make_his(e, got)

            @block.vector
            def _(e):
                make_los(e, got)
                e.wait_ge(used, got[-1].n + 1)
                copied.inc(v.tensor_copy(dst[:], psum[:, 0:4 * BANK].rearrange("p (j n) -> p j n", j=4)[:, :, 0:SEQ]))

    def last_bc(ap, n):
        return ap.unsqueeze(len(ap.shape)).to_broadcast([*ap.shape, n])

    def row_bc(ap, groups):
        for _ in groups:
            ap = ap.unsqueeze(1)
        return ap.to_broadcast([P, *groups, ap.shape[-1]])

    def group_norms(items):
        dve, act, sums, roots = S("dve_chain"), S("act_chain"), S("group_sums"), S("group_roots")
        with ExitStack() as st:
            n = [i[0].shape[2] for i in items]
            sq = [tmp(st, "sq", [P, HALVES, a, i[3]]) for a, i in zip(n, items)]
            ss = [tmp(st, "gss", [P, HALVES, a]) for a in n]
            rt = [tmp(st, "grt", [P, HALVES, a]) for a in n]
            with stage() as block:
                sync_stage(block)

                @block.vector
                def _(e):
                    for (src, _, _, _), q in zip(items, sq):
                        dve.inc(v.tensor_tensor(q[:], src, src, ALU.mult))
                    e.wait_ge(dve.sem, dve.total)
                    for q, s_ in zip(sq, ss):
                        sums.inc(v.tensor_reduce(s_[:], q[:], AXX, ALU.add))
                    for i, (src, dst, gain, d) in enumerate(items):
                        e.wait_ge(roots.sem, roots.at(i + 1))
                        dve.inc(v.reciprocal(ss[i][:], rt[i][:]))
                        e.wait_ge(dve.sem, dve.total)
                        dve.inc(v.tensor_tensor(dst, src, last_bc(ss[i][:], d), ALU.mult))
                        e.wait_ge(dve.sem, dve.total)
                        dve.inc(v.tensor_tensor(dst, dst, row_bc(gain, [HALVES, n[i]]), ALU.mult))

                @block.scalar
                def _(e):
                    for i, (_, _, _, d) in enumerate(items):
                        e.wait_ge(sums.sem, sums.at(i + 1))
                        roots.inc(sc.activation(rt[i][:], ss[i][:], ACT.Sqrt, scale=1.0 / d, bias=eps))

    def attend(heads, n_keys, dv, scale, weight, dst, mask=None, keep=None, accumulate=False):
        nh = len(heads)
        tiles = (n_keys + P - 1) // P
        rows = min(P, n_keys)
        scores, shifted, exped, pT, pT_v, pT_s, o = (S(n) for n in (
            "scores_ready", "scores_shifted", "exp_ready", "probs_transposed", "probsT_dve", "probsT_act", "attended"))
        dve, ready = S("dve_chain"), S("exp_kept")
        kw = n_keys if n_keys < P else SEQ
        with ExitStack() as st:
            E = tmp(st, "E", [P, nh, n_keys])
            PT = tmp(st, "PT", [P, nh * tiles, P])
            mx, rs, ri = (tmp(st, n, [P, nh]) for n in ("mx", "rs", "ri"))
            O = tmp(st, "O", [P, nh, dv])
            sp_ = psum[:, 0:nh * kw].rearrange("p (h k) -> p h k", h=nh)
            tp = psum[:, 4 * BANK:4 * BANK + nh * tiles * P].rearrange("p (h k) -> p h k", k=P)
            op = psum[:, 0:nh * dv].rearrange("p (h k) -> p h k", h=nh)
            groups = [(a, min(a + 4, nh * tiles)) for a in range(0, nh * tiles, 4)]
            with stage() as block:
                sync_stage(block)

                @block.tensor
                def _(e):
                    for h, (qT, kT, _) in enumerate(heads):
                        last = pe.matmul(sp_[:, h, :], qT, kT, start=True, stop=True)
                    scores.inc(last)
                    e.wait_ge(ready.sem, ready.at(1))
                    for a, b in groups:
                        for n in range(a, b):
                            h, k = divmod(n, tiles)
                            last = pe.transpose(tp[0:rows, n, :], E[:, h, k * P:k * P + rows], ident)
                        pT.inc(last)
                    e.wait_ge(pT_v.sem, pT_v.at((len(groups) + 1) // 2))
                    if len(groups) > 1:
                        e.wait_ge(pT_s.sem, pT_s.at(len(groups) // 2))
                    for h, (_, _, vals) in enumerate(heads):
                        for k in range(tiles):
                            last = pe.matmul(op[:, h, :], PT[0:rows, h * tiles + k, :], vals[k],
                                             start=(k == 0), stop=(k == tiles - 1))
                    o.inc(last)

                @block.vector
                def _(e):
                    def step(ins, sig=dve):
                        sig.inc(ins)
                        e.wait_ge(sig.sem, sig.total)
                    e.wait_ge(scores.sem, scores.at(1))
                    if mask is None:
                        step(v.tensor_scalar(E[:], sp_, scale, None, ALU.mult))
                    else:
                        step(v.scalar_tensor_tensor(out=E[:], in0=sp_, scalar=scale, in1=row_bc(mask, [nh]),
                                                    op0=ALU.mult, op1=ALU.add))
                    step(v.tensor_reduce(mx[:], E[:], AXX, ALU.max))
                    step(v.tensor_tensor(E[:], E[:], last_bc(mx[:], n_keys), ALU.subtract), shifted)
                    e.wait_ge(exped.sem, exped.at(1))
                    step(v.tensor_reduce(rs[:], E[:], AXX, ALU.add))
                    if keep is not None:
                        step(v.tensor_tensor(E[:], E[:], row_bc(keep, [nh]), ALU.mult), ready)
                    step(v.reciprocal(ri[:], rs[:]))
                    if weight is not None:
                        weight(step, ri[:])
                    for g, (a, b) in enumerate(groups):
                        if g % 2 == 0:
                            e.wait_ge(pT.sem, pT.at(g + 1))
                            pT_v.inc(v.tensor_copy(PT[0:rows, a:b, :], tp[0:rows, a:b, :]))
                    e.wait_ge(o.sem, o.at(1))
                    if accumulate:
                        step(v.tensor_tensor(O[:], op, last_bc(ri[:], dv), ALU.mult))
                        step(v.tensor_tensor(dst, dst, O[:], ALU.add))
                    else:
                        step(v.tensor_tensor(dst, op, last_bc(ri[:], dv), ALU.mult))

                @block.scalar
                def _(e):
                    e.wait_ge(shifted.sem, shifted.at(1))
                    exped.inc(sc.activation(E[:], E[:], ACT.Exp))
                    if keep is None:
                        e.wait_ge(exped.sem, exped.total)
                        ready.total += 1
                        e.sem_inc(ready.sem, 1)
                    for g, (a, b) in enumerate(groups):
                        if g % 2 == 1:
                            e.wait_ge(pT.sem, pT.at(g + 1))
                            pT_s.inc(sc.activation(PT[0:rows, a:b, :], tp[0:rows, a:b, :], ACT.Copy))

    def dense_experts(group, combine, tag):
        G, U = psum[:, 0:2 * BANK], psum[:, 2 * BANK:4 * BANK]
        silu, hidden, hid_hi, hid, y_out = (S(n + tag) for n in (
            "silu_ready", "hidden_made", "hidden_hi_ready", "hidden_ready", "expert_output_added"))
        counted = (silu, hidden, hid_hi, hid, y_out)

        def programs(st):
            s_g = tmp(st, "silu_gT", [P, 4, SEQ])
            h_hi, h_lo = tmp_split(st, "hiddenT", [P, 4, SEQ])
            flat_g = s_g[:].rearrange("p j n -> p (j n)")

            def tensor(e):
                def body(i, cur, prev, done):
                    if cur:
                        for part, to in enumerate((G, U)):
                            for q in range(4):
                                num = group.number(4 * part + q, i)
                                e.wait_ge(lo_ready, count_after(num))
                                if part and q == 0 and prev:
                                    e.wait_ge(hid_hi.sem, i + hid_hi.at(0))
                                w = [raw_view(r, FINE, num, 2, FF) for r in (ring_hi, ring_lo)]
                                for a in range(2):
                                    k = 2 * q + a
                                    for j in range(4):
                                        last = three_passes(to[:, j * SEQ:(j + 1) * SEQ],
                                                            [w_[:, a, j * P:(j + 1) * P] for w_ in w],
                                                            [x_[:, k, :] for x_ in xT],
                                                            k == 0 and j % 2 == 0, k == KT - 1 and j % 2 == 1)
                                last.then_inc(used, 1)
                    if prev:
                        e.wait_ge(hid.sem, i + hid.at(0))
                        if not (isinstance(i, int) and i == 1):
                            e.wait_ge(y_out.sem, i + y_out.at(-1))
                        for j in range(4):
                            num = group.number(8 + j, i, cur)
                            e.wait_ge(lo_ready, count_after(num))
                            w = [raw_view(r, FINE, num, 1, 1024) for r in (ring_hi, ring_lo)]
                            for h in range(HALVES):
                                for c in range(2):
                                    last = three_passes(bank(4 + 2 * h + c), [t[:, j, h * P:(h + 1) * P] for t in (h_hi, h_lo)],
                                                        [w_[:, 0, c * BANK:(c + 1) * BANK] for w_ in w], j == 0, j == 3)
                            last.then_inc(used, 1)
                group.iterations(e, body)

            def scalar(e):
                def body(i, cur, prev, done):
                    if cur:
                        for k in range(8):
                            make_hi(e, group.number(k, i))
                        e.wait_ge(used, count_after(group.number(3, i)))
                        if prev:
                            e.wait_ge(hid.sem, i + hid.at(0))
                        sc.activation(flat_g, G, ACT.Silu).then_inc(silu.sem, 1)
                    if prev:
                        for k in range(8, 12):
                            make_hi(e, group.number(k, i, cur), 1, 1024)
                    if cur:
                        e.wait_ge(hidden.sem, i + hidden.at(1))
                        sc.activation(h_hi[:], s_g[:], ACT.Copy).then_inc(hid_hi.sem, 1)
                group.iterations(e, body)

            def vector(e):
                def body(i, cur, prev, done):
                    if cur:
                        for k in range(8):
                            make_lo(e, group.number(k, i))
                    if prev:
                        for k in range(8, 12):
                            make_lo(e, group.number(k, i, cur), 1, 1024)
                        e.wait_ge(used, count_after(group.number(11, i, cur)))
                    if cur:
                        e.wait_ge(used, count_after(group.number(7, i)))
                        e.wait_ge(silu.sem, i + silu.at(1))
                        v.tensor_tensor(flat_g, flat_g, U, ALU.mult).then_inc(hidden.sem, 1)
                        e.wait_ge(hid_hi.sem, i + hid_hi.at(1))
                        v.tensor_tensor(h_lo[:], s_g[:], h_hi[:].bitcast(F32), ALU.subtract).then_inc(hid.sem, 1)
                    if prev:
                        then_registers(e)
                        for h in range(HALVES):
                            last = v.scalar_tensor_tensor(
                                out=x[:, h, :], in0=psum[:, (4 + 2 * h) * BANK:(6 + 2 * h) * BANK],
                                scalar=combine(h, prev[0]), in1=x[:, h, :], op0=ALU.mult, op1=ALU.add)
                        last.then_inc(y_out.sem, 1)
                        e.wait_ge(y_out.sem, i + y_out.at(0))
                        then_registers(e)
                group.iterations(e, body)
            return tensor, scalar, vector
        return programs, counted

    def experts_sync(block, group):
        @block.sync
        def _(sp):
            issue_loads(sp)
            assert to_load.pop(0) is group

            def body(i, cur, prev, done):
                if prev and cur:
                    for k in range(12):
                        load_piece(sp, group.number(k, i), group.src(k, cur[0:2], prev[0:2]), *((2, FF) if k < 8 else (1, 1024)))
            group.iterations(sp, body)
            issue_loads(sp)

    def take_group():
        for _ in range(8):
            to_take.pop(0)
        group = to_take.pop(0)
        for _ in range(4):
            last = to_take.pop(0)
        return group, last.n + 1

    def gather_rows(xn, dispatch):
        for k in range(KT):
            for h in range(HALVES):
                last = pe.matmul(psum[:, 5 * BANK + k * P:5 * BANK + (k + 1) * P], xn[:, h, k * P:(k + 1) * P],
                                 dispatch[:, h, :], start=(h == 0), stop=(h == HALVES - 1))
        return last

    def make_dispatch(to, ex):
        col = 1 + ex if isinstance(ex, int) else bass.ds(ex + 1, 1)
        col = slice(col, col + 1) if isinstance(ex, int) else col
        for h in range(HALVES):
            last = v.tensor_scalar(to[:, h, :], const("iota"), place[:, h, col], chosen[:, h, col],
                                   ALU.is_equal, ALU.mult)
        return last

    gathered_psum = psum[:, 5 * BANK:7 * BANK].rearrange("p (k s) -> p k s", k=KT)

    def sparse_experts(group, xn, gain, tag):
        names = ("silu_ready", "hidden_rows", "hidden_transposed", "hidden_hi_ready", "hidden_ready",
                 "next_dispatch", "tokens_gathered", "tokens_scaled", "tokens_hi_ready", "tokens_ready",
                 "return_dispatch", "dispatch_transposed", "return_ready", "outputs_hi_ready", "outputs_ready",
                 "outputs_scattered", "outputs_added")
        (silu, rows_done, hT_t, hT_hi, hT_lo, next_p, gathered, scaled, xg_hi_ok, xg_ok,
         ret_p, ret_t, ret_ok, y_hi_ok, y_ok, scattered, added) = (
            ctx.enter_context(nc.semaphore(n + tag)) for n in names)
        E, C = group.E, group.C
        end = group.n0 + 12 * group.steps

        def gathers(cur):
            return cur and cur[3] and not (C > 1 and isinstance(cur[0], int) and cur[0] == E - 1)

        def used_before(i):
            return end if i is None else count_after(group.number(0, i), 0)

        def programs(st):
            s_g, rows = tmp(st, "silu_g", [P, FF]), tmp(st, "hidden_rows", [P, FF])
            h_hi, h_lo = tmp_split(st, "hT", [P, 4, P])
            xg = tmp(st, "xg", [P, KT, P])
            xg_hi, xg_lo = tmp_split(st, "xg", [P, KT, P])
            disp, ret = tmp(st, "dispatch", [P, HALVES, P]), tmp(st, "return_p", [P, HALVES, P])
            retT = tmp(st, "return_pT", [P, HALVES, P], F32R)
            y_hi, y_lo = tmp_split(st, "y", [P, D])
            Y = bank(3, 2)

            def first_gather():
                d, g, c, h, l = (S(n) for n in ("first_dispatch", "first_gathered", "first_scaled", "first_hi", "first_lo"))
                with stage() as block:
                    sync_stage(block)

                    @block.tensor
                    def _(e):
                        e.wait_ge(d.sem, d.at(1))
                        g.inc(gather_rows(xn, disp))

                    @block.vector
                    def _(e):
                        d.inc(make_dispatch(disp, 0))
                        e.wait_ge(g.sem, g.at(1))
                        c.inc(v.tensor_tensor(xg[:], gathered_psum, last_bc(gain[:], P), ALU.mult))
                        e.wait_ge(h.sem, h.at(1))
                        l.inc(v.tensor_tensor(xg_lo[:], xg[:], xg_hi[:].bitcast(F32), ALU.subtract))

                    @block.scalar
                    def _(e):
                        e.wait_ge(c.sem, c.at(1))
                        h.inc(sc.activation(xg_hi[:], xg[:], ACT.Copy))

            def tensor(e):
                def gate_or_up(part, qs, i):
                    for q in qs:
                        num = group.number(4 * part + q, i)
                        e.wait_ge(lo_ready, count_after(num))
                        w = [raw_view(r, FINE, num, 2, FF) for r in (ring_hi, ring_lo)]
                        for a in range(2):
                            k = 2 * q + a
                            last = three_passes(bank(part), [t[:, k, :] for t in (xg_hi, xg_lo)],
                                                [w_[:, a, :] for w_ in w], k == 0, k == KT - 1)
                        last.then_inc(used, 1)

                def body(i, cur, prev, done):
                    if cur:
                        if cur[2] and not (isinstance(cur[0], int) and cur[0] == 0):
                            e.wait_ge(xg_ok, cur[0])
                        if prev:
                            e.wait_ge(silu, i)
                        gate_or_up(0, range(4), i)
                    if prev:
                        e.wait_ge(rows_done, i)
                        for j in range(4):
                            last = pe.transpose(bank(2)[:, j * P:(j + 1) * P], rows[:, j * P:(j + 1) * P], ident)
                        last.then_inc(hT_t, 1)
                    if done is not None:
                        e.wait_ge(ret_p, done + 2)
                        for h in range(HALVES):
                            last = pe.transpose(bank(7)[:, h * P:(h + 1) * P], ret[:, h, :], ident)
                        last.then_inc(ret_t, 1)
                    if cur:
                        gate_or_up(1, range(2), i)
                    if done is not None:
                        e.wait_ge(ret_ok, done + 2)
                        e.wait_ge(y_ok, done + 2)
                        for h in range(HALVES):
                            for c in range(2):
                                to = bank((5 if h == 0 else 3) + c)
                                for m, y in enumerate((y_hi, y_lo)):
                                    last = pe.matmul(to, retT[:, h, :], y[:, c * BANK:(c + 1) * BANK],
                                                     start=(m == 0), stop=(m == 1))
                            last.then_inc(scattered, 1)
                    if cur:
                        gate_or_up(1, range(2, 4), i)
                        if gathers(cur):
                            e.wait_ge(next_p, cur[0] + 1)
                            if C > 1:
                                e.wait_ge(added, cur[0] * 2 + 2)
                            elif done is not None:
                                e.wait_ge(added, done * 2 + 3)
                            gather_rows(xn, disp).then_inc(gathered, 1)
                    if prev:
                        e.wait_ge(hT_lo, i)
                        if done is not None:
                            e.wait_ge(added, done * 2 + 4)
                        for j in range(4):
                            num = group.number(8 + j, i, cur)
                            e.wait_ge(lo_ready, count_after(num))
                            w = [raw_view(r, FINE, num, 1, 1024) for r in (ring_hi, ring_lo)]
                            for c in range(2):
                                last = three_passes(bank(3 + c), [t[:, j, :] for t in (h_hi, h_lo)],
                                                    [w_[:, 0, c * BANK:(c + 1) * BANK] for w_ in w],
                                                    prev[2] and j == 0, prev[3] and j == 3)
                            last.then_inc(used, 1)
                group.iterations(e, body)

            def scalar(e):
                def body(i, cur, prev, done):
                    if cur:
                        for k in range(4):
                            make_hi(e, group.number(k, i))
                    if done is not None:
                        e.wait_ge(used, used_before(i))
                        sc.activation(y_hi[:], Y, ACT.Copy).then_inc(y_hi_ok, 1)
                    if cur:
                        for k in range(4, 8):
                            make_hi(e, group.number(k, i))
                        e.wait_ge(used, count_after(group.number(3, i)))
                        if prev:
                            e.wait_ge(rows_done, i)
                        sc.activation(s_g[:], bank(0), ACT.Silu).then_inc(silu, 1)
                    if prev:
                        e.wait_ge(hT_t, i)
                        sc.activation(h_hi[:].rearrange("p j s -> p (j s)"), bank(2), ACT.Copy).then_inc(hT_hi, 1)
                    if done is not None:
                        e.wait_ge(ret_t, done + 2)
                        sc.activation(retT[:].rearrange("p h t -> p (h t)"), bank(7)[:, 0:SEQ], ACT.Copy).then_inc(ret_ok, 1)
                    if prev:
                        for k in range(8, 12):
                            make_hi(e, group.number(k, i, cur), 1, 1024)
                    if gathers(cur):
                        e.wait_ge(used, count_after(group.number(7, i)))
                        e.wait_ge(scaled, cur[0] + 1)
                        sc.activation(xg_hi[:], xg[:], ACT.Copy).then_inc(xg_hi_ok, 1)
                group.iterations(e, body)

            def vector(e):
                def body(i, cur, prev, done):
                    if done is not None:
                        make_dispatch(ret, done).then_inc(ret_p, 1)
                    if cur:
                        for k in range(4):
                            make_lo(e, group.number(k, i))
                    if done is not None:
                        e.wait_ge(y_hi_ok, done + 2)
                        v.tensor_tensor(y_lo[:], Y, y_hi[:].bitcast(F32), ALU.subtract).then_inc(y_ok, 1)
                    if cur:
                        for k in range(4, 8):
                            make_lo(e, group.number(k, i))
                    if gathers(cur):
                        then_registers(e)
                        make_dispatch(disp, cur[0] + 1).then_inc(next_p, 1)
                    if prev:
                        e.wait_ge(hT_hi, i)
                        v.tensor_tensor(h_lo[:].rearrange("p j s -> p (j s)"), bank(2),
                                        h_hi[:].rearrange("p j s -> p (j s)").bitcast(F32), ALU.subtract).then_inc(hT_lo, 1)
                        for k in (8, 9):
                            make_lo(e, group.number(k, i, cur), 1, 1024)
                    if done is not None:
                        col = slice(done + 1, done + 2) if isinstance(done, int) else bass.ds(done + 1, 1)
                        for h in range(HALVES):
                            e.wait_ge(scattered, done * 2 + 3 + h)
                            then_registers(e)
                            b = 5 if h == 0 else 3
                            v.scalar_tensor_tensor(out=x[:, h, :], in0=bank(b, 2), scalar=comb[:, h, col],
                                                   in1=x[:, h, :], op0=ALU.mult, op1=ALU.add).then_inc(added, 1)
                            e.wait_ge(added, done * 2 + 3 + h)
                    if prev:
                        for k in (10, 11):
                            make_lo(e, group.number(k, i, cur), 1, 1024)
                    if cur:
                        e.wait_ge(used, count_after(group.number(7, i)))
                        e.wait_ge(silu, 1 if isinstance(i, int) and i == 0 else i + 1)
                        v.tensor_tensor(rows[:], s_g[:], bank(1), ALU.mult).then_inc(rows_done, 1)
                    if gathers(cur):
                        e.wait_ge(gathered, cur[0] + 1)
                        v.tensor_tensor(xg[:], gathered_psum, last_bc(gain[:], P), ALU.mult).then_inc(scaled, 1)
                        e.wait_ge(xg_hi_ok, cur[0] + 1)
                        v.tensor_tensor(xg_lo[:], xg[:], xg_hi[:].bitcast(F32), ALU.subtract).then_inc(xg_ok, 1)
                    then_registers(e)
                group.iterations(e, body)
            return first_gather, tensor, scalar, vector
        return programs

    routed = [0]

    def routed_experts(xn, gain):
        place_tokens(N_EXP2 if routed[0] else N_EXP1)
        routed[0] += 1
        group, after = take_group()
        tag = f"_of_moe{routed[0]}"
        with ExitStack() as st:
            programs, counted = dense_experts(group, lambda h, ex: comb[:, h, slice(ex + 1, ex + 2) if isinstance(ex, int)
                                                                        else bass.ds(ex + 1, 1)], "_dense" + tag)
            dense = programs(st)
            first_gather, *sparse = sparse_experts(group, xn, gain, tag)(st)
            first_gather()
            with stage() as block:
                taken[0] = after
                experts_sync(block, group)

                def either(e, few, many):
                    count = e.value_load(largest[0:1, 0:1], min_val=0, max_val=SEQ)
                    with e.If(count < P + 1):
                        few(e)
                    with e.Else():
                        many(e)

                @block.tensor
                def _(e):
                    either(e, sparse[0], dense[0])

                @block.scalar
                def _(e):
                    either(e, sparse[1], dense[1])

                @block.vector
                def _(e):
                    either(e, sparse[2], dense[2])

    def all_tokens_experts(combine):
        group, after = take_group()
        with ExitStack() as st:
            programs, counted = dense_experts(group, combine, "")
            tensor, scalar, vector = programs(st)
            with stage() as block:
                taken[0] = after
                experts_sync(block, group)
                block.tensor(tensor)
                block.scalar(scalar)
                block.vector(vector)
        for s in counted:
            s.total += group.steps

    def route(jobs, finish):
        done = S("router_ready")
        with stage() as block:
            sync_stage(block)

            @block.tensor
            def _(e):
                for w, c, n in jobs:
                    for h in range(HALVES):
                        for k in range(KT):
                            for m, part in enumerate(xT):
                                last = pe.matmul(bank(h)[:, c:c + n], part[:, k, h * P:(h + 1) * P].bitcast(F32),
                                                 w[:, k, :], start=(k == 0 and m == 0), stop=(k == KT - 1 and m == 1))
                done.inc(last)

            finish(block, done)

    logits_psum = psum[:, 0:HALVES * BANK].rearrange("p (h c) -> p h c", h=HALVES)

    def make_step(e):
        dve = S("dve_chain")

        def step(ins, sig=dve):
            sig.inc(ins)
            e.wait_ge(sig.sem, sig.total)
        return step

    def pick(step, scores, n, best, cand, idx, onehot):
        step(v.tensor_reduce(best, scores, AXX, ALU.max))
        step(v.tensor_tensor(cand, scores, last_bc(best, n), ALU.is_equal))
        step(v.scalar_tensor_tensor(out=cand, in0=cand, scalar=-64.0, in1=row_bc(const("iota")[:, 0:n], [HALVES]),
                                    op0=ALU.mult, op1=ALU.add))
        step(v.tensor_reduce(idx, cand, AXX, ALU.min))
        step(v.tensor_tensor(onehot, cand, last_bc(idx, n), ALU.is_equal))

    def top_two_weights(e, step, scores, n, out_w, out_mask, t, other=None):
        best1, best2, idx, cand, one1, one2, left = t
        diff_ready, diff_exp = S("top_two_difference"), S("top_two_exp")
        pick(step, scores, n, best1, cand, idx, one1)
        step(v.scalar_tensor_tensor(out=left, in0=one1, scalar=-3e38, in1=scores, op0=ALU.mult, op1=ALU.add))
        pick(step, left, n, best2, cand, idx, one2)
        step(v.tensor_tensor(out_mask, one1, one2, ALU.add))
        step(v.tensor_tensor(best2, best2, best1, ALU.subtract), diff_ready)
        e.wait_ge(diff_exp.sem, diff_exp.at(1))
        step(v.tensor_scalar(best1, best2, 1.0, None, ALU.add))
        step(v.reciprocal(best1, best1))
        step(v.tensor_tensor(best2, best2, best1, ALU.mult))
        if other is not None:
            step(v.tensor_tensor(best1, best1, other, ALU.mult))
            step(v.tensor_tensor(best2, best2, other, ALU.mult))
        step(v.tensor_tensor(one1, one1, last_bc(best1, n), ALU.mult))
        step(v.tensor_tensor(one2, one2, last_bc(best2, n), ALU.mult))
        step(v.tensor_tensor(out_w, one1, one2, ALU.add))

    def hybrid_mixers(layer, L2):
        loads = []

        def par(name, shape, src):
            t = tmp(L2, name, shape)
            loads.append((t, src))
            return t

        qk_gain = par("nsa_gain", [P, 4, HD], A["nsa_qk_gain_2"][layer].rearrange("a d -> (a d)").partition_broadcast(P)
                      .rearrange("p (a d) -> p a d", a=4))
        d_gain = par("diff_gain", [P, 2, DIFF_QK], A["diff_qk_gain_2"][layer].rearrange("a d -> (a d)").partition_broadcast(P)
                     .rearrange("p (a d) -> p a d", a=2))
        lam_p = par("diff_lambda", [P, 4, DIFF_QK], A["diff_lambda_2"][layer].rearrange("a d -> (a d)").partition_broadcast(P)
                    .rearrange("p (a d) -> p a d", a=4))
        d_norm = par("diff_norm", [P, HD], A["diff_norm_2"][layer].partition_broadcast(P))
        w_gate2 = par("gla_w_gate2", [GLA_RANK, MH * GLA_DK], A["gla_w_gate2_2"][layer])
        b_gate = par("gla_b_gate", [P, MH * GLA_DK], A["gla_b_gate_2"][layer].partition_broadcast(P))
        gla_gain = par("gla_gain", [P, HD], A["gla_norm_2"][layer].partition_broadcast(P))
        hg_gain = par("hgrn_gain", [P, HD], A["hgrn_norm_2"][layer].partition_broadcast(P))
        cmp_w2 = par("cmp_w2", [P, 2, 2, HD], A["nsa_cmp_w2_2"][layer].rearrange("j (c p) d -> p j c d", p=P))
        pos = tmp(L2, "cmp_pos", [P, CMP_LEN])
        u = tmp(L2, "u2", [P, HALVES, IN2_COLS])
        mix = tmp(L2, "mix", [P, HALVES, D])
        lam = tmp(L2, "lam", [P, 2])
        lam_init = 0.8 - 0.6 * math.exp(-0.3 * layer)
        with stage() as block:
            @block.sync
            def _(sp):
                for dst, src in loads:
                    params_loaded.inc(sp.dma_start(dst[:], src), 16)
                for j in range(2):
                    params_loaded.inc(sp.dma_start(pos[j * HD:(j + 1) * HD, :],
                                                   A["nsa_cmp_pos_2"][layer, j]), 16)
                issue_loads(sp)
                sp.wait_ge(params_loaded.sem, params_loaded.total)
        normed_T(x, g_attn2[layer], xT)
        product(xT, KT, IN2_COLS, copy_to=u)

        def uc(name, lo=0, width=None):
            a, w = IN2[name]
            return u[:, :, a + lo:a + (w if width is None else lo + width)]

        def heads_of(ap, d):
            return ap.rearrange("p h (n d) -> p h n d", d=d)

        with ExitStack() as st:
            nq = tmp(st, "nq", [P, HALVES, MH, HD])
            nks = tmp(st, "nks", [P, HALVES, 1, HD])
            nkw = tmp(st, "nkw", [P, HALVES, 1, HD])
            group_norms([(heads_of(uc("nq"), HD), nq[:], qk_gain[:, 0, :], HD),
                         (heads_of(uc("ks"), HD), nks[:], qk_gain[:, 2, :], HD),
                         (heads_of(uc("kw"), HD), nkw[:], qk_gain[:, 3, :], HD)])
            qT = tmp(st, "nqT", [HD, MH + 2, SEQ])
            transposes([nq[:, h, n, :] for n in range(MH) for h in range(HALVES)]
                       + [k[:, h, 0, :] for k in (nks, nkw) for h in range(HALVES)], HD,
                       qT[:].rearrange("p n t -> p (n t)"))
            kvT = tmp(st, "kvT", [P, SEQ])
            a0 = IN2["kc"][0]
            transposes([u[:, h, a0:a0 + 2 * HD] for h in range(HALVES)], P, kvT[:])
            blocks = tmp(st, "cmp_blocks", [P, CMP_LEN, N_CMP])
            blocks_split = tmp_split(st, "cmp_blocks", [P, CMP_LEN, N_CMP])
            hid, hid_e = (tmp(st, n, [N_CMP, 2, CMP_HID]) for n in ("cmp_hid", "cmp_sig"))
            hidT = tmp(st, "cmp_hidT", [P, 4, N_CMP])
            ckv = tmp(st, "ckv", [N_CMP, 2, HD])
            csq, css, crt = tmp(st, "csq", [N_CMP, HD]), tmp(st, "css", [N_CMP, 1]), tmp(st, "crt", [N_CMP, 1])
            ckT = tmp(st, "ckT", [HD, N_CMP])
            got = take(CMP_PIECES)
            ready, ready_hi, sig, act_hid, hT, hTc, out2, ssr, root, kn, knT = (S(n) for n in (
                "blocks_ready", "blocks_hi_ready", "hidden_sigmoid", "hidden_active", "hidden_transposed", "hiddenT_copied",
                "compressed_ready", "group_sums", "group_roots", "key_normed", "key_transposed"))
            with stage() as block:
                sync_stage(block)

                @block.vector
                def _(e):
                    step = make_step(e)
                    for l in range(CMP_LEN):
                        last = v.tensor_scalar(blocks[:, l, :], kvT[:, l:l + CMP_STRIDE * (N_CMP - 1) + 1:CMP_STRIDE],
                                               pos[:, l:l + 1], None, ALU.add)
                    ready.inc(last)
                    e.wait_ge(ready_hi.sem, ready_hi.at(1))
                    ready.inc(v.tensor_tensor(blocks_split[1][:], blocks[:], blocks_split[0][:].bitcast(F32), ALU.subtract))
                    make_los(e, got)
                    e.wait_ge(sig.sem, sig.at(2))
                    for j in range(2):
                        last = v.tensor_tensor(hid[:, j, :], bank(j)[0:N_CMP, 0:CMP_HID], hid_e[:, j, :], ALU.mult)
                    act_hid.inc(last)
                    e.wait_ge(hT.sem, hT.at(1))
                    hTc.inc(v.tensor_copy(hidT[:], bank(2)[:, 0:4 * P].rearrange("p (n k) -> p n k", n=4)[:, :, 0:N_CMP]))
                    e.wait_ge(out2.sem, out2.at(1))
                    step(v.tensor_copy(ckv[:], bank(3)[0:N_CMP, 0:2 * HD].rearrange("p (j d) -> p j d", j=2)))
                    step(v.tensor_tensor(csq[:], ckv[:, 0, :], ckv[:, 0, :], ALU.mult))
                    step(v.tensor_reduce(css[:], csq[:], AXX, ALU.add), ssr)
                    e.wait_ge(root.sem, root.at(1))
                    step(v.reciprocal(css[:], crt[:]))
                    step(v.tensor_scalar(csq[:], ckv[:, 0, :], css[:], None, ALU.mult))
                    step(v.tensor_tensor(csq[:], csq[:], qk_gain[0:N_CMP, 1, :], ALU.mult), kn)
                    e.wait_ge(knT.sem, knT.at(1))
                    step(v.tensor_copy(ckT[:], bank(4)[0:HD, 0:N_CMP]))

                @block.scalar
                def _(e):
                    e.wait_ge(ready.sem, ready.at(1))
                    ready_hi.inc(sc.activation(blocks_split[0][:], blocks[:], ACT.Copy))
                    make_his(e, got)
                    e.wait_ge(used, got[-1].n + 1)
                    for j in range(2):
                        sig.inc(sc.activation(hid_e[:, j, :], bank(j)[0:N_CMP, 0:CMP_HID], ACT.Sigmoid))
                    e.wait_ge(ssr.sem, ssr.at(1))
                    root.inc(sc.activation(crt[:], css[:], ACT.Sqrt, scale=1.0 / HD, bias=eps[0:N_CMP, :]))

                @block.tensor
                def _(e):
                    e.wait_ge(ready.sem, ready.at(2))
                    for q, p in enumerate(got):
                        e.wait_ge(lo_ready, p.n + 1)
                        w = [raw_view(r, FINE, (p.n, 0), 4, CMP_HID) for r in (ring_hi, ring_lo)]
                        for a in range(4):
                            l = 4 * q + a
                            for j in range(2):
                                rows = slice(j * HD, (j + 1) * HD)
                                last = three_passes(bank(j)[0:N_CMP, 0:CMP_HID], [b_[rows, l, :] for b_ in blocks_split],
                                                    [w_[rows, a, :] for w_ in w], l == 0, l == CMP_LEN - 1)
                        last.then_inc(used, 1)
                    e.wait_ge(act_hid.sem, act_hid.at(1))
                    for n in range(4):
                        last = pe.transpose(bank(2)[:, n * P:n * P + N_CMP], hid[:, n // 2, (n % 2) * P:(n % 2 + 1) * P],
                                            ident[0:N_CMP, 0:N_CMP])
                    hT.inc(last)
                    e.wait_ge(hTc.sem, hTc.at(1))
                    for j in range(2):
                        for c in range(2):
                            last = pe.matmul(bank(3)[0:N_CMP, j * HD:(j + 1) * HD], hidT[:, 2 * j + c, :], cmp_w2[:, j, c, :],
                                             start=(c == 0), stop=(c == 1))
                    out2.inc(last)
                    e.wait_ge(kn.sem, kn.at(1))
                    knT.inc(pe.transpose(bank(4)[0:HD, 0:N_CMP], csq[:], ident[0:N_CMP, 0:N_CMP]))
            gate = tmp(st, "nsa_gate", [P, HALVES, MH, 3])
            gates = S("gates_ready")
            with stage() as block:
                sync_stage(block)

                @block.scalar
                def _(e):
                    gates.inc(sc.activation(gate[:], uc("ng").rearrange("p h (n b) -> p h n b", b=3), ACT.Sigmoid))
            for h in range(HALVES):
                dst = mix[:, h, 0:MH * HD].rearrange("p (n d) -> p n d", d=HD)

                def weight(b, h=h):
                    return lambda step, r: step(v.tensor_tensor(r, r, gate[:, h, :, b], ALU.mult))
                qs = [qT[:, n, h * P:(h + 1) * P] for n in range(MH)]
                attend([(q, ckT[:], [ckv[:, 1, :]]) for q in qs], N_CMP, HD, HD ** -0.5, weight(0), dst,
                       mask=const("cmp_add")[:, h * N_CMP:(h + 1) * N_CMP],
                       keep=const("cmp_mul")[:, h * N_CMP:(h + 1) * N_CMP])
                for b, keys, vals in ((1, MH, "vs"), (2, MH + 1, "vw")):
                    attend([(q, qT[:, keys, :], [uc(vals)[:, k, :] for k in range(HALVES)]) for q in qs], SEQ, HD,
                           HD ** -0.5, weight(b), dst, mask=const("causal")[:, h * SEQ:(h + 1) * SEQ], accumulate=True)

        with ExitStack() as st:
            n2 = 2 * MH
            dq, dk = (tmp(st, n, [P, HALVES, n2, DIFF_QK]) for n in ("dq", "dk"))
            group_norms([(heads_of(uc("dq"), DIFF_QK), dq[:], d_gain[:, 0, :], DIFF_QK),
                         (heads_of(uc("dk"), DIFF_QK), dk[:], d_gain[:, 1, :], DIFF_QK)])
            dqT, dkT = (tmp(st, n, [DIFF_QK, n2, SEQ]) for n in ("dqT", "dkT"))
            for src, dst in ((dq, dqT), (dk, dkT)):
                transposes([src[:, h, n, :] for n in range(n2) for h in range(HALVES)], DIFF_QK,
                           dst[:].rearrange("p n t -> p (n t)"))
            prod, dots = tmp(st, "lam_prod", [P, 2, DIFF_QK]), tmp(st, "lam_dots", [P, 2])
            dots_ready, exp_ready = S("group_sums"), S("exp_ready")
            with stage() as block:
                sync_stage(block)

                @block.vector
                def _(e):
                    step = make_step(e)
                    pairs = lam_p[:].rearrange("p (a two) d -> p a two d", two=2)
                    step(v.tensor_tensor(prod[:], pairs[:, :, 0, :], pairs[:, :, 1, :], ALU.mult))
                    step(v.tensor_reduce(dots[:], prod[:], AXX, ALU.add), dots_ready)
                    e.wait_ge(exp_ready.sem, exp_ready.at(1))
                    step(v.tensor_tensor(lam[:, 0:1], dots[:, 1:2], dots[:, 0:1], ALU.subtract))
                    step(v.tensor_scalar(lam[:, 0:1], lam[:, 0:1], -lam_init, None, ALU.add))

                @block.scalar
                def _(e):
                    e.wait_ge(dots_ready.sem, dots_ready.at(1))
                    exp_ready.inc(sc.activation(dots[:], dots[:], ACT.Exp))
            o8 = tmp(st, "o8", [P, HALVES, n2, HD])
            for h in range(HALVES):
                def weight(step, r):
                    second = r.rearrange("p (n c) -> p n c", c=2)[:, :, 1]
                    step(v.tensor_scalar(second, second, lam[:, 0:1], None, ALU.mult))
                attend([(dqT[:, n, h * P:(h + 1) * P], dkT[:, n, :],
                         [uc("dv", (n // 2) * HD, HD)[:, k, :] for k in range(HALVES)]) for n in range(n2)],
                       SEQ, HD, DIFF_QK ** -0.5, weight, o8[:, h, :, :],
                       mask=const("causal")[:, h * SEQ:(h + 1) * SEQ])
            od = tmp(st, "od", [P, HALVES, MH, HD])
            dve = S("dve_chain")
            with stage() as block:
                sync_stage(block)

                @block.vector
                def _(e):
                    for h in range(HALVES):
                        both = o8[:, h, :, :].rearrange("p (n c) d -> p n c d", c=2)
                        dve.inc(v.tensor_tensor(od[:, h, :, :], both[:, :, 0, :], both[:, :, 1, :], ALU.add))
                    dve.inc(v.tensor_scalar(d_norm[:], d_norm[:], 1.0 - lam_init, None, ALU.mult))
            group_norms([(od[:], heads_of(mix[:, :, 256:512], HD), d_norm[:], HD)])

        def linear_attention(q, k, log_g, vals, groups, dk, dst):
            nh = P // dk
            with ExitStack() as st:
                qkT = tmp(st, "qkT", [P, 2, SEQ])
                decay = tmp(st, "decay", [P, N_LEVELS + 1, P])
                QD = tmp(st, "QD", [P, HALVES, N_LEVELS + 2, P])
                KD = tmp(st, "KD", [P, HALVES, N_LEVELS + 2, P])
                pairs = tmp(st, "pairs", [P, 2, N_LEVELS + 1, P])
                cross = tmp(st, "cross", [P, 2, P])
                for g in range(groups):
                    cols = slice(g * P, (g + 1) * P)
                    transposes([a[:, h, cols] for a in (q, k) for h in range(HALVES)], P,
                               qkT[:].rearrange("p a t -> p (a t)"))
                    exps, exped, dve, decayed = S("exponents_ready"), S("exp_ready"), S("dve_chain"), S("decayed")
                    with stage() as block:
                        sync_stage(block)

                        @block.tensor
                        def _(e):
                            for h in range(HALVES):
                                if h:
                                    e.wait_ge(exped.sem, exped.at(h))
                                pe.matmul(bank(0), log_g[:, h, cols], const("gate_sums")[:, 0:4 * P], start=True, stop=True)
                                pe.matmul(bank(1)[:, 0:3 * P], log_g[:, h, cols], const("gate_sums")[:, 4 * P:7 * P],
                                          start=True, stop=True)
                                exps.inc(pe.matmul(bank(1)[:, 3 * P:4 * P], log_g[:, h, cols],
                                                   const("gate_cross")[:, h * P:(h + 1) * P], start=True, stop=True))

                        @block.scalar
                        def _(e):
                            for h in range(HALVES):
                                e.wait_ge(exps.sem, exps.at(h + 1))
                                if h:
                                    e.wait_ge(decayed.sem, decayed.at(h))
                                exped.inc(sc.activation(decay[:].rearrange("p l t -> p (l t)"), bank(0, 2), ACT.Exp))

                        @block.vector
                        def _(e):
                            for h in range(HALVES):
                                tok = slice(h * P, (h + 1) * P)
                                v.tensor_copy(QD[:, h, N_LEVELS + 1, :], qkT[:, 0, tok])
                                dve.inc(v.tensor_copy(KD[:, h, N_LEVELS + 1, :], qkT[:, 1, tok]))
                                e.wait_ge(exped.sem, exped.at(h + 1))
                                for a, to in ((0, QD), (1, KD)):
                                    last = v.tensor_tensor(to[:, h, 0:N_LEVELS + 1, :], decay[:],
                                                           row_bc(qkT[:, a, tok], [N_LEVELS + 1]), ALU.mult)
                                decayed.inc(last)
                    in_half = [*range(N_LEVELS), N_LEVELS + 1]
                    ready, masked, masked_a, o, taken_o = (S(n) for n in (
                        "pairs_ready", "pairs_masked", "cross_copied", "attended", "output_copied"))
                    jobs = [(h, n) for h in range(HALVES) for n in range(nh)]
                    with stage() as block:
                        sync_stage(block)

                        @block.tensor
                        def _(e):
                            def pv(m):
                                h, n = jobs[m]
                                e.wait_ge(masked.sem, masked.at(m + 1))
                                if h:
                                    e.wait_ge(masked_a.sem, masked_a.at(m - nh + 1))
                                if m >= 2:
                                    e.wait_ge(taken_o.sem, taken_o.at(m - 1))
                                to = bank(6 + m % 2)[:, 0:HD]
                                va = [vals[:, hh, (g * nh + n) * HD:(g * nh + n + 1) * HD] for hh in range(HALVES)]
                                for l in range(N_LEVELS + 1):
                                    last = pe.matmul(to, pairs[:, m % 2, l, :], va[h], start=(l == 0),
                                                     stop=(l == N_LEVELS and h == 0))
                                if h:
                                    last = pe.matmul(to, cross[:, m % 2, :], va[0], start=False, stop=True)
                                o.inc(last)

                            for m, (h, n) in enumerate(jobs):
                                ch = slice(n * dk, (n + 1) * dk)
                                if m >= 2:
                                    e.wait_ge(masked.sem, masked.at(m - 1))
                                    if h and m - 2 >= nh:
                                        e.wait_ge(masked_a.sem, masked_a.at(m - 1 - nh))
                                for s, l in enumerate(in_half):
                                    last = pe.matmul(psum[:, (m % 2) * 2 * BANK + s * P:(m % 2) * 2 * BANK + (s + 1) * P],
                                                     KD[ch, h, l, :], QD[ch, h, l, :], start=True, stop=True)
                                if h:
                                    last = pe.matmul(bank(4 + m % 2)[:, 0:P], KD[ch, 0, N_LEVELS, :],
                                                     QD[ch, 1, N_LEVELS, :], start=True, stop=True)
                                ready.inc(last)
                                if m:
                                    pv(m - 1)
                            pv(len(jobs) - 1)

                        @block.vector
                        def _(e):
                            def take_out(m):
                                h, n = jobs[m]
                                e.wait_ge(o.sem, o.at(m + 1))
                                taken_o.inc(v.tensor_copy(dst[:, h, g * nh + n, :], bank(6 + m % 2)[:, 0:HD]))

                            for m, (h, n) in enumerate(jobs):
                                e.wait_ge(ready.sem, ready.at(m + 1))
                                if m >= 2:
                                    e.wait_ge(o.sem, o.at(m - 1))
                                masked.inc(v.tensor_tensor(
                                    pairs[:, m % 2, :, :].rearrange("p l t -> p (l t)"),
                                    psum[:, (m % 2) * 2 * BANK:(m % 2 + 1) * 2 * BANK], const("level_mask"), ALU.mult))
                                if m:
                                    take_out(m - 1)
                            take_out(len(jobs) - 1)

                        @block.scalar
                        def _(e):
                            for m, (h, n) in enumerate(jobs):
                                if h:
                                    e.wait_ge(ready.sem, ready.at(m + 1))
                                    if m >= 2:
                                        e.wait_ge(o.sem, o.at(m - 1))
                                    masked_a.inc(sc.activation(cross[:, m % 2, :], bank(4 + m % 2)[:, 0:P], ACT.Copy))

        def gated_output(o, gain, gate_name, dst):
            sig, dve = S("gates_ready"), S("dve_chain")
            with ExitStack() as st:
                sg = tmp(st, "sg", [P, HALVES, MH * HD])
                group_norms([(o[:], heads_of(dst, HD), gain[:], HD)])
                with stage() as block:
                    sync_stage(block)

                    @block.scalar
                    def _(e):
                        sig.inc(sc.activation(sg[:], uc(gate_name), ACT.Silu))

                    @block.vector
                    def _(e):
                        e.wait_ge(sig.sem, sig.at(1))
                        dve.inc(v.tensor_tensor(dst, dst, sg[:], ALU.mult))

        with ExitStack() as st:
            gT = tmp(st, "glrT", [GLA_RANK, SEQ])
            transposes([uc("glr")[:, h, :] for h in range(HALVES)], GLA_RANK, gT[:])
            lg, ab, mn = (tmp(st, n, [P, HALVES, MH * GLA_DK]) for n in ("lg", "gabs", "gmin"))
            pre, abs_ready, log_ready = S("router_ready"), S("gate_abs"), S("gate_log")
            with stage() as block:
                sync_stage(block)

                @block.tensor
                def _(e):
                    for h in range(HALVES):
                        last = pe.matmul(bank(h)[:, 0:P], gT[:, h * P:(h + 1) * P], w_gate2[:], start=True, stop=True)
                    pre.inc(last)

                @block.vector
                def _(e):
                    step = make_step(e)
                    e.wait_ge(pre.sem, pre.at(1))
                    step(v.tensor_tensor(lg[:], logits_psum[:, :, 0:P], row_bc(b_gate[:], [HALVES]), ALU.add))
                    step(v.tensor_scalar(mn[:], lg[:], 0.0, 1.0 / GLA_TAU, ALU.min, ALU.mult))
                    step(v.scalar_tensor_tensor(out=ab[:], in0=lg[:], scalar=-1.0, in1=lg[:], op0=ALU.mult, op1=ALU.max), abs_ready)
                    e.wait_ge(log_ready.sem, log_ready.at(1))
                    step(v.scalar_tensor_tensor(out=lg[:], in0=ab[:], scalar=-1.0 / GLA_TAU, in1=mn[:],
                                                op0=ALU.mult, op1=ALU.add))
                    step(v.tensor_scalar(uc("gq"), uc("gq"), GLA_DK ** -0.5, None, ALU.mult))

                @block.scalar
                def _(e):
                    act = S("act_chain")
                    e.wait_ge(abs_ready.sem, abs_ready.at(1))
                    act.inc(sc.activation(ab[:], ab[:], ACT.Exp, scale=-1.0))
                    e.wait_ge(act.sem, act.total)
                    log_ready.inc(sc.activation(ab[:], ab[:], ACT.Ln, scale=1.0, bias=const("all_ones")[:, 0:1]))
            o = tmp(st, "o_gla", [P, HALVES, MH, HD])
            linear_attention(uc("gq"), uc("gk"), lg, uc("gv"), 1, GLA_DK, o)
            gated_output(o, gla_gain, "gog", mix[:, :, 512:768])

        with ExitStack() as st:
            f, k1 = (tmp(st, n, [P, HALVES, MH * HD]) for n in ("forget", "hkeys"))
            lb, top = (tmp(st, n, [P, MH * HD]) for n in ("lower_bound", "lb_max"))
            ex = tmp(st, "lb_exp", [P, LAYERS, MH * HD])
            sig, lb_ready, lb_exp, f_ready, log_ready = (S(n) for n in (
                "gates_ready", "bounds_shifted", "bounds_exp", "forget_ready", "gate_log"))
            with stage() as block:
                sync_stage(block)

                @block.scalar
                def _(e):
                    if layer:
                        e.wait_ge(lb_ready.sem, lb_ready.at(1))
                        lb_exp.inc(sc.activation(ex[:], ex[:], ACT.Exp))
                    sc.activation(f[:], uc("rf"), ACT.Sigmoid)
                    sig.inc(sc.activation(k1[:], uc("rf"), ACT.Sigmoid, scale=-1.0))
                    e.wait_ge(f_ready.sem, f_ready.at(1))
                    log_ready.inc(sc.activation(f[:], f[:], ACT.Ln))

                @block.vector
                def _(e):
                    step = make_step(e)
                    if layer:
                        step(v.tensor_tensor(top[:], hg_logits[:, 0, :], hg_logits[:, 1, :], ALU.max))
                        step(v.tensor_tensor(ex[:], hg_logits[:], row_bc(top[:], [LAYERS]), ALU.subtract), lb_ready)
                        e.wait_ge(lb_exp.sem, lb_exp.at(1))
                        step(v.tensor_tensor(top[:], ex[:, 0, :], ex[:, 1, :], ALU.add))
                        step(v.reciprocal(top[:], top[:]))
                        step(v.tensor_tensor(lb[:], ex[:, 1, :], top[:], ALU.mult))
                        step(v.tensor_scalar(top[:], lb[:], -1.0, 1.0, ALU.mult, ALU.add))
                    e.wait_ge(sig.sem, sig.at(1))
                    if layer:
                        for a in (f, k1):
                            step(v.tensor_tensor(a[:], a[:], row_bc(top[:], [HALVES]), ALU.mult))
                        step(v.tensor_tensor(f[:], f[:], row_bc(lb[:], [HALVES]), ALU.add))
                    step(v.tensor_scalar(f[:], f[:], 2.0 ** -63, None, ALU.max), f_ready)
                    e.wait_ge(log_ready.sem, log_ready.at(1))
                    step(v.tensor_scalar(f[:], f[:], 0.0, None, ALU.min))
            o = tmp(st, "o_hgrn", [P, HALVES, MH, HD])
            linear_attention(uc("rq"), k1, f, uc("ri"), 2, HD, o)
            gated_output(o, hg_gain, "rog", mix[:, :, 768:1024])

        transposes([mix[:, h, k * P:(k + 1) * P] for k in range(KT) for h in range(HALVES)], P,
                   flat(xT))
        product(xT, KT, D, add_to=x)

    with stage() as block:
        @block.sync
        def _(sp):
            for dst, src in small:
                params_loaded.inc(sp.dma_start(dst, src), 16)
            issue_loads(sp)
            sp.wait_ge(params_loaded.sem, params_loaded.total)

    comb, chosen, place = (sb(n, [P, HALVES, N_EXP1 + 2]) for n in ("comb", "chosen", "place"))
    largest = ctx.enter_context(nc.sbuf_tensor("largest_count", [P, 1], mybir.dt.int32))

    def clear_routing():
        with stage() as block:
            sync_stage(block)
            dve = S("dve_chain")

            @block.vector
            def _(e):
                for t in (comb, chosen, place):
                    last = v.memset(t[:], 0.0)
                v.memset(bank(3, 2), 0.0)
                dve.inc(last)

    def place_tokens(n):
        counted, dve = S("tokens_counted"), S("dve_chain")
        with ExitStack() as st:
            top = tmp(st, "top_count", [P, 1])
            with stage() as block:
                sync_stage(block)

                @block.tensor
                def _(e):
                    before, ones = const("before"), const("all_ones")
                    m = [chosen[:, h, 1:n + 1] for h in range(HALVES)]
                    pe.matmul(bank(0)[:, 0:n], before, m[0], start=True, stop=True)
                    pe.matmul(bank(1)[:, 0:n], before, m[1], start=True, stop=False)
                    pe.matmul(bank(1)[:, 0:n], ones, m[0], start=False, stop=True)
                    pe.matmul(bank(2)[:, 0:n], ones, m[0], start=True, stop=False)
                    counted.inc(pe.matmul(bank(2)[:, 0:n], ones, m[1], start=False, stop=True))

                @block.vector
                def _(e):
                    step = make_step(e)
                    e.wait_ge(counted.sem, counted.at(1))
                    step(v.tensor_copy(place[:, :, 1:n + 1], logits_psum[:, :, 0:n]))
                    step(v.tensor_reduce(top[:], bank(2)[:, 0:n], AXX, ALU.max))
                    step(v.tensor_copy(largest[:], top[:]))

    with ExitStack() as L1:
        z = tmp(L1, "z", [P, HALVES, IN1_COLS])
        normed_T(x, g_mix, xT)
        product(xT, KT, IN1_COLS, copy_to=z)

        def zc(name, lo=0, width=None):
            a, w = IN1[name]
            return z[:, :, a + lo:a + (w if width is None else lo + width)]

        y_att = tmp(L1, "y_att", [P, HALVES, D])
        with ExitStack() as st:
            qn, kn = (zc(n).rearrange("p h (n d) -> p h n d", d=HD) for n in ("q", "k"))
            group_norms([(qn, qn, g_q[:], HD), (kn, kn, g_k[:], HD)])
            qr = tmp(st, "qr", [P, HALVES, ATT_HEADS, HD])
            kr = tmp(st, "kr", [P, HALVES, ATT_KV, HD])
            t1 = tmp(st, "t1", [P, ATT_HEADS, HD // 2])
            t2 = tmp(st, "t2", [P, ATT_HEADS, HD // 2])
            with stage() as block:
                sync_stage(block)

                @block.vector
                def _(e):
                    step = make_step(e)
                    for src, dst, nh in ((qn, qr, ATT_HEADS), (kn, kr, ATT_KV)):
                        for h in range(HALVES):
                            x0, x1 = (src[:, h, :, :].rearrange("p n (d two) -> p n d two", two=2)[:, :, :, i] for i in range(2))
                            o0, o1 = (dst[:, h, :, :].rearrange("p n (d two) -> p n d two", two=2)[:, :, :, i] for i in range(2))
                            cos = row_bc(const("cos")[:, h * 32:(h + 1) * 32], [nh])
                            sin = row_bc(const("sin")[:, h * 32:(h + 1) * 32], [nh])
                            step(v.tensor_tensor(t1[:, 0:nh, :], x0, cos, ALU.mult))
                            step(v.tensor_tensor(t2[:, 0:nh, :], x1, sin, ALU.mult))
                            step(v.tensor_tensor(o0, t1[:, 0:nh, :], t2[:, 0:nh, :], ALU.subtract))
                            step(v.tensor_tensor(t1[:, 0:nh, :], x0, sin, ALU.mult))
                            step(v.tensor_tensor(t2[:, 0:nh, :], x1, cos, ALU.mult))
                            step(v.tensor_tensor(o1, t1[:, 0:nh, :], t2[:, 0:nh, :], ALU.add))
            qT = tmp(st, "qT", [HD, ATT_HEADS, SEQ])
            kT = tmp(st, "kT", [HD, ATT_KV, SEQ])
            transposes([qr[:, h, n, :] for n in range(ATT_HEADS) for h in range(HALVES)], HD,
                       qT[:].rearrange("p n t -> p (n t)"))
            transposes([kr[:, h, n, :] for n in range(ATT_KV) for h in range(HALVES)], HD,
                       kT[:].rearrange("p n t -> p (n t)"))
            att = tmp(st, "att", [P, HALVES, ATT_HEADS, HD])
            for h in range(HALVES):
                attend([(qT[:, n, h * P:(h + 1) * P], kT[:, n // 4, :],
                         [zc("v", (n // 4) * HD, HD)[:, k, :] for k in range(HALVES)]) for n in range(ATT_HEADS)],
                       SEQ, HD, HD ** -0.5, None, att[:, h, :, :])
            attT = tmp_split(st, "attT", [P, 4, SEQ])
            att_rows = att[:].rearrange("p h n d -> p h (n d)")
            transposes([att_rows[:, h, k * P:(k + 1) * P] for k in range(4) for h in range(HALVES)], P,
                       flat(attT))
            product(attT, 4, D, copy_to=y_att)

        y_sgu = tmp(L1, "y_sgu", [P, HALVES, D])
        with ExitStack() as st:
            sgu_ln_g = tmp(st, "sgu_g", [P, SGU_W])
            sgu_ln_b = tmp(st, "sgu_b", [P, SGU_W])
            w_sT = tmp(st, "w_sT", [P, SGU_G, P])
            u = tmp(st, "u", [P, HALVES, SGU_W])
            vn = tmp(st, "vn", [P, HALVES, SGU_W])
            sq = tmp(st, "sgu_sq", [P, HALVES, SGU_W])
            mean, var, rt = (tmp(st, n, [P, HALVES]) for n in ("mean", "var", "rt"))
            gelu, var_ready, root = S("gelu_ready"), S("group_sums"), S("group_roots")
            with stage() as block:
                @block.sync
                def _(sp):
                    for dst, src in ((sgu_ln_g[:], A["sgu_ln_g"][0].partition_broadcast(P)),
                                     (sgu_ln_b[:], A["sgu_ln_b"][0].partition_broadcast(P)),
                                     (w_sT[:], A["w_s"][0].rearrange("g q p -> q g p"))):
                        params_loaded.inc(sp.dma_start(dst, src), 16)
                    issue_loads(sp)

                @block.scalar
                def _(e):
                    gelu.inc(sc.activation(vn[:], zc("sv"), ACT.Gelu_apprx_tanh))
                    gelu.inc(sc.activation(u[:], zc("su"), ACT.Gelu_apprx_tanh))
                    e.wait_ge(var_ready.sem, var_ready.at(1))
                    root.inc(sc.activation(rt[:], var[:], ACT.Sqrt, scale=1.0 / SGU_W, bias=eps))

                @block.vector
                def _(e):
                    step = make_step(e)
                    e.wait_ge(gelu.sem, gelu.at(1))
                    step(v.tensor_reduce(mean[:], vn[:], AXX, ALU.add))
                    step(v.tensor_scalar(mean[:], mean[:], 1.0 / SGU_W, None, ALU.mult))
                    step(v.tensor_tensor(vn[:], vn[:], last_bc(mean[:], SGU_W), ALU.subtract))
                    step(v.tensor_tensor(sq[:], vn[:], vn[:], ALU.mult))
                    step(v.tensor_reduce(var[:], sq[:], AXX, ALU.add), var_ready)
                    e.wait_ge(root.sem, root.at(1))
                    step(v.reciprocal(var[:], rt[:]))
                    step(v.tensor_tensor(vn[:], vn[:], last_bc(var[:], SGU_W), ALU.mult))
                    e.wait_ge(params_loaded.sem, params_loaded.at(48))
                    step(v.tensor_tensor(vn[:], vn[:], row_bc(sgu_ln_g[:], [HALVES]), ALU.mult))
                    step(v.tensor_tensor(vn[:], vn[:], row_bc(sgu_ln_b[:], [HALVES]), ALU.add))
            mixed, dve = S("tokens_mixed"), S("dve_chain")
            with stage() as block:
                sync_stage(block)

                @block.tensor
                def _(e):
                    for h in range(HALVES):
                        for g in range(SGU_G):
                            last = pe.matmul(bank(h)[:, g * P:(g + 1) * P], w_sT[:, g, :], vn[:, h, g * P:(g + 1) * P],
                                             start=True, stop=True)
                        mixed.inc(last)

                @block.vector
                def _(e):
                    for h in range(HALVES):
                        e.wait_ge(mixed.sem, mixed.at(h + 1))
                        for g in range(SGU_G):
                            uu = u[:, h, g * P:(g + 1) * P]
                            last = v.scalar_tensor_tensor(out=uu, in0=bank(h)[:, g * P:(g + 1) * P], scalar=b_s[:, g:g + 1],
                                                          in1=uu, op0=ALU.add, op1=ALU.mult)
                        dve.inc(last)
            uT = tmp_split(st, "uT", [P, 4, SEQ])
            transposes([u[:, h, k * P:(k + 1) * P] for k in range(4) for h in range(HALVES)], P,
                       flat(uT))
            product(uT, 4, D, copy_to=y_sgu)

        gates, dve = S("gates_ready"), S("dve_chain")
        with stage() as block:
            sync_stage(block)

            @block.scalar
            def _(e):
                for n in ("ga", "gb"):
                    gates.inc(sc.activation(zc(n), zc(n), ACT.Sigmoid))

            @block.vector
            def _(e):
                step = make_step(e)
                e.wait_ge(gates.sem, gates.at(1))
                step(v.tensor_tensor(y_att[:], y_att[:], zc("ga"), ALU.mult))
                e.wait_ge(gates.sem, gates.at(2))
                step(v.tensor_tensor(y_sgu[:], y_sgu[:], zc("gb"), ALU.mult))
                step(v.tensor_tensor(y_att[:], y_att[:], y_sgu[:], ALU.add))
        transposes([y_att[:, h, k * P:(k + 1) * P] for k in range(KT) for h in range(HALVES)], P,
                   flat(xT))
        product(xT, KT, D, add_to=x)

    with ExitStack() as st:
        mem = tmp(st, "mem", [P, HALVES, D])
        memT = tmp_split(st, "memT", [P, KT, SEQ])
        with stage() as block:
            @block.sync
            def _(sp):
                params_loaded.inc(sp.dma_start(mem[:], A["mem"][0].rearrange("(h p) d -> p h d", p=P)), 16)
                issue_loads(sp)
                sp.wait_ge(params_loaded.sem, params_loaded.total)
        normed_T(mem, g_mem, memT)
        normed_T(x, g_cross, xT)
        cqT, ckT = tmp(st, "cqT", [P, X_HEADS, SEQ]), tmp(st, "ckT", [P, X_HEADS, SEQ])
        cv = tmp(st, "cv", [P, HALVES, X_HEADS * X_HD])
        product_T(xT, cqT)
        product_T(memT, ckT)
        product(memT, KT, X_HEADS * X_HD, copy_to=cv)
        catt = tmp(st, "catt", [P, HALVES, X_HEADS, X_HD])
        for h in range(HALVES):
            attend([(cqT[:, n, h * P:(h + 1) * P], ckT[:, n, :],
                     [cv[:, k, n * X_HD:(n + 1) * X_HD] for k in range(HALVES)]) for n in range(X_HEADS)],
                   SEQ, X_HD, X_HD ** -0.5, None, catt[:, h, :, :])
        cT = tmp_split(st, "cT", [P, 4, SEQ])
        transposes([catt[:, h, k, :] for k in range(4) for h in range(HALVES)], P, flat(cT))
        product(cT, 4, D, add_to=x)

    moe_x = ExitStack()
    xn = tmp(moe_x, "xn_moe", [P, HALVES, D])
    clear_routing()
    normed_T(x, g_moe, xT, xn)
    with ExitStack() as st:
        gl, goh = tmp(st, "gl", [P, HALVES, N_GROUPS]), tmp(st, "goh", [P, HALVES, N_GROUPS])
        ge = tmp(st, "ge", [P, HALVES, N_GROUPS])
        el = tmp(st, "el", [P, HALVES, N_EXP1])
        sel, c4, m4 = (tmp(st, n, [P, HALVES, PER_GROUP]) for n in ("sel", "c4", "m4"))
        gbest, gsum = tmp(st, "gbest", [P, HALVES]), tmp(st, "gsum", [P, HALVES])
        t = [tmp(st, n, [P, HALVES]) for n in ("best1", "best2", "idx")] + \
            [tmp(st, n, [P, HALVES, PER_GROUP]) for n in ("cand", "one1", "one2", "left")]
        t = [a[:] for a in t]

        def finish(block, done):
            gshift, gexp = S("group_logits_shifted"), S("group_exp_ready")
            diff_ready, diff_exp = S("top_two_difference"), S("top_two_exp")

            @block.vector
            def _(e):
                step = make_step(e)
                e.wait_ge(done.sem, done.at(1))
                step(v.tensor_tensor(gl[:], logits_psum[:, :, 0:N_GROUPS], row_bc(b_rg[:], [HALVES]), ALU.add))
                step(v.tensor_tensor(el[:], logits_psum[:, :, 16:16 + N_EXP1], row_bc(b_re[:], [HALVES]), ALU.add))
                pick(step, gl[:], N_GROUPS, gbest[:], t[3], t[2], goh[:])
                step(v.tensor_tensor(ge[:], gl[:], last_bc(gbest[:], N_GROUPS), ALU.subtract), gshift)
                for h in range(HALVES):
                    for g in range(N_GROUPS):
                        src = el[:, h, g * PER_GROUP:(g + 1) * PER_GROUP]
                        if g == 0:
                            step(v.tensor_scalar(sel[:, h, :], src, goh[:, h, g:g + 1], None, ALU.mult))
                        else:
                            step(v.scalar_tensor_tensor(out=sel[:, h, :], in0=src, scalar=goh[:, h, g:g + 1],
                                                        in1=sel[:, h, :], op0=ALU.mult, op1=ALU.add))
                e.wait_ge(gexp.sem, gexp.at(1))
                step(v.tensor_reduce(gsum[:], ge[:], AXX, ALU.add))
                step(v.reciprocal(gsum[:], gsum[:]))
                top_two_weights(e, step, sel[:], PER_GROUP, c4[:], m4[:], t, other=gsum[:])
                for h in range(HALVES):
                    for g in range(N_GROUPS):
                        for out_, in_ in ((comb, c4), (chosen, m4)):
                            step(v.tensor_scalar(out_[:, h, 1 + g * PER_GROUP:1 + (g + 1) * PER_GROUP], in_[:, h, :],
                                                 goh[:, h, g:g + 1], None, ALU.mult))

            @block.scalar
            def _(e):
                e.wait_ge(gshift.sem, gshift.at(1))
                gexp.inc(sc.activation(ge[:], ge[:], ACT.Exp))
                e.wait_ge(diff_ready.sem, diff_ready.at(1))
                diff_exp.inc(sc.activation(t[1], t[1], ACT.Exp))

        route([(w_rg, 0, N_GROUPS), (w_re, 16, N_EXP1)], finish)
    routed_experts(xn, g_moe)
    moe_x.close()

    with ExitStack() as st:
        g_final = tmp(st, "g_final", [P, D])
        junk = tmp(st, "junk", [P, HALVES, D])
        ss, rms, rinv = (tmp(st, n, [P, HALVES]) for n in ("ss", "rms", "rinv"))
        with stage() as block:
            @block.sync
            def _(sp):
                params_loaded.inc(sp.dma_start(g_final[:], A["g_final"].partition_broadcast(P)), 16)
                issue_loads(sp)
            row_rms(block, x, rinv, junk, ss[:], rms[:])
            rms_done = S("rms_done")

            @block.vector
            def _(e):
                step = make_step(e)
                e.wait_ge(rms_done.sem, rms_done.at(1))
                step(v.reciprocal(rinv[:], rms[:]))
                e.wait_ge(params_loaded.sem, params_loaded.at(16))
                for h in range(HALVES):
                    step(v.scalar_tensor_tensor(out=x[:, h, :], in0=x[:, h, :], scalar=rinv[:, h:h + 1],
                                                in1=g_final[:], op0=ALU.mult, op1=ALU.mult))

    for layer in range(LAYERS):
        with ExitStack() as L2:
            hybrid_mixers(layer, L2)

        moe_x = ExitStack()
        xn = tmp(moe_x, "xn_moe", [P, HALVES, D])
        if layer % 2:
            clear_routing()
        normed_T(x, g_ffn2[layer], xT, xn)
        if layer % 2 == 0:
            all_tokens_experts(lambda h, ex: const("all_ones")[:, 0:1])
        else:
            with ExitStack() as st:
                lg = tmp(st, "lg", [P, HALVES, N_EXP2])
                t = [tmp(st, n, [P, HALVES]) for n in ("best1", "best2", "idx")] + \
                    [tmp(st, n, [P, HALVES, N_EXP2]) for n in ("cand", "one1", "one2", "left")]
                t = [a[:] for a in t]

                def finish(block, done):
                    diff_ready, diff_exp = S("top_two_difference"), S("top_two_exp")

                    @block.vector
                    def _(e):
                        step = make_step(e)
                        e.wait_ge(done.sem, done.at(1))
                        step(v.tensor_copy(lg[:], logits_psum[:, :, 0:N_EXP2]))
                        top_two_weights(e, step, lg[:], N_EXP2, comb[:, :, 1:1 + N_EXP2], chosen[:, :, 1:1 + N_EXP2], t)

                    @block.scalar
                    def _(e):
                        e.wait_ge(diff_ready.sem, diff_ready.at(1))
                        diff_exp.inc(sc.activation(t[1], t[1], ACT.Exp))

                route([(router2, 0, N_EXP2)], finish)
            routed_experts(xn, g_ffn2[layer])
        moe_x.close()

        with ExitStack() as st:
            pr = tmp(st, "pr", [P, HALVES, PLE])
            with stage() as block:
                @block.sync
                def _(sp):
                    params_loaded.inc(sp.dma_start(pr[:], A["p_2"][layer, 0].rearrange("(h p) d -> p h d", p=P)), 16)
                    issue_loads(sp)
                    sp.wait_ge(params_loaded.sem, params_loaded.total)
            pT = tmp_split(st, "pT", [P, PLE // P, SEQ])
            transposes([pr[:, h, k * P:(k + 1) * P] for k in range(PLE // P) for h in range(HALVES)], P,
                       flat(pT))
            proj, gate = tmp(st, "proj", [P, HALVES, D]), tmp(st, "gate", [P, HALVES, D])
            product(pT, PLE // P, D, copy_to=proj)
            normed_T(x, g_ple2[layer], xT)
            product(xT, KT, D, copy_to=gate)
            gates = S("gates_ready")
            with stage() as block:
                sync_stage(block)

                @block.scalar
                def _(e):
                    gates.inc(sc.activation(gate[:], gate[:], ACT.Sigmoid))

                @block.vector
                def _(e):
                    step = make_step(e)
                    e.wait_ge(gates.sem, gates.at(1))
                    step(v.tensor_tensor(gate[:], gate[:], proj[:], ALU.mult))
                    step(v.tensor_tensor(x[:], x[:], gate[:], ALU.add))

    stored = S("output_stored")
    with stage() as block:
        @block.sync
        def _(sp):
            stored.inc(sp.dma_start(out[0].rearrange("(h p) d -> p h d", p=P), x[:]), 16)
            sp.wait_ge(stored.sem, stored.total)


_INS = ["x", "mem", "g_mix", "w_in", "g_q", "g_k", "w_att_out", "sgu_ln_g", "sgu_ln_b", "w_s", "b_s",
        "w_sgu_out", "w_out", "g_cross", "g_mem", "w_cq", "w_ckv", "w_co", "g_moe", "w_rg", "b_rg", "w_re",
        "b_re", "w_gate", "w_up", "w_down", "g_final", "p_2", "norm_attn_2", "w_in_2", "w_out_2",
        "nsa_cmp_pos_2", "nsa_cmp_w1_2", "nsa_cmp_w2_2", "nsa_qk_gain_2", "diff_qk_gain_2", "diff_lambda_2",
        "diff_norm_2", "gla_w_gate2_2", "gla_b_gate_2", "gla_norm_2", "hgrn_lb_logits_2", "hgrn_norm_2",
        "norm_ffn_2", "ffn_w_gate_2", "ffn_w_up_2", "ffn_w_down_2", "moe_router_2", "moe_w_gate_2",
        "moe_w_up_2", "moe_w_down_2", "ple_norm_2", "ple_w_gate_2", "ple_w_proj_2"]

_TILED_GAINS = ("g_mix", "g_cross", "g_mem", "g_moe", "norm_attn_2", "norm_ffn_2", "ple_norm_2")
_LAST_TWO_SWAPPED = ("b_s", "nsa_cmp_pos_2", "w_s")


def kernel(**inputs):
    import numpy as _np
    import concourse.bacc as _bacc
    from concourse import mybir as _mybir
    from concourse.bass_utils import run_bass_kernel_spmd as _run

    nc = _bacc.Bacc("TRN2", target_bir_lowering=False, num_devices=1)
    arrays, aps = {}, {}
    for name in _INS:
        a = _np.asarray(inputs[name])
        if name in _TILED_GAINS:
            a = a.reshape(a.shape[0], KT, P).transpose(0, 2, 1)
        elif name == "nsa_cmp_w1_2":
            a = a.reshape(LAYERS, 2, CMP_LEN, HD, CMP_HID).transpose(0, 1, 3, 2, 4) \
                .reshape(LAYERS, P, CMP_LEN, CMP_HID)
        elif name in _LAST_TWO_SWAPPED:
            a = a.swapaxes(-1, -2)
        a = _np.ascontiguousarray(a)
        arrays[f"in_{name}_dram"] = a
        aps[name] = nc.dram_tensor(f"in_{name}_dram", a.shape, _mybir.dt.from_np(a.dtype), kind="ExternalInput").ap()
    cols, values = shape_constants()
    arrays["shape_constants"] = values
    consts = nc.dram_tensor("shape_constants", values.shape, _mybir.dt.float32, kind="ExternalInput").ap()
    out = nc.dram_tensor("out_dram", (1, SEQ, D), _mybir.dt.float32, kind="ExternalOutput").ap()
    fused_layers(nc, aps, consts, cols, out)
    r = _run(nc, [arrays], core_ids=[0])
    return r.results[0]["out_dram"]
```

```python
from contextlib import ExitStack, contextmanager
import math

import numpy as np

import concourse.bass as bass
from concourse import mybir

F32 = mybir.dt.float32
F32R = mybir.dt.float32r
ALU = mybir.AluOpType
ACT = mybir.ActivationFunctionType
AXX = mybir.AxisListType.X

P = 128
SEQ = 256
HALVES = SEQ // P
D = 1024
KT = D // P
EPS = 1e-6
BANK = 512
GRID_W = 64
ATT_HEADS, ATT_KV, HD = 8, 2, 64
SGU_W, SGU_G = 512, 4
X_HEADS, X_HD = 4, 128
N_GROUPS, PER_GROUP = 4, 4
N_EXP1, N_EXP2 = 16, 8
D_FF = 3584
FF = 512
FF_STEPS = D_FF // FF
LAYERS = 2
MH = 4
DIFF_QK = 32
GLA_DK = 32
GLA_RANK = 16
GLA_TAU = 16.0
PLE = 256
CMP_LEN, CMP_STRIDE = 32, 16
N_CMP = (SEQ - CMP_LEN) // CMP_STRIDE + 1
CMP_HID = 4 * HD
NEG = -1e30
LEVELS = [64, 32, 16, 8, 4, 2, 1]
N_LEVELS = len(LEVELS)

IN1 = dict(q=(0, 512), k=(512, 128), v=(640, 128), su=(768, 512), sv=(1280, 512),
           ga=(1792, 1024), gb=(2816, 1024))
IN1_COLS = 3840
IN2_SIZES = dict(nq=256, kc=64, vc=64, ks=64, vs=64, kw=64, vw=64, ng=12, dq=256, dk=256, dv=256,
                 gq=128, gk=128, gv=256, glr=16, gog=256, rq=256, rf=256, ri=256, rog=256)
IN2, _at = {}, 0
for _n, _w in IN2_SIZES.items():
    IN2[_n] = (_at, _w)
    _at += _w
IN2_COLS = _at


def shape_constants():
    cols, parts = {}, []

    def put(name, a):
        a = np.asarray(a, np.float32).reshape(P, -1)
        cols[name] = (sum(x.shape[1] for x in parts), a.shape[1])
        parts.append(a)

    tok = np.arange(SEQ)
    halves = lambda a: np.ascontiguousarray(a.reshape(HALVES, P, -1).transpose(1, 0, 2))
    put("ident", np.eye(P))
    pairs = HD // 4
    inv = (np.float32(10000.0) ** (-np.arange(pairs, dtype=np.float32) / np.float32(pairs))).astype(np.float32)
    ang = np.concatenate([(tok // GRID_W).astype(np.float32)[:, None] * inv,
                          (tok % GRID_W).astype(np.float32)[:, None] * inv], axis=1)
    put("cos", halves(np.cos(ang)))
    put("sin", halves(np.sin(ang)))
    put("causal", halves(np.where(tok[None, :] <= tok[:, None], 0.0, NEG)))
    ok = (np.arange(N_CMP) * CMP_STRIDE + CMP_LEN - 1)[None, :] <= tok[:, None]
    put("cmp_add", halves(np.where(ok, 0.0, NEG)))
    put("cmp_mul", halves(ok.astype(np.float32)))
    t, i = np.arange(P)[:, None], np.arange(P)[None, :]
    sums = []
    for size in LEVELS:
        b = (i // (2 * size)) * 2 * size + size
        sums.append(np.where(i >= b, (t >= b) & (t <= i), (t > i) & (t < b)))
    put("gate_sums", np.stack(sums, 1))
    put("gate_cross", np.stack([t > i, t <= i], 1))
    j = t
    pairs_of = [((j // (2 * s)) == (i // (2 * s))) & ((j % (2 * s)) < s) & ((i % (2 * s)) >= s) for s in LEVELS]
    put("level_mask", np.stack([*pairs_of, i == j], 1))
    put("iota", np.tile(np.arange(P, dtype=np.float32), (P, 1)))
    put("before", t < i)
    put("all_ones", np.ones((P, P)))
    put("eps", np.full((P, 1), EPS))
    return cols, np.ascontiguousarray(np.concatenate(parts, 1))


class Signal:

    def __init__(self, sem):
        self.sem, self.total, self.base = sem, 0, 0

    def inc(self, ins, by=1):
        ins.then_inc(self.sem, by)
        self.total += by
        return ins

    def at(self, k):
        return self.base + k


class Piece:

    def __init__(self, n, src, a, width):
        self.n, self.src, self.a, self.width = n, src, a, width
        self.early = False


class WeightStream:

    RAW, FINE, AHEAD = 12, 4, 2

    def __init__(self):
        self.items, self.count = [], 0

    def add(self, src, a, width):
        self.items.append(Piece(self.count, src, a, width))
        self.count += 1


def fused_layers(nc, A, consts_dram, const_cols, out):
    ctx = ExitStack()
    with ctx:
        build(nc, ctx, A, consts_dram, const_cols, out)


def build(nc, ctx, A, consts_dram, const_cols, out):
    def sb(name, shape, stack=ctx, dtype=F32):
        return stack.enter_context(nc.sbuf_tensor(name, shape, dtype))

    serial = [0]

    def tmp(stack, name, shape, dtype=F32):
        serial[0] += 1
        return sb(f"{name}_{serial[0]}", shape, stack, dtype)

    def tmp_split(stack, name, shape):
        return tmp(stack, name + "_hi", shape, F32R), tmp(stack, name + "_lo", shape, F32R)

    signals = {}

    def S(name):
        if name not in signals:
            signals[name] = Signal(ctx.enter_context(nc.semaphore(name)))
        return signals[name]

    @contextmanager
    def stage():
        for s in signals.values():
            s.base = s.total
        with nc.Block() as block:
            yield block

    v, sc, pe = nc.vector, nc.scalar, nc.tensor

    ring = sb("ring", [P, WeightStream.RAW, 1024])
    ring_hi = sb("ring_hi", [P, WeightStream.FINE, 1024], dtype=F32R)
    ring_lo = sb("ring_lo", [P, WeightStream.FINE, 1024], dtype=F32R)
    x = sb("x", [P, HALVES, D])
    xT = (sb("xT_hi", [P, KT, SEQ], dtype=F32R),
          sb("xT_lo", [P, KT, SEQ], dtype=F32R))
    consts = sb("consts", [P, consts_dram.shape[1]])

    def const(name):
        a, w = const_cols[name]
        return consts[:, a:a + w]

    ident = const("ident")
    eps = const("eps")
    psum = ctx.enter_context(nc.psum_tensor("psum", [P, 8 * BANK], F32))

    def bank(b, n=1):
        return psum[:, b * BANK:(b + n) * BANK]

    small = []

    def row_param(name, ap):
        t = sb(name, [P, ap.shape[-1]])
        small.append((t[:], ap.partition_broadcast(P)))
        return t

    def col_param(name, ap):
        t = sb(name, [P, KT])
        small.append((t[:], ap))
        return t

    def tile_param(name, shape, ap):
        t = sb(name, shape)
        small.append((t[:], ap))
        return t

    small.append((consts[:], consts_dram))
    small.append((x[:], A["x"][0].rearrange("(h p) d -> p h d", p=P)))
    g_mix, g_cross, g_mem, g_moe = (col_param("c_" + n, A[n][0]) for n in ("g_mix", "g_cross", "g_mem", "g_moe"))
    g_attn2 = [col_param(f"g_attn2_{i}", A["norm_attn_2"][i]) for i in range(LAYERS)]
    g_ffn2 = [col_param(f"g_ffn2_{i}", A["norm_ffn_2"][i]) for i in range(LAYERS)]
    g_ple2 = [col_param(f"g_ple2_{i}", A["ple_norm_2"][i]) for i in range(LAYERS)]
    g_q, g_k = row_param("r_g_q", A["g_q"][0]), row_param("r_g_k", A["g_k"][0])
    b_s = tile_param("b_s", [P, SGU_G], A["b_s"][0])
    w_rg = tile_param("w_rg", [P, KT, N_GROUPS], A["w_rg"][0].rearrange("(k p) n -> p k n", p=P))
    w_re = tile_param("w_re", [P, KT, N_EXP1], A["w_re"][0].rearrange("(k p) n -> p k n", p=P))
    b_rg, b_re = row_param("r_b_rg", A["b_rg"][0]), row_param("r_b_re", A["b_re"][0])
    router2 = tile_param("router2", [P, KT, N_EXP2], A["moe_router_2"][0].rearrange("(k p) n -> p k n", p=P))
    hg_logits = tile_param("hg_logits", [P, LAYERS, 256],
                           A["hgrn_lb_logits_2"].rearrange("l c -> (l c)").partition_broadcast(P)
                           .rearrange("p (l c) -> p l c", l=LAYERS))

    ws = WeightStream()

    def stream_matrix(w):
        k, n = w.shape
        for c in range(0, n, FF):
            width = min(FF, n - c)
            for q in range(k // (2 * P)):
                ws.add(w[q * 2 * P:(q + 1) * 2 * P, c:c + width].rearrange("(a p) n -> p a n", p=P), 2, width)

    CMP_PIECES = CMP_LEN // 4

    def stream_cmp(w1):
        for q in range(CMP_PIECES):
            j, r = q // (CMP_PIECES // 2), q % (CMP_PIECES // 2)
            ws.add(w1[j, r * 4 * P:(r + 1) * 4 * P, :].rearrange("(a p) f -> p a f", p=P), 4, CMP_HID)

    class Experts:

        def __init__(self, gate, up, down, n_experts, n_chunks):
            self.gate, self.up, self.down, self.E, self.C = gate, up, down, n_experts, n_chunks
            self.steps = n_experts * n_chunks
            self.n0 = ws.count
            for k in range(8):
                ws.add(self.src(k, (0, 0), None), 2, FF)
            ws.items.append(self)
            ws.count = self.n0 - 4 + 12 * self.steps
            for k in range(8, 12):
                ws.add(self.src(k, None, (n_experts - 1, n_chunks - 1)), 1, 1024)

        def src(self, k, cur, prev):
            if k < 8:
                w = (self.gate if k < 4 else self.up)(*cur)
                return w.rearrange("(q a p) f -> q p a f", p=P, a=2)[k % 4]
            return self.down(*prev).rearrange("(q a p) d -> q p a d", p=P, a=1)[k - 8]

        def number(self, k, i, cur=True):
            if not cur:
                k -= 8
            return (self.n0 + k, 0) if isinstance(i, int) and i == 0 else (self.n0 - 4 + k, i)

        def firsts(self, i):
            return range(self.early if isinstance(i, int) and i == 0 else 0, 4)

        def iterations(self, e, body):
            E, C = self.E, self.C

            def step(ex, c, last=False):
                return (ex, c, isinstance(c, int) and c == 0, last or (isinstance(c, int) and c == C - 1))

            def expert(ex, final):
                if C == 1:
                    body(ex + 1, None if final else step(ex + 1, 0), step(ex, 0), ex - 1)
                    return
                body(ex * C + 1, step(ex, 1), step(ex, 0), ex - 1)
                if C > 3:
                    with e.Fori(2, C - 1) as c:
                        body(ex * C + c, step(ex, c), step(ex, c - 1), None)
                body(ex * C + C - 1, step(ex, C - 1), step(ex, C - 2), None)
                body(ex * C + C, None if final else step(ex + 1, 0), step(ex, C - 1), None)

            body(0, step(0, 0), None, None)
            if E > 1:
                with e.Fori(0, E - 1) as ex:
                    expert(ex, False)
            expert(E - 1, True)
            body(None, None, None, E - 1)

    stream_matrix(A["w_in"][0])
    stream_matrix(A["w_att_out"][0])
    stream_matrix(A["w_sgu_out"][0])
    stream_matrix(A["w_out"][0])
    stream_matrix(A["w_cq"][0])
    stream_matrix(A["w_ckv"][0])
    stream_matrix(A["w_co"][0])
    Experts(lambda e, c: A["w_gate"][0, e], lambda e, c: A["w_up"][0, e], lambda e, c: A["w_down"][0, e], N_EXP1, 1)
    for i in range(LAYERS):
        stream_matrix(A["w_in_2"][i])
        stream_cmp(A["nsa_cmp_w1_2"][i])
        stream_matrix(A["w_out_2"][i])
        if i % 2 == 0:
            wg = A["ffn_w_gate_2"][0].rearrange("k (c f) -> c k f", f=FF)
            wu = A["ffn_w_up_2"][0].rearrange("k (c f) -> c k f", f=FF)
            wd = A["ffn_w_down_2"][0].rearrange("(c f) d -> c f d", f=FF)
            Experts(lambda e, c, w=wg: w[c], lambda e, c, w=wu: w[c], lambda e, c, w=wd: w[c], 1, FF_STEPS)
        else:
            wg = A["moe_w_gate_2"][0].rearrange("e k (c f) -> e c k f", f=FF)
            wu = A["moe_w_up_2"][0].rearrange("e k (c f) -> e c k f", f=FF)
            wd = A["moe_w_down_2"][0].rearrange("e (c f) d -> e c f d", f=FF)
            Experts(lambda e, c, w=wg: w[e, c], lambda e, c, w=wu: w[e, c], lambda e, c, w=wd: w[e, c],
                    N_EXP2, FF_STEPS)
        stream_matrix(A["ple_w_gate_2"][i])
        stream_matrix(A["ple_w_proj_2"][i])

    RAW, FINE = ws.RAW, ws.FINE
    params_loaded = S("params_loaded")
    arrived = [ctx.enter_context(nc.semaphore(f"piece_in_raw_slot{s}")) for s in range(RAW)]
    hi_ready, lo_ready, used = (ctx.enter_context(nc.semaphore(n)) for n in
                                ("piece_hi_ready", "piece_lo_ready", "pieces_used"))

    def count_after(num, off=1):
        return num[1] * 12 + (num[0] + off)

    def raw_view(buf, slots, num, a, width):
        w = buf[:, num[0] % slots, :].rearrange("p (a n) -> p a n", a=a)
        return w if width * a == 1024 else w[:, :, 0:width]

    def then_registers(e):
        e.sem_inc(passed_waits, 1)

    def load_piece(sp, num, src, a, width):
        if not (isinstance(num[1], int) and num[0] + 12 * num[1] < RAW):
            sp.wait_ge(lo_ready, count_after(num, 1 - RAW))
            if not isinstance(num[1], int):
                then_registers(sp)
        sp.dma_start(raw_view(ring, RAW, num, a, width), src).then_inc(arrived[num[0] % RAW], 16)

    def make_hi(e, num, a=2, width=FF):
        e.wait_ge(arrived[num[0] % RAW], num[1] * 16 + 16 * (num[0] // RAW + 1))
        if not (isinstance(num[1], int) and num[0] + 12 * num[1] < FINE):
            e.wait_ge(used, count_after(num, 1 - FINE))
        sc.activation(raw_view(ring_hi, FINE, num, a, width), raw_view(ring, RAW, num, a, width), ACT.Copy) \
            .then_inc(hi_ready, 1)

    def make_lo(e, num, a=2, width=FF):
        e.wait_ge(hi_ready, count_after(num))
        v.tensor_tensor(raw_view(ring_lo, FINE, num, a, width), raw_view(ring, RAW, num, a, width),
                        raw_view(ring_hi, FINE, num, a, width).bitcast(F32), ALU.subtract).then_inc(lo_ready, 1)

    def make_his(e, pcs):
        for p in pcs:
            make_hi(e, (p.n, 0), p.a, p.width)

    def make_los(e, pcs):
        for p in pcs:
            make_lo(e, (p.n, 0), p.a, p.width)

    def not_early(pcs):
        return [p for p in pcs if not p.early]

    def three_passes(out_, lhsT, rhs, start, stop):
        pe.matmul(out_, lhsT[0], rhs[0], start=start, stop=False)
        pe.matmul(out_, lhsT[0], rhs[1], start=False, stop=False)
        return pe.matmul(out_, lhsT[1], rhs[0], start=False, stop=stop)

    passed_waits = ctx.enter_context(nc.semaphore("passed_waits"))
    to_load, to_take = list(ws.items), list(ws.items)
    taken = [0]

    def take(n):
        got = [to_take.pop(0) for _ in range(n)]
        taken[0] = got[-1].n + 1
        return got

    def take_early():
        got = [p for p in to_take[:ws.AHEAD] if isinstance(p, Piece)]
        for p in got:
            p.early = True
            taken[0] = p.n + 1
        return got

    def issue_loads(sp):
        while to_load and isinstance(to_load[0], Piece) and to_load[0].n + 1 - RAW <= taken[0]:
            p = to_load.pop(0)
            load_piece(sp, (p.n, 0), p.src, p.a, p.width)

    def sync_stage(block, loads=()):
        @block.sync
        def _(sp):
            for dst, src in loads:
                params_loaded.inc(sp.dma_start(dst, src), 16)
            issue_loads(sp)
            if loads:
                sp.wait_ge(params_loaded.sem, params_loaded.total)

    def transposes(jobs, width, dst, scale=None):
        done, free_v, free_s = S("transposed"), S("bank_copied_dve"), S("bank_copied_act")
        split = isinstance(dst, tuple)
        groups = [list(range(i, min(i + 4, len(jobs)))) for i in range(0, len(jobs), 4)]
        assert len(groups) <= 8
        with stage() as block:
            sync_stage(block)

            @block.tensor
            def _(e):
                for g, group in enumerate(groups):
                    for m, n in enumerate(group):
                        last = pe.transpose(psum[0:width, g * BANK + m * P:g * BANK + (m + 1) * P], jobs[n], ident)
                    done.inc(last)

            def source(g, n0, a, b):
                return psum[0:width, g * BANK + a - n0:g * BANK + b - n0]

            def parts(group):
                n0, n1 = group[0] * P, (group[-1] + 1) * P
                return n0, [(n0, n1, None)] if scale is None else \
                    [(a, a + 2 * P, scale[:, a // (2 * P):a // (2 * P) + 1]) for a in range(n0, n1, 2 * P)]

            @block.vector
            def _(e):
                for g, group in enumerate(groups):
                    n0, todo = parts(group)
                    if split:
                        e.wait_ge(free_s.sem, free_s.at(g + 1))
                        for a, b, k in todo:
                            hi = dst[0][:, a:b].bitcast(F32)
                            if k is None:
                                last = v.tensor_tensor(dst[1][:, a:b], source(g, n0, a, b), hi, ALU.subtract)
                            else:
                                last = v.scalar_tensor_tensor(out=dst[1][:, a:b], in0=source(g, n0, a, b), scalar=k,
                                                              in1=hi, op0=ALU.mult, op1=ALU.subtract)
                        free_v.inc(last)
                    elif g % 2 == 0:
                        e.wait_ge(done.sem, done.at(g + 1))
                        free_v.inc(v.tensor_copy(dst[:, n0:todo[-1][1]], source(g, n0, n0, todo[-1][1])))

            @block.scalar
            def _(e):
                for g, group in enumerate(groups):
                    if not split and g % 2 == 0:
                        continue
                    n0, todo = parts(group)
                    e.wait_ge(done.sem, done.at(g + 1))
                    for a, b, k in todo:
                        to = dst[0] if split else dst
                        last = sc.activation(to[:, a:b], source(g, n0, a, b), ACT.Copy, scale=1.0 if k is None else k)
                    free_s.inc(last)

    def row_rms(block, src, rinv, junk, ss, rms):
        sq, rms_done = S("squares_summed"), S("rms_done")

        @block.scalar
        def _(e):
            for h in range(HALVES):
                sq.inc(sc.activation(junk[:, h, :], src[:, h, :], ACT.Square, accum_out=ss[:, h:h + 1]))
            e.wait_ge(sq.sem, sq.at(HALVES))
            rms_done.inc(sc.activation(rms, ss, ACT.Sqrt, scale=1.0 / D, bias=eps))

    def flat(pair):
        return tuple(t[:].rearrange("p k n -> p (k n)") for t in pair)

    def normed_T(src, gain, dst, xn=None):
        with ExitStack() as st:
            if xn is None:
                xn = tmp(st, "xn", [P, HALVES, D])
            ss, rms, rinv = (tmp(st, n, [P, HALVES]) for n in ("ss", "rms", "rinv"))
            dve = S("dve_chain")
            with stage() as block:
                sync_stage(block)
                row_rms(block, src, rinv, xn, ss[:], rms[:])
                rms_done = S("rms_done")

                @block.vector
                def _(e):
                    e.wait_ge(rms_done.sem, rms_done.at(1))
                    dve.inc(v.reciprocal(rinv[:], rms[:]))
                    e.wait_ge(dve.sem, dve.total)
                    for h in range(HALVES):
                        dve.inc(v.tensor_scalar(xn[:, h, :], src[:, h, :], rinv[:, h:h + 1], None, ALU.mult))
            transposes([xn[:, h, k * P:(k + 1) * P] for k in range(KT) for h in range(HALVES)], P,
                       flat(dst), scale=gain[:])

    def product(lhsT, kt, cols, copy_to=None, add_to=None, loads=()):
        chunks = [(c, min(FF, cols - c)) for c in range(0, cols, FF)]
        per = kt // 2
        got = take(per * len(chunks))
        of_chunk = [got[n * per:(n + 1) * per] for n in range(len(chunks))]
        to_split = [not_early(c) for c in of_chunk] + [take_early()]
        free_v, free_s = S("bank_copied_dve"), S("bank_copied_act")
        with stage() as block:
            sync_stage(block, loads)

            @block.tensor
            def _(e):
                for n, (c, width) in enumerate(chunks):
                    if n >= 4:
                        e.wait_ge(free_v.sem, free_v.at(n - 3))
                        if add_to is None:
                            e.wait_ge(free_s.sem, free_s.at(n - 3))
                    for q, p in enumerate(of_chunk[n]):
                        e.wait_ge(lo_ready, p.n + 1)
                        w = [raw_view(r, FINE, (p.n, 0), 2, width) for r in (ring_hi, ring_lo)]
                        for a in range(2):
                            k = 2 * q + a
                            for h in range(HALVES):
                                last = three_passes(bank((2 * n + h) % 8)[:, 0:width],
                                                    [x_[:, k, h * P:(h + 1) * P] for x_ in lhsT], [w_[:, a, :] for w_ in w],
                                                    k == 0, k == kt - 1)
                        last.then_inc(used, 1)

            @block.vector
            def _(e):
                make_los(e, to_split[0])
                for n, (c, width) in enumerate(chunks):
                    make_los(e, to_split[n + 1])
                    e.wait_ge(used, of_chunk[n][-1].n + 1)
                    if add_to is None:
                        free_v.inc(v.tensor_copy(copy_to[:, 0, c:c + width], bank(2 * n % 8)[:, 0:width]))
                    else:
                        for h in range(HALVES):
                            to = add_to[:, h, c:c + width]
                            last = v.tensor_tensor(to, to, bank((2 * n + h) % 8)[:, 0:width], ALU.add)
                        free_v.inc(last)

            @block.scalar
            def _(e):
                make_his(e, to_split[0])
                for n, (c, width) in enumerate(chunks):
                    make_his(e, to_split[n + 1])
                    if add_to is None:
                        e.wait_ge(used, of_chunk[n][-1].n + 1)
                        free_s.inc(sc.activation(copy_to[:, 1, c:c + width], bank((2 * n + 1) % 8)[:, 0:width], ACT.Copy))

    def product_T(rhsT, dst, loads=()):
        got = take(KT // 2)
        to_split = not_early(got) + take_early()
        copied = S("bank_copied_dve")
        with stage() as block:
            sync_stage(block, loads)

            @block.tensor
            def _(e):
                for q, p in enumerate(got):
                    e.wait_ge(lo_ready, p.n + 1)
                    w = [raw_view(r, FINE, (p.n, 0), 2, FF) for r in (ring_hi, ring_lo)]
                    for a in range(2):
                        k = 2 * q + a
                        for j in range(4):
                            last = three_passes(bank(j)[:, 0:SEQ], [w_[:, a, j * P:(j + 1) * P] for w_ in w],
                                                [x_[:, k, :] for x_ in rhsT], k == 0, k == KT - 1)
                    last.then_inc(used, 1)

            @block.scalar
            def _(e):
                make_his(e, to_split)

            @block.vector
            def _(e):
                make_los(e, to_split)
                e.wait_ge(used, got[-1].n + 1)
                copied.inc(v.tensor_copy(dst[:], psum[:, 0:4 * BANK].rearrange("p (j n) -> p j n", j=4)[:, :, 0:SEQ]))

    def last_bc(ap, n):
        return ap.unsqueeze(len(ap.shape)).to_broadcast([*ap.shape, n])

    def row_bc(ap, groups):
        for _ in groups:
            ap = ap.unsqueeze(1)
        return ap.to_broadcast([P, *groups, ap.shape[-1]])

    def group_norms(items):
        dve, act, sums, roots = S("dve_chain"), S("act_chain"), S("group_sums"), S("group_roots")
        with ExitStack() as st:
            n = [i[0].shape[2] for i in items]
            sq = [tmp(st, "sq", [P, HALVES, a, i[3]]) for a, i in zip(n, items)]
            ss = [tmp(st, "gss", [P, HALVES, a]) for a in n]
            rt = [tmp(st, "grt", [P, HALVES, a]) for a in n]
            with stage() as block:
                sync_stage(block)

                @block.vector
                def _(e):
                    for (src, _, _, _), q in zip(items, sq):
                        dve.inc(v.tensor_tensor(q[:], src, src, ALU.mult))
                    e.wait_ge(dve.sem, dve.total)
                    for q, s_ in zip(sq, ss):
                        sums.inc(v.tensor_reduce(s_[:], q[:], AXX, ALU.add))
                    for i, (src, dst, gain, d) in enumerate(items):
                        e.wait_ge(roots.sem, roots.at(i + 1))
                        dve.inc(v.reciprocal(ss[i][:], rt[i][:]))
                        e.wait_ge(dve.sem, dve.total)
                        dve.inc(v.tensor_tensor(dst, src, last_bc(ss[i][:], d), ALU.mult))
                        e.wait_ge(dve.sem, dve.total)
                        dve.inc(v.tensor_tensor(dst, dst, row_bc(gain, [HALVES, n[i]]), ALU.mult))

                @block.scalar
                def _(e):
                    for i, (_, _, _, d) in enumerate(items):
                        e.wait_ge(sums.sem, sums.at(i + 1))
                        roots.inc(sc.activation(rt[i][:], ss[i][:], ACT.Sqrt, scale=1.0 / d, bias=eps))

    def attend(jobs, scale):
        scores, max_ready, exped, kept, pT, pT_v, pT_s, o = (S(n) for n in (
            "scores_ready", "maximum_ready", "exp_ready", "exp_kept", "probs_transposed", "probsT_dve", "probsT_act",
            "attended"))
        dve = S("dve_chain")
        n_kept = n_pT = n_pT_s = 0
        for j in jobs:
            j["nh"], j["tiles"], j["rows"] = len(j["heads"]), (j["keys"] + P - 1) // P, min(P, j["keys"])
            total = j["nh"] * j["tiles"]
            j["groups"] = [(a, min(a + 4, total)) for a in range(0, total, 4)]
            n_kept += "keep" in j
            j["kept"], j["pT0"] = n_kept, n_pT
            n_pT += len(j["groups"])
            n_pT_s += len(j["groups"]) == 2
            j["pT_s"] = n_pT_s
        with ExitStack() as st:
            nh = max(j["nh"] for j in jobs)
            tiles = max(j["tiles"] for j in jobs)
            dv = max(j["dv"] for j in jobs)
            E_, PT_, O_ = ([tmp(st, n, shape) for _ in range(2)] for n, shape in (
                ("E", [P, nh * tiles * P]), ("PT", [P, nh * tiles, P]), ("O", [P, nh * dv])))
            small = [[tmp(st, n, [P, nh]) for n in ("mx", "rs", "ri")] for _ in range(2)]

            def views(m):
                j = jobs[m]
                n, k, d = j["nh"], j["keys"], j["dv"]
                E = E_[m % 2][:, 0:n * k].rearrange("p (h k) -> p h k", h=n)
                s_ = psum[:, (m % 2) * 2 * BANK:(m % 2) * 2 * BANK + n * k].rearrange("p (h k) -> p h k", h=n)
                t_ = psum[:, 4 * BANK:4 * BANK + n * j["tiles"] * P].rearrange("p (h k) -> p h k", k=P)
                o_ = bank(6 + m % 2)[:, 0:n * d].rearrange("p (h k) -> p h k", h=n)
                return j, E, s_, PT_[m % 2], t_, o_

            with stage() as block:
                sync_stage(block)

                @block.tensor
                def _(e):
                    def score(m):
                        if m >= len(jobs):
                            return
                        j, E, s_, PT, t_, o_ = views(m)
                        if m >= 2:
                            e.wait_ge(max_ready.sem, max_ready.at(m - 1))
                        for h, (qT, kT, _) in enumerate(j["heads"]):
                            last = pe.matmul(s_[:, h, :], qT, kT, start=True, stop=True)
                        scores.inc(last)

                    score(0)
                    score(1)
                    for m in range(len(jobs)):
                        j, E, s_, PT, t_, o_ = views(m)
                        if "keep" in j:
                            e.wait_ge(kept.sem, kept.at(j["kept"]))
                        else:
                            e.wait_ge(exped.sem, exped.at(m + 1))
                        for a, b in j["groups"]:
                            for n in range(a, b):
                                h, k = divmod(n, j["tiles"])
                                last = pe.transpose(t_[0:j["rows"], n, :], E[:, h, k * P:k * P + j["rows"]], ident)
                            pT.inc(last)
                        score(m + 2)
                        e.wait_ge(pT_v.sem, pT_v.at(m + 1))
                        if len(j["groups"]) == 2:
                            e.wait_ge(pT_s.sem, pT_s.at(j["pT_s"]))
                        for h, (_, _, vals) in enumerate(j["heads"]):
                            for k in range(j["tiles"]):
                                last = pe.matmul(o_[:, h, :], PT[0:j["rows"], h * j["tiles"] + k, :], vals[k],
                                                 start=(k == 0), stop=(k == j["tiles"] - 1))
                        o.inc(last)

                @block.vector
                def _(e):
                    step = make_step(e)

                    def shift(m):
                        if m >= len(jobs):
                            return
                        j, E, s_, PT, t_, o_ = views(m)
                        mx = small[m % 2][0][:, 0:j["nh"]]
                        e.wait_ge(scores.sem, scores.at(m + 1))
                        if "mask" in j:
                            step(v.scalar_tensor_tensor(out=E, in0=s_, scalar=scale, in1=row_bc(j["mask"], [j["nh"]]),
                                                        op0=ALU.mult, op1=ALU.add))
                        else:
                            step(v.tensor_scalar(E, s_, scale, None, ALU.mult))
                        step(v.tensor_reduce(mx, E, AXX, ALU.max))
                        step(v.tensor_scalar(mx, mx, -1.0, None, ALU.mult), max_ready)

                    shift(0)
                    shift(1)
                    for m in range(len(jobs)):
                        j, E, s_, PT, t_, o_ = views(m)
                        rs, ri = (t[:, 0:j["nh"]] for t in small[m % 2][1:])
                        e.wait_ge(exped.sem, exped.at(m + 1))
                        if "keep" in j:
                            step(v.tensor_tensor(E, E, row_bc(j["keep"], [j["nh"]]), ALU.mult), kept)
                        a, b = j["groups"][0]
                        e.wait_ge(pT.sem, pT.at(j["pT0"] + 1))
                        pT_v.inc(v.tensor_copy(PT[0:j["rows"], a:b, :], t_[0:j["rows"], a:b, :]))
                        step(v.reciprocal(ri, rs))
                        if "weight" in j:
                            j["weight"](step, ri)
                        if len(j["groups"]) == 2:
                            e.wait_ge(pT.sem, pT.at(j["pT0"] + 2))
                        shift(m + 2)
                        e.wait_ge(o.sem, o.at(m + 1))
                        if j.get("accumulate"):
                            O = O_[m % 2][:, 0:j["nh"] * j["dv"]].rearrange("p (h k) -> p h k", h=j["nh"])
                            step(v.tensor_tensor(O, o_, last_bc(ri, j["dv"]), ALU.mult))
                            step(v.tensor_tensor(j["dst"], j["dst"], O, ALU.add))
                        else:
                            step(v.tensor_tensor(j["dst"], o_, last_bc(ri, j["dv"]), ALU.mult))

                @block.scalar
                def _(e):
                    def exp(m):
                        if m >= len(jobs):
                            return
                        E = views(m)[1]
                        mx, rs = small[m % 2][0], small[m % 2][1]
                        e.wait_ge(max_ready.sem, max_ready.at(m + 1))
                        for h in range(jobs[m]["nh"]):
                            last = sc.activation(E[:, h, :], E[:, h, :], ACT.Exp, bias=mx[:, h:h + 1],
                                                 accum_out=rs[:, h:h + 1])
                        exped.inc(last)

                    exp(0)
                    exp(1)
                    for m in range(len(jobs)):
                        j, E, s_, PT, t_, o_ = views(m)
                        if len(j["groups"]) == 2:
                            a, b = j["groups"][1]
                            e.wait_ge(pT.sem, pT.at(j["pT0"] + 2))
                            pT_s.inc(sc.activation(PT[0:j["rows"], a:b, :], t_[0:j["rows"], a:b, :], ACT.Copy))
                        exp(m + 2)

    def dense_experts(group, combine, tag):
        one = group.E == 1
        G, U = psum[:, 0:2 * BANK], psum[:, 2 * BANK:4 * BANK]
        silu, hidden, hid_hi, hid, y_out = (S(n + tag) for n in (
            "silu_ready", "hidden_made", "hidden_hi_ready", "hidden_ready", "expert_output_added"))
        counted = (silu, hidden, hid_hi, hid, y_out)

        def programs(st):
            s_g = tmp(st, "silu_gT", [P, 4, SEQ])
            h_hi, h_lo = tmp_split(st, "hiddenT", [P, 4, SEQ])
            flat_g = s_g[:].rearrange("p j n -> p (j n)")

            def tensor(e):
                def body(i, cur, prev, done):
                    if cur:
                        for part, to in enumerate((G, U)):
                            for q in range(4):
                                num = group.number(4 * part + q, i)
                                e.wait_ge(lo_ready, count_after(num))
                                if part == 0 and q == 0 and prev:
                                    e.wait_ge(silu.sem, i + silu.at(0))
                                if part and q == 0 and prev:
                                    e.wait_ge(hidden.sem, i + hidden.at(0))
                                w = [raw_view(r, FINE, num, 2, FF) for r in (ring_hi, ring_lo)]
                                for a in range(2):
                                    k = 2 * q + a
                                    for j in range(4):
                                        last = three_passes(to[:, j * SEQ:(j + 1) * SEQ],
                                                            [w_[:, a, j * P:(j + 1) * P] for w_ in w],
                                                            [x_[:, k, :] for x_ in xT],
                                                            k == 0 and j % 2 == 0, k == KT - 1 and j % 2 == 1)
                                last.then_inc(used, 1)
                    if prev:
                        e.wait_ge(hid.sem, i + hid.at(0))
                        if not (isinstance(i, int) and i == 1):
                            e.wait_ge(y_out.sem, i + y_out.at(-1))
                        for j in range(4):
                            num = group.number(8 + j, i, cur)
                            e.wait_ge(lo_ready, count_after(num))
                            w = [raw_view(r, FINE, num, 1, 1024) for r in (ring_hi, ring_lo)]
                            for h in range(HALVES):
                                for c in range(2):
                                    last = three_passes(bank(4 + 2 * h + c), [t[:, j, h * P:(h + 1) * P] for t in (h_hi, h_lo)],
                                                        [w_[:, 0, c * BANK:(c + 1) * BANK] for w_ in w], j == 0, j == 3)
                            last.then_inc(used, 1)
                group.iterations(e, body)

            def scalar(e):
                def body(i, cur, prev, done):
                    if cur:
                        for k in group.firsts(i):
                            make_hi(e, group.number(k, i))
                    if prev:
                        e.wait_ge(hidden.sem, i + hidden.at(0))
                        sc.activation(h_hi[:], s_g[:], ACT.Copy).then_inc(hid_hi.sem, 1)
                    if cur:
                        for k in range(4, 8):
                            make_hi(e, group.number(k, i))
                        e.wait_ge(used, count_after(group.number(3, i)))
                        if prev:
                            e.wait_ge(hid.sem, i + hid.at(0))
                        sc.activation(flat_g, G, ACT.Silu).then_inc(silu.sem, 1)
                    if prev:
                        for k in range(8, 12):
                            make_hi(e, group.number(k, i, cur), 1, 1024)
                    if i is None:
                        make_his(e, group.next)
                group.iterations(e, body)

            def vector(e):
                def add_outputs(ex):
                    for h in range(HALVES):
                        last = v.scalar_tensor_tensor(
                            out=x[:, h, :], in0=psum[:, (4 + 2 * h) * BANK:(6 + 2 * h) * BANK],
                            scalar=combine(h, ex), in1=x[:, h, :], op0=ALU.mult, op1=ALU.add)
                    last.then_inc(y_out.sem, 1)

                def body(i, cur, prev, done):
                    if cur:
                        for k in group.firsts(i):
                            make_lo(e, group.number(k, i))
                    if prev:
                        e.wait_ge(used, count_after(group.number(0 if cur else 8, i, cur), 0))
                        e.wait_ge(silu.sem, i + silu.at(0))
                        v.tensor_tensor(flat_g, flat_g, U, ALU.mult).then_inc(hidden.sem, 1)
                        e.wait_ge(hid_hi.sem, i + hid_hi.at(0))
                        v.tensor_tensor(h_lo[:], s_g[:], h_hi[:].bitcast(F32), ALU.subtract).then_inc(hid.sem, 1)
                    if one and ((prev and not prev[2]) or done == 0):
                        add_outputs(0)
                        e.wait_ge(y_out.sem, group.steps + y_out.at(0) if i is None else i + y_out.at(-1))
                    if cur:
                        for k in range(4, 8):
                            make_lo(e, group.number(k, i))
                    if prev:
                        for k in range(8, 12):
                            make_lo(e, group.number(k, i, cur), 1, 1024)
                        if not one or not cur:
                            e.wait_ge(used, count_after(group.number(11, i, cur)))
                        if not one:
                            then_registers(e)
                            add_outputs(prev[0])
                            e.wait_ge(y_out.sem, i + y_out.at(0))
                    if i is None:
                        make_los(e, group.next)
                    then_registers(e)
                group.iterations(e, body)
            return tensor, scalar, vector
        return programs, counted

    def experts_sync(block, group):
        @block.sync
        def _(sp):
            issue_loads(sp)
            assert to_load.pop(0) is group

            def body(i, cur, prev, done):
                if prev and cur:
                    for k in range(12):
                        load_piece(sp, group.number(k, i), group.src(k, cur[0:2], prev[0:2]), *((2, FF) if k < 8 else (1, 1024)))
            group.iterations(sp, body)
            issue_loads(sp)

    def take_group():
        first = [to_take.pop(0) for _ in range(8)]
        group = to_take.pop(0)
        group.early = sum(p.early for p in first)
        for _ in range(4):
            last = to_take.pop(0)
        taken[0] = last.n + 1
        group.next = take_early()
        return group

    def gather_rows(xn, dispatch):
        for k in range(KT):
            for h in range(HALVES):
                last = pe.matmul(psum[:, 5 * BANK + k * P:5 * BANK + (k + 1) * P], xn[:, h, k * P:(k + 1) * P],
                                 dispatch[:, h, :], start=(h == 0), stop=(h == HALVES - 1))
        return last

    def make_dispatch(to, ex):
        col = 1 + ex if isinstance(ex, int) else bass.ds(ex + 1, 1)
        col = slice(col, col + 1) if isinstance(ex, int) else col
        for h in range(HALVES):
            last = v.tensor_scalar(to[:, h, :], const("iota"), place[:, h, col], chosen[:, h, col],
                                   ALU.is_equal, ALU.mult)
        return last

    gathered_psum = psum[:, 5 * BANK:7 * BANK].rearrange("p (k s) -> p k s", k=KT)

    def sparse_experts(group, xn, tag):
        names = ("silu_ready", "hidden_rows", "hidden_transposed", "hidden_hi_ready", "hidden_ready",
                 "next_dispatch", "tokens_gathered", "tokens_hi_ready", "tokens_ready",
                 "return_dispatch", "dispatch_transposed", "return_ready", "outputs_hi_ready", "outputs_ready",
                 "outputs_scattered", "outputs_added")
        (silu, rows_done, hT_t, hT_hi, hT_lo, next_p, gathered, xg_hi_ok, xg_ok,
         ret_p, ret_t, ret_ok, y_hi_ok, y_ok, scattered, added) = (
            ctx.enter_context(nc.semaphore(n + tag)) for n in names)
        E, C = group.E, group.C
        end = group.n0 + 12 * group.steps

        def gathers(cur):
            return cur and cur[3] and not (C > 1 and isinstance(cur[0], int) and cur[0] == E - 1)

        def used_before(i):
            return end if i is None else count_after(group.number(0, i), 0)

        def programs(st):
            s_g, rows = tmp(st, "silu_g", [P, FF]), tmp(st, "hidden_rows", [P, FF])
            h_hi, h_lo = tmp_split(st, "hT", [P, 4, P])
            xg_hi, xg_lo = tmp_split(st, "xg", [P, KT, P])
            disp, ret = tmp(st, "dispatch", [P, HALVES, P]), tmp(st, "return_p", [P, HALVES, P])
            retT = tmp(st, "return_pT", [P, HALVES, P], F32R)
            y_hi, y_lo = tmp_split(st, "y", [P, D])
            Y = bank(3, 2)

            def first_gather():
                d, g, h, l = (S(n) for n in ("first_dispatch", "first_gathered", "first_hi", "first_lo"))
                with stage() as block:
                    sync_stage(block)

                    @block.tensor
                    def _(e):
                        e.wait_ge(d.sem, d.at(1))
                        g.inc(gather_rows(xn, disp))

                    @block.vector
                    def _(e):
                        d.inc(make_dispatch(disp, 0))
                        e.wait_ge(h.sem, h.at(1))
                        l.inc(v.tensor_tensor(xg_lo[:], gathered_psum, xg_hi[:].bitcast(F32), ALU.subtract))

                    @block.scalar
                    def _(e):
                        e.wait_ge(g.sem, g.at(1))
                        h.inc(sc.activation(xg_hi[:], gathered_psum, ACT.Copy))

            def tensor(e):
                def gate_or_up(part, qs, i):
                    for q in qs:
                        num = group.number(4 * part + q, i)
                        e.wait_ge(lo_ready, count_after(num))
                        w = [raw_view(r, FINE, num, 2, FF) for r in (ring_hi, ring_lo)]
                        for a in range(2):
                            k = 2 * q + a
                            last = three_passes(bank(part), [t[:, k, :] for t in (xg_hi, xg_lo)],
                                                [w_[:, a, :] for w_ in w], k == 0, k == KT - 1)
                        last.then_inc(used, 1)

                def body(i, cur, prev, done):
                    if cur:
                        if cur[2] and not (isinstance(cur[0], int) and cur[0] == 0):
                            e.wait_ge(xg_ok, cur[0])
                        if prev:
                            e.wait_ge(silu, i)
                        gate_or_up(0, range(4), i)
                    if prev:
                        e.wait_ge(rows_done, i)
                        for j in range(4):
                            last = pe.transpose(bank(2)[:, j * P:(j + 1) * P], rows[:, j * P:(j + 1) * P], ident)
                        last.then_inc(hT_t, 1)
                    if done is not None:
                        e.wait_ge(ret_p, done + 2)
                        for h in range(HALVES):
                            last = pe.transpose(bank(7)[:, h * P:(h + 1) * P], ret[:, h, :], ident)
                        last.then_inc(ret_t, 1)
                    if cur:
                        gate_or_up(1, range(2), i)
                    if done is not None:
                        e.wait_ge(ret_ok, done + 2)
                        e.wait_ge(y_ok, done + 2)
                        for h in range(HALVES):
                            for c in range(2):
                                to = bank((5 if h == 0 else 3) + c)
                                for m, y in enumerate((y_hi, y_lo)):
                                    last = pe.matmul(to, retT[:, h, :], y[:, c * BANK:(c + 1) * BANK],
                                                     start=(m == 0), stop=(m == 1))
                            last.then_inc(scattered, 1)
                    if cur:
                        gate_or_up(1, range(2, 4), i)
                        if gathers(cur):
                            e.wait_ge(next_p, cur[0] + 1)
                            if C > 1:
                                e.wait_ge(added, cur[0] * 2 + 2)
                            elif done is not None:
                                e.wait_ge(added, done * 2 + 3)
                            gather_rows(xn, disp).then_inc(gathered, 1)
                    if prev:
                        e.wait_ge(hT_lo, i)
                        if done is not None:
                            e.wait_ge(added, done * 2 + 4)
                        for j in range(4):
                            num = group.number(8 + j, i, cur)
                            e.wait_ge(lo_ready, count_after(num))
                            w = [raw_view(r, FINE, num, 1, 1024) for r in (ring_hi, ring_lo)]
                            for c in range(2):
                                last = three_passes(bank(3 + c), [t[:, j, :] for t in (h_hi, h_lo)],
                                                    [w_[:, 0, c * BANK:(c + 1) * BANK] for w_ in w],
                                                    prev[2] and j == 0, prev[3] and j == 3)
                            last.then_inc(used, 1)
                group.iterations(e, body)

            def scalar(e):
                def body(i, cur, prev, done):
                    if cur:
                        for k in group.firsts(i):
                            make_hi(e, group.number(k, i))
                    if done is not None:
                        e.wait_ge(used, used_before(i))
                        sc.activation(y_hi[:], Y, ACT.Copy).then_inc(y_hi_ok, 1)
                    if cur:
                        for k in range(4, 8):
                            make_hi(e, group.number(k, i))
                        e.wait_ge(used, count_after(group.number(3, i)))
                        if prev:
                            e.wait_ge(rows_done, i)
                        sc.activation(s_g[:], bank(0), ACT.Silu).then_inc(silu, 1)
                    if prev:
                        e.wait_ge(hT_t, i)
                        sc.activation(h_hi[:].rearrange("p j s -> p (j s)"), bank(2), ACT.Copy).then_inc(hT_hi, 1)
                    if done is not None:
                        e.wait_ge(ret_t, done + 2)
                        sc.activation(retT[:].rearrange("p h t -> p (h t)"), bank(7)[:, 0:SEQ], ACT.Copy).then_inc(ret_ok, 1)
                    if prev:
                        for k in range(8, 12):
                            make_hi(e, group.number(k, i, cur), 1, 1024)
                    if gathers(cur):
                        e.wait_ge(used, count_after(group.number(7, i)))
                        e.wait_ge(gathered, cur[0] + 1)
                        sc.activation(xg_hi[:], gathered_psum, ACT.Copy).then_inc(xg_hi_ok, 1)
                    if i is None:
                        make_his(e, group.next)
                group.iterations(e, body)

            def vector(e):
                def body(i, cur, prev, done):
                    if done is not None:
                        make_dispatch(ret, done).then_inc(ret_p, 1)
                    if cur:
                        for k in group.firsts(i):
                            make_lo(e, group.number(k, i))
                    if done is not None:
                        e.wait_ge(y_hi_ok, done + 2)
                        v.tensor_tensor(y_lo[:], Y, y_hi[:].bitcast(F32), ALU.subtract).then_inc(y_ok, 1)
                    if cur:
                        for k in range(4, 8):
                            make_lo(e, group.number(k, i))
                    if gathers(cur):
                        then_registers(e)
                        make_dispatch(disp, cur[0] + 1).then_inc(next_p, 1)
                    if prev:
                        e.wait_ge(hT_hi, i)
                        v.tensor_tensor(h_lo[:].rearrange("p j s -> p (j s)"), bank(2),
                                        h_hi[:].rearrange("p j s -> p (j s)").bitcast(F32), ALU.subtract).then_inc(hT_lo, 1)
                        for k in (8, 9):
                            make_lo(e, group.number(k, i, cur), 1, 1024)
                    if done is not None:
                        col = slice(done + 1, done + 2) if isinstance(done, int) else bass.ds(done + 1, 1)
                        for h in range(HALVES):
                            e.wait_ge(scattered, done * 2 + 3 + h)
                            then_registers(e)
                            b = 5 if h == 0 else 3
                            v.scalar_tensor_tensor(out=x[:, h, :], in0=bank(b, 2), scalar=comb[:, h, col],
                                                   in1=x[:, h, :], op0=ALU.mult, op1=ALU.add).then_inc(added, 1)
                            e.wait_ge(added, done * 2 + 3 + h)
                    if prev:
                        for k in (10, 11):
                            make_lo(e, group.number(k, i, cur), 1, 1024)
                    if cur:
                        e.wait_ge(used, count_after(group.number(7, i)))
                        e.wait_ge(silu, 1 if isinstance(i, int) and i == 0 else i + 1)
                        v.tensor_tensor(rows[:], s_g[:], bank(1), ALU.mult).then_inc(rows_done, 1)
                    if gathers(cur):
                        e.wait_ge(xg_hi_ok, cur[0] + 1)
                        v.tensor_tensor(xg_lo[:], gathered_psum, xg_hi[:].bitcast(F32), ALU.subtract).then_inc(xg_ok, 1)
                    if i is None:
                        make_los(e, group.next)
                    then_registers(e)
                group.iterations(e, body)
            return first_gather, tensor, scalar, vector
        return programs

    routed = [0]

    def routed_experts(xn):
        place_tokens(N_EXP2 if routed[0] else N_EXP1)
        routed[0] += 1
        group = take_group()
        tag = f"_of_moe{routed[0]}"
        with ExitStack() as st:
            programs, counted = dense_experts(group, lambda h, ex: comb[:, h, slice(ex + 1, ex + 2) if isinstance(ex, int)
                                                                        else bass.ds(ex + 1, 1)], "_dense" + tag)
            dense = programs(st)
            first_gather, *sparse = sparse_experts(group, xn, tag)(st)
            first_gather()
            with stage() as block:
                experts_sync(block, group)

                def either(e, few, many):
                    count = e.value_load(largest[0:1, 0:1], min_val=0, max_val=SEQ)
                    with e.If(count < P + 1):
                        few(e)
                    with e.Else():
                        many(e)

                @block.tensor
                def _(e):
                    either(e, sparse[0], dense[0])

                @block.scalar
                def _(e):
                    either(e, sparse[1], dense[1])

                @block.vector
                def _(e):
                    either(e, sparse[2], dense[2])

    def all_tokens_experts(combine):
        group = take_group()
        with ExitStack() as st:
            programs, counted = dense_experts(group, combine, "")
            tensor, scalar, vector = programs(st)
            with stage() as block:
                experts_sync(block, group)
                block.tensor(tensor)
                block.scalar(scalar)
                block.vector(vector)
        for s in counted:
            s.total += group.steps

    def route(jobs, finish):
        done = S("router_ready")
        with stage() as block:
            sync_stage(block)

            @block.tensor
            def _(e):
                for w, c, n in jobs:
                    for h in range(HALVES):
                        for k in range(KT):
                            for m, part in enumerate(xT):
                                last = pe.matmul(bank(h)[:, c:c + n], part[:, k, h * P:(h + 1) * P].bitcast(F32),
                                                 w[:, k, :], start=(k == 0 and m == 0), stop=(k == KT - 1 and m == 1))
                done.inc(last)

            finish(block, done)

    gain_loaded = S("gain_row_loaded")

    def scale_tokens(e, step, xn, gain_row):
        e.wait_ge(gain_loaded.sem, gain_loaded.total)
        step(v.tensor_tensor(xn[:], xn[:], row_bc(gain_row[:], [HALVES]), ALU.mult))

    logits_psum = psum[:, 0:HALVES * BANK].rearrange("p (h c) -> p h c", h=HALVES)

    def make_step(e):
        dve = S("dve_chain")

        def step(ins, sig=dve):
            sig.inc(ins)
            e.wait_ge(sig.sem, sig.total)
        return step

    def pick(step, scores, n, best, cand, idx, onehot):
        step(v.tensor_reduce(best, scores, AXX, ALU.max))
        step(v.tensor_tensor(cand, scores, last_bc(best, n), ALU.is_equal))
        step(v.scalar_tensor_tensor(out=cand, in0=cand, scalar=-64.0, in1=row_bc(const("iota")[:, 0:n], [HALVES]),
                                    op0=ALU.mult, op1=ALU.add))
        step(v.tensor_reduce(idx, cand, AXX, ALU.min))
        step(v.tensor_tensor(onehot, cand, last_bc(idx, n), ALU.is_equal))

    def top_two_weights(e, step, scores, n, out_w, out_mask, t, other=None):
        best1, best2, idx, cand, one1, one2, left = t
        diff_ready, diff_exp = S("top_two_difference"), S("top_two_exp")
        pick(step, scores, n, best1, cand, idx, one1)
        step(v.scalar_tensor_tensor(out=left, in0=one1, scalar=-3e38, in1=scores, op0=ALU.mult, op1=ALU.add))
        pick(step, left, n, best2, cand, idx, one2)
        step(v.tensor_tensor(out_mask, one1, one2, ALU.add))
        step(v.tensor_tensor(best2, best2, best1, ALU.subtract), diff_ready)
        e.wait_ge(diff_exp.sem, diff_exp.at(1))
        step(v.tensor_scalar(best1, best2, 1.0, None, ALU.add))
        step(v.reciprocal(best1, best1))
        step(v.tensor_tensor(best2, best2, best1, ALU.mult))
        if other is not None:
            step(v.tensor_tensor(best1, best1, other, ALU.mult))
            step(v.tensor_tensor(best2, best2, other, ALU.mult))
        step(v.tensor_tensor(one1, one1, last_bc(best1, n), ALU.mult))
        step(v.tensor_tensor(one2, one2, last_bc(best2, n), ALU.mult))
        step(v.tensor_tensor(out_w, one1, one2, ALU.add))

    def hybrid_mixers(layer, L2):
        loads = []

        def par(name, shape, src):
            t = tmp(L2, name, shape)
            loads.append((t[:], src))
            return t

        qk_gain = par("nsa_gain", [P, 4, HD], A["nsa_qk_gain_2"][layer].rearrange("a d -> (a d)").partition_broadcast(P)
                      .rearrange("p (a d) -> p a d", a=4))
        d_gain = par("diff_gain", [P, 2, DIFF_QK], A["diff_qk_gain_2"][layer].rearrange("a d -> (a d)").partition_broadcast(P)
                     .rearrange("p (a d) -> p a d", a=2))
        lam_p = par("diff_lambda", [P, 4, DIFF_QK], A["diff_lambda_2"][layer].rearrange("a d -> (a d)").partition_broadcast(P)
                    .rearrange("p (a d) -> p a d", a=4))
        d_norm = par("diff_norm", [P, HD], A["diff_norm_2"][layer].partition_broadcast(P))
        w_gate2 = par("gla_w_gate2", [GLA_RANK, MH * GLA_DK], A["gla_w_gate2_2"][layer])
        b_gate = par("gla_b_gate", [P, MH * GLA_DK], A["gla_b_gate_2"][layer].partition_broadcast(P))
        gla_gain = par("gla_gain", [P, HD], A["gla_norm_2"][layer].partition_broadcast(P))
        hg_gain = par("hgrn_gain", [P, HD], A["hgrn_norm_2"][layer].partition_broadcast(P))
        cmp_w2 = par("cmp_w2", [P, 2, 2, HD], A["nsa_cmp_w2_2"][layer].rearrange("j (c p) d -> p j c d", p=P))
        pos = par("cmp_pos", [P, 2, CMP_LEN // 2], A["nsa_cmp_pos_2"][layer])
        u = tmp(L2, "u2", [P, HALVES, IN2_COLS])
        mix = tmp(L2, "mix", [P, HALVES, D])
        lam = tmp(L2, "lam", [P, 2])
        lam_init = 0.8 - 0.6 * math.exp(-0.3 * layer)
        normed_T(x, g_attn2[layer], xT)
        product(xT, KT, IN2_COLS, copy_to=u, loads=loads)

        def uc(name, lo=0, width=None):
            a, w = IN2[name]
            return u[:, :, a + lo:a + (w if width is None else lo + width)]

        def heads_of(ap, d):
            return ap.rearrange("p h (n d) -> p h n d", d=d)

        with ExitStack() as st:
            nq = tmp(st, "nq", [P, HALVES, MH, HD])
            nks = tmp(st, "nks", [P, HALVES, 1, HD])
            nkw = tmp(st, "nkw", [P, HALVES, 1, HD])
            group_norms([(heads_of(uc("nq"), HD), nq[:], qk_gain[:, 0, :], HD),
                         (heads_of(uc("ks"), HD), nks[:], qk_gain[:, 2, :], HD),
                         (heads_of(uc("kw"), HD), nkw[:], qk_gain[:, 3, :], HD)])
            qT = tmp(st, "nqT", [HD, MH + 2, SEQ])
            transposes([nq[:, h, n, :] for n in range(MH) for h in range(HALVES)]
                       + [k[:, h, 0, :] for k in (nks, nkw) for h in range(HALVES)], HD,
                       qT[:].rearrange("p n t -> p (n t)"))
            twice = tmp(st, "kv_twice", [P, HALVES, 2, 2, HD])
            gate = tmp(st, "nsa_gate", [P, HALVES, MH, 3])
            gates, dve = S("gates_ready"), S("dve_chain")
            a0 = IN2["kc"][0]
            with stage() as block:
                sync_stage(block)

                @block.scalar
                def _(e):
                    gates.inc(sc.activation(gate[:], uc("ng").rearrange("p h (n b) -> p h n b", b=3), ACT.Sigmoid))

                @block.vector
                def _(e):
                    for h in range(HALVES):
                        kv = u[:, h, a0:a0 + 2 * HD].rearrange("p (j d) -> p j d", j=2)
                        dve.inc(v.tensor_copy(twice[:, h, :, :, :], kv.unsqueeze(2).to_broadcast([P, 2, 2, HD])))
            kvT = tmp(st, "kvT", [P, 2, SEQ])
            transposes([twice[:, h, j, :, :].rearrange("p c d -> p (c d)") for j in range(2) for h in range(HALVES)], P,
                       kvT[:].rearrange("p j t -> p (j t)"))
            blocks = tmp(st, "cmp_blocks", [P, 2, CMP_LEN // 2, N_CMP])
            blocks_split = tmp_split(st, "cmp_blocks", [P, 2, CMP_LEN // 2, N_CMP])
            hid, hid_e = (tmp(st, n, [N_CMP, 2, CMP_HID]) for n in ("cmp_hid", "cmp_sig"))
            hidT = tmp(st, "cmp_hidT", [P, 4, N_CMP])
            ckv = tmp(st, "ckv", [N_CMP, 2, HD])
            csq, css, crt = tmp(st, "csq", [N_CMP, HD]), tmp(st, "css", [N_CMP, 1]), tmp(st, "crt", [N_CMP, 1])
            ckT = tmp(st, "ckT", [HD, N_CMP])
            got = take(CMP_PIECES)
            to_split = not_early(got) + take_early()
            ready, ready_hi, sig, act_hid, hT, hTc, out2, ssr, root, kn, knT = (S(n) for n in (
                "blocks_ready", "blocks_hi_ready", "hidden_sigmoid", "hidden_active", "hidden_transposed", "hiddenT_copied",
                "compressed_ready", "group_sums", "group_roots", "key_normed", "key_transposed"))
            with stage() as block:
                sync_stage(block)

                @block.vector
                def _(e):
                    step = make_step(e)
                    for odd in range(2):
                        rows = slice(odd * HD, (odd + 1) * HD)
                        half = kvT[rows, :, :]
                        windows = bass.AP(half.tensor, half.offset + odd,
                                          [half.ap[0], [SEQ, 2], [2, CMP_LEN // 2], [CMP_STRIDE, N_CMP]])
                        ready.inc(v.tensor_tensor(blocks[rows], windows, last_bc(pos[rows], N_CMP), ALU.add))
                    e.wait_ge(ready_hi.sem, ready_hi.at(1))
                    ready.inc(v.tensor_tensor(blocks_split[1][:], blocks[:], blocks_split[0][:].bitcast(F32), ALU.subtract))
                    make_los(e, to_split)
                    e.wait_ge(sig.sem, sig.at(2))
                    for j in range(2):
                        last = v.tensor_tensor(hid[:, j, :], bank(j)[0:N_CMP, 0:CMP_HID], hid_e[:, j, :], ALU.mult)
                    act_hid.inc(last)
                    e.wait_ge(hT.sem, hT.at(1))
                    hTc.inc(v.tensor_copy(hidT[:], bank(2)[:, 0:4 * P].rearrange("p (n k) -> p n k", n=4)[:, :, 0:N_CMP]))
                    e.wait_ge(out2.sem, out2.at(1))
                    step(v.tensor_copy(ckv[:], bank(3)[0:N_CMP, 0:2 * HD].rearrange("p (j d) -> p j d", j=2)))
                    step(v.tensor_tensor(csq[:], ckv[:, 0, :], ckv[:, 0, :], ALU.mult))
                    step(v.tensor_reduce(css[:], csq[:], AXX, ALU.add), ssr)
                    e.wait_ge(root.sem, root.at(1))
                    step(v.reciprocal(css[:], crt[:]))
                    step(v.tensor_scalar(csq[:], ckv[:, 0, :], css[:], None, ALU.mult))
                    step(v.tensor_tensor(csq[:], csq[:], qk_gain[0:N_CMP, 1, :], ALU.mult), kn)
                    e.wait_ge(knT.sem, knT.at(1))
                    step(v.tensor_copy(ckT[:], bank(4)[0:HD, 0:N_CMP]))

                @block.scalar
                def _(e):
                    e.wait_ge(ready.sem, ready.at(2))
                    ready_hi.inc(sc.activation(blocks_split[0][:], blocks[:], ACT.Copy))
                    make_his(e, to_split)
                    e.wait_ge(used, got[-1].n + 1)
                    for j in range(2):
                        sig.inc(sc.activation(hid_e[:, j, :], bank(j)[0:N_CMP, 0:CMP_HID], ACT.Sigmoid))
                    e.wait_ge(ssr.sem, ssr.at(1))
                    root.inc(sc.activation(crt[:], css[:], ACT.Sqrt, scale=1.0 / HD, bias=eps[0:N_CMP, :]))

                @block.tensor
                def _(e):
                    e.wait_ge(ready.sem, ready.at(3))
                    for q, p in enumerate(got):
                        e.wait_ge(lo_ready, p.n + 1)
                        w = [raw_view(r, FINE, (p.n, 0), 4, CMP_HID) for r in (ring_hi, ring_lo)]
                        j, r = q // (CMP_PIECES // 2), q % (CMP_PIECES // 2)
                        for a in range(4):
                            pair = 4 * r + a
                            last = three_passes(bank(j)[0:N_CMP, 0:CMP_HID], [b_[:, j, pair, :] for b_ in blocks_split],
                                                [w_[:, a, :] for w_ in w], pair == 0, pair == CMP_LEN // 2 - 1)
                        last.then_inc(used, 1)
                    e.wait_ge(act_hid.sem, act_hid.at(1))
                    for n in range(4):
                        last = pe.transpose(bank(2)[:, n * P:n * P + N_CMP], hid[:, n // 2, (n % 2) * P:(n % 2 + 1) * P],
                                            ident[0:N_CMP, 0:N_CMP])
                    hT.inc(last)
                    e.wait_ge(hTc.sem, hTc.at(1))
                    for j in range(2):
                        for c in range(2):
                            last = pe.matmul(bank(3)[0:N_CMP, j * HD:(j + 1) * HD], hidT[:, 2 * j + c, :], cmp_w2[:, j, c, :],
                                             start=(c == 0), stop=(c == 1))
                    out2.inc(last)
                    e.wait_ge(kn.sem, kn.at(1))
                    knT.inc(pe.transpose(bank(4)[0:HD, 0:N_CMP], csq[:], ident[0:N_CMP, 0:N_CMP]))
            jobs = []
            for h in range(HALVES):
                dst = mix[:, h, 0:MH * HD].rearrange("p (n d) -> p n d", d=HD)

                def weight(b, h=h):
                    return lambda step, r: step(v.tensor_tensor(r, r, gate[:, h, :, b], ALU.mult))
                qs = [qT[:, n, h * P:(h + 1) * P] for n in range(MH)]
                jobs.append(dict(heads=[(q, ckT[:], [ckv[:, 1, :]]) for q in qs], keys=N_CMP, dv=HD, dst=dst,
                                 weight=weight(0), mask=const("cmp_add")[:, h * N_CMP:(h + 1) * N_CMP],
                                 keep=const("cmp_mul")[:, h * N_CMP:(h + 1) * N_CMP]))
                for b, keys, vals in ((1, MH, "vs"), (2, MH + 1, "vw")):
                    n = (h + 1) * P
                    jobs.append(dict(heads=[(q, qT[:, keys, 0:n], [uc(vals)[:, k, :] for k in range(h + 1)]) for q in qs],
                                     keys=n, dv=HD, dst=dst, weight=weight(b), accumulate=True,
                                     mask=const("causal")[:, h * SEQ:h * SEQ + n]))
            attend(jobs, HD ** -0.5)

        with ExitStack() as st:
            n2 = 2 * MH
            dq, dk = (tmp(st, n, [P, HALVES, n2, DIFF_QK]) for n in ("dq", "dk"))
            group_norms([(heads_of(uc("dq"), DIFF_QK), dq[:], d_gain[:, 0, :], DIFF_QK),
                         (heads_of(uc("dk"), DIFF_QK), dk[:], d_gain[:, 1, :], DIFF_QK)])
            dqT, dkT = (tmp(st, n, [DIFF_QK, n2, SEQ]) for n in ("dqT", "dkT"))
            for src, dst in ((dq, dqT), (dk, dkT)):
                transposes([src[:, h, n, :] for n in range(n2) for h in range(HALVES)], DIFF_QK,
                           dst[:].rearrange("p n t -> p (n t)"))
            prod, dots = tmp(st, "lam_prod", [P, 2, DIFF_QK]), tmp(st, "lam_dots", [P, 2])
            dots_ready, exp_ready = S("group_sums"), S("exp_ready")
            with stage() as block:
                sync_stage(block)

                @block.vector
                def _(e):
                    step = make_step(e)
                    pairs = lam_p[:].rearrange("p (a two) d -> p a two d", two=2)
                    step(v.tensor_tensor(prod[:], pairs[:, :, 0, :], pairs[:, :, 1, :], ALU.mult))
                    step(v.tensor_reduce(dots[:], prod[:], AXX, ALU.add), dots_ready)
                    e.wait_ge(exp_ready.sem, exp_ready.at(1))
                    step(v.tensor_tensor(lam[:, 0:1], dots[:, 1:2], dots[:, 0:1], ALU.subtract))
                    step(v.tensor_scalar(lam[:, 0:1], lam[:, 0:1], -lam_init, None, ALU.add))

                @block.scalar
                def _(e):
                    e.wait_ge(dots_ready.sem, dots_ready.at(1))
                    exp_ready.inc(sc.activation(dots[:], dots[:], ACT.Exp))
            o8 = tmp(st, "o8", [P, HALVES, n2, HD])
            def weight(step, r):
                second = r.rearrange("p (n c) -> p n c", c=2)[:, :, 1]
                step(v.tensor_scalar(second, second, lam[:, 0:1], None, ALU.mult))
            attend([dict(heads=[(dqT[:, n, h * P:(h + 1) * P], dkT[:, n, 0:(h + 1) * P],
                                 [uc("dv", (n // 2) * HD, HD)[:, k, :] for k in range(h + 1)]) for n in range(n0, n0 + 4)],
                         keys=(h + 1) * P, dv=HD, dst=o8[:, h, n0:n0 + 4, :], weight=weight,
                         mask=const("causal")[:, h * SEQ:h * SEQ + (h + 1) * P])
                    for h in range(HALVES) for n0 in (0, 4)], DIFF_QK ** -0.5)
            od = tmp(st, "od", [P, HALVES, MH, HD])
            dve = S("dve_chain")
            with stage() as block:
                sync_stage(block)

                @block.vector
                def _(e):
                    for h in range(HALVES):
                        both = o8[:, h, :, :].rearrange("p (n c) d -> p n c d", c=2)
                        dve.inc(v.tensor_tensor(od[:, h, :, :], both[:, :, 0, :], both[:, :, 1, :], ALU.add))
                    dve.inc(v.tensor_scalar(d_norm[:], d_norm[:], 1.0 - lam_init, None, ALU.mult))
            group_norms([(od[:], heads_of(mix[:, :, 256:512], HD), d_norm[:], HD)])

        def linear_attention(q, k, log_g, vals, groups, dk, dst):
            nh = P // dk
            with ExitStack() as st:
                qkT = tmp(st, "qkT", [P, 2, SEQ])
                decay = tmp(st, "decay", [P, N_LEVELS + 1, P])
                QD = tmp(st, "QD", [P, HALVES, N_LEVELS + 2, P])
                KD = tmp(st, "KD", [P, HALVES, N_LEVELS + 2, P])
                pairs = tmp(st, "pairs", [P, N_LEVELS + 1, P])
                summed = tmp(st, "pairs_summed", [P, 2, P])
                cross = tmp(st, "cross", [P, 2, P])
                for g in range(groups):
                    cols = slice(g * P, (g + 1) * P)
                    transposes([a[:, h, cols] for a in (q, k) for h in range(HALVES)], P,
                               qkT[:].rearrange("p a t -> p (a t)"))
                    exps, exped, dve, decayed = S("exponents_ready"), S("exp_ready"), S("dve_chain"), S("decayed")
                    with stage() as block:
                        sync_stage(block)

                        @block.tensor
                        def _(e):
                            for h in range(HALVES):
                                if h:
                                    e.wait_ge(exped.sem, exped.at(h))
                                pe.matmul(bank(0), log_g[:, h, cols], const("gate_sums")[:, 0:4 * P], start=True, stop=True)
                                pe.matmul(bank(1)[:, 0:3 * P], log_g[:, h, cols], const("gate_sums")[:, 4 * P:7 * P],
                                          start=True, stop=True)
                                exps.inc(pe.matmul(bank(1)[:, 3 * P:4 * P], log_g[:, h, cols],
                                                   const("gate_cross")[:, h * P:(h + 1) * P], start=True, stop=True))

                        @block.scalar
                        def _(e):
                            for h in range(HALVES):
                                e.wait_ge(exps.sem, exps.at(h + 1))
                                if h:
                                    e.wait_ge(decayed.sem, decayed.at(h))
                                exped.inc(sc.activation(decay[:].rearrange("p l t -> p (l t)"), bank(0, 2), ACT.Exp))

                        @block.vector
                        def _(e):
                            for h in range(HALVES):
                                tok = slice(h * P, (h + 1) * P)
                                v.tensor_copy(QD[:, h, N_LEVELS + 1, :], qkT[:, 0, tok])
                                dve.inc(v.tensor_copy(KD[:, h, N_LEVELS + 1, :], qkT[:, 1, tok]))
                                e.wait_ge(exped.sem, exped.at(h + 1))
                                for a, to in ((0, QD), (1, KD)):
                                    last = v.tensor_tensor(to[:, h, 0:N_LEVELS + 1, :], decay[:],
                                                           row_bc(qkT[:, a, tok], [N_LEVELS + 1]), ALU.mult)
                                decayed.inc(last)
                    in_half = [*range(N_LEVELS), N_LEVELS + 1]
                    ready, masked, sums, masked_a, o, taken_o = (S(n) for n in (
                        "pairs_ready", "pairs_masked", "pairs_summed", "cross_copied", "attended", "output_copied"))
                    jobs = [(h, n) for h in range(HALVES) for n in range(nh)]
                    with stage() as block:
                        sync_stage(block)

                        @block.tensor
                        def _(e):
                            def pv(m):
                                h, n = jobs[m]
                                e.wait_ge(sums.sem, sums.at(m + 1))
                                if h:
                                    e.wait_ge(masked_a.sem, masked_a.at(m - nh + 1))
                                if m >= 2:
                                    e.wait_ge(taken_o.sem, taken_o.at(m - 1))
                                to = bank(6 + m % 2)[:, 0:HD]
                                va = [vals[:, hh, (g * nh + n) * HD:(g * nh + n + 1) * HD] for hh in range(HALVES)]
                                last = pe.matmul(to, summed[:, m % 2, :], va[h], start=True, stop=(h == 0))
                                if h:
                                    last = pe.matmul(to, cross[:, m % 2, :], va[0], start=False, stop=True)
                                o.inc(last)

                            for m, (h, n) in enumerate(jobs):
                                ch = slice(n * dk, (n + 1) * dk)
                                if m >= 2:
                                    e.wait_ge(masked.sem, masked.at(m - 1))
                                    if h and m - 2 >= nh:
                                        e.wait_ge(masked_a.sem, masked_a.at(m - 1 - nh))
                                for s, l in enumerate(in_half):
                                    last = pe.matmul(psum[:, (m % 2) * 2 * BANK + s * P:(m % 2) * 2 * BANK + (s + 1) * P],
                                                     KD[ch, h, l, :], QD[ch, h, l, :], start=True, stop=True)
                                if h:
                                    last = pe.matmul(bank(4 + m % 2)[:, 0:P], KD[ch, 0, N_LEVELS, :],
                                                     QD[ch, 1, N_LEVELS, :], start=True, stop=True)
                                ready.inc(last)
                                if m:
                                    pv(m - 1)
                            pv(len(jobs) - 1)

                        @block.vector
                        def _(e):
                            def take_out(m):
                                h, n = jobs[m]
                                e.wait_ge(o.sem, o.at(m + 1))
                                taken_o.inc(v.tensor_copy(dst[:, h, g * nh + n, :], bank(6 + m % 2)[:, 0:HD]))

                            for m, (h, n) in enumerate(jobs):
                                e.wait_ge(ready.sem, ready.at(m + 1))
                                if m >= 2:
                                    e.wait_ge(o.sem, o.at(m - 1))
                                masked.inc(v.tensor_tensor(
                                    pairs[:].rearrange("p l t -> p (l t)"),
                                    psum[:, (m % 2) * 2 * BANK:(m % 2 + 1) * 2 * BANK], const("level_mask"), ALU.mult))
                                e.wait_ge(masked.sem, masked.total)
                                sums.inc(v.tensor_reduce(summed[:, m % 2, :], pairs[:].rearrange("p l t -> p t l"),
                                                         AXX, ALU.add))
                                e.wait_ge(sums.sem, sums.total)
                                if m:
                                    take_out(m - 1)
                            take_out(len(jobs) - 1)

                        @block.scalar
                        def _(e):
                            for m, (h, n) in enumerate(jobs):
                                if h:
                                    e.wait_ge(ready.sem, ready.at(m + 1))
                                    if m >= 2:
                                        e.wait_ge(o.sem, o.at(m - 1))
                                    masked_a.inc(sc.activation(cross[:, m % 2, :], bank(4 + m % 2)[:, 0:P], ACT.Copy))

        def gated_output(o, gain, gate_name, dst):
            sig, dve = S("gates_ready"), S("dve_chain")
            with ExitStack() as st:
                sg = tmp(st, "sg", [P, HALVES, MH * HD])
                group_norms([(o[:], heads_of(dst, HD), gain[:], HD)])
                with stage() as block:
                    sync_stage(block)

                    @block.scalar
                    def _(e):
                        sig.inc(sc.activation(sg[:], uc(gate_name), ACT.Silu))

                    @block.vector
                    def _(e):
                        e.wait_ge(sig.sem, sig.at(1))
                        dve.inc(v.tensor_tensor(dst, dst, sg[:], ALU.mult))

        with ExitStack() as st:
            gT = tmp(st, "glrT", [GLA_RANK, SEQ])
            transposes([uc("glr")[:, h, :] for h in range(HALVES)], GLA_RANK, gT[:])
            lg, ab, mn = (tmp(st, n, [P, HALVES, MH * GLA_DK]) for n in ("lg", "gabs", "gmin"))
            pre, abs_ready, log_ready = S("router_ready"), S("gate_abs"), S("gate_log")
            with stage() as block:
                sync_stage(block)

                @block.tensor
                def _(e):
                    for h in range(HALVES):
                        last = pe.matmul(bank(h)[:, 0:P], gT[:, h * P:(h + 1) * P], w_gate2[:], start=True, stop=True)
                    pre.inc(last)

                @block.vector
                def _(e):
                    step = make_step(e)
                    e.wait_ge(pre.sem, pre.at(1))
                    step(v.tensor_tensor(lg[:], logits_psum[:, :, 0:P], row_bc(b_gate[:], [HALVES]), ALU.add))
                    step(v.tensor_scalar(mn[:], lg[:], 0.0, 1.0 / GLA_TAU, ALU.min, ALU.mult))
                    step(v.scalar_tensor_tensor(out=ab[:], in0=lg[:], scalar=-1.0, in1=lg[:], op0=ALU.mult, op1=ALU.max), abs_ready)
                    e.wait_ge(log_ready.sem, log_ready.at(1))
                    step(v.scalar_tensor_tensor(out=lg[:], in0=ab[:], scalar=-1.0 / GLA_TAU, in1=mn[:],
                                                op0=ALU.mult, op1=ALU.add))
                    step(v.tensor_scalar(uc("gq"), uc("gq"), GLA_DK ** -0.5, None, ALU.mult))

                @block.scalar
                def _(e):
                    act = S("act_chain")
                    e.wait_ge(abs_ready.sem, abs_ready.at(1))
                    act.inc(sc.activation(ab[:], ab[:], ACT.Exp, scale=-1.0))
                    e.wait_ge(act.sem, act.total)
                    log_ready.inc(sc.activation(ab[:], ab[:], ACT.Ln, scale=1.0, bias=const("all_ones")[:, 0:1]))
            o = tmp(st, "o_gla", [P, HALVES, MH, HD])
            linear_attention(uc("gq"), uc("gk"), lg, uc("gv"), 1, GLA_DK, o)
            gated_output(o, gla_gain, "gog", mix[:, :, 512:768])

        with ExitStack() as st:
            f, k1 = (tmp(st, n, [P, HALVES, MH * HD]) for n in ("forget", "hkeys"))
            lb, top = (tmp(st, n, [P, MH * HD]) for n in ("lower_bound", "lb_max"))
            ex = tmp(st, "lb_exp", [P, LAYERS, MH * HD])
            sig, lb_ready, lb_exp, f_ready, log_ready = (S(n) for n in (
                "gates_ready", "bounds_max_ready", "bounds_exp", "forget_ready", "gate_log"))
            with stage() as block:
                sync_stage(block)

                @block.scalar
                def _(e):
                    if layer:
                        e.wait_ge(lb_ready.sem, lb_ready.at(1))
                        lb_exp.inc(sc.activation(ex[:], ex[:], ACT.Exp))
                    sc.activation(f[:], uc("rf"), ACT.Sigmoid)
                    sig.inc(sc.activation(k1[:], uc("rf"), ACT.Sigmoid, scale=-1.0))
                    e.wait_ge(f_ready.sem, f_ready.at(1))
                    log_ready.inc(sc.activation(f[:], f[:], ACT.Ln))

                @block.vector
                def _(e):
                    step = make_step(e)
                    if layer:
                        step(v.tensor_tensor(top[:], hg_logits[:, 0, :], hg_logits[:, 1, :], ALU.max))
                        step(v.tensor_tensor(ex[:], hg_logits[:], row_bc(top[:], [LAYERS]), ALU.subtract), lb_ready)
                        e.wait_ge(lb_exp.sem, lb_exp.at(1))
                        step(v.tensor_tensor(top[:], ex[:, 0, :], ex[:, 1, :], ALU.add))
                        step(v.reciprocal(top[:], top[:]))
                        step(v.tensor_tensor(lb[:], ex[:, 1, :], top[:], ALU.mult))
                        step(v.tensor_scalar(top[:], lb[:], -1.0, 1.0, ALU.mult, ALU.add))
                    e.wait_ge(sig.sem, sig.at(1))
                    if layer:
                        for a in (f, k1):
                            step(v.tensor_tensor(a[:], a[:], row_bc(top[:], [HALVES]), ALU.mult))
                        step(v.tensor_tensor(f[:], f[:], row_bc(lb[:], [HALVES]), ALU.add))
                    step(v.tensor_scalar(f[:], f[:], 2.0 ** -63, None, ALU.max), f_ready)
                    e.wait_ge(log_ready.sem, log_ready.at(1))
                    step(v.tensor_scalar(f[:], f[:], 0.0, None, ALU.min))
            o = tmp(st, "o_hgrn", [P, HALVES, MH, HD])
            linear_attention(uc("rq"), k1, f, uc("ri"), 2, HD, o)
            gated_output(o, hg_gain, "rog", mix[:, :, 768:1024])

        transposes([mix[:, h, k * P:(k + 1) * P] for k in range(KT) for h in range(HALVES)], P,
                   flat(xT))
        product(xT, KT, D, add_to=x)

    with stage() as block:
        @block.sync
        def _(sp):
            for dst, src in small[:3]:
                params_loaded.inc(sp.dma_start(dst, src), 16)
            sp.wait_ge(params_loaded.sem, params_loaded.total)

    comb, chosen, place = (sb(n, [P, HALVES, N_EXP1 + 2]) for n in ("comb", "chosen", "place"))
    largest = ctx.enter_context(nc.sbuf_tensor("largest_count", [P, 1], mybir.dt.int32))

    def clear_routing(gain_row, src):
        with stage() as block:
            @block.sync
            def _(sp):
                gain_loaded.inc(sp.dma_start(gain_row[:], src.partition_broadcast(P)), 16)
                issue_loads(sp)
            dve = S("dve_chain")

            @block.vector
            def _(e):
                for t in (comb, chosen, place):
                    last = v.memset(t[:], 0.0)
                v.memset(bank(3, 2), 0.0)
                dve.inc(last)

    def place_tokens(n):
        counted, dve = S("tokens_counted"), S("dve_chain")
        with ExitStack() as st:
            top = tmp(st, "top_count", [P, 1])
            with stage() as block:
                sync_stage(block)

                @block.tensor
                def _(e):
                    before, ones = const("before"), const("all_ones")
                    m = [chosen[:, h, 1:n + 1] for h in range(HALVES)]
                    pe.matmul(bank(0)[:, 0:n], before, m[0], start=True, stop=True)
                    pe.matmul(bank(1)[:, 0:n], before, m[1], start=True, stop=False)
                    pe.matmul(bank(1)[:, 0:n], ones, m[0], start=False, stop=True)
                    pe.matmul(bank(2)[:, 0:n], ones, m[0], start=True, stop=False)
                    counted.inc(pe.matmul(bank(2)[:, 0:n], ones, m[1], start=False, stop=True))

                @block.vector
                def _(e):
                    step = make_step(e)
                    e.wait_ge(counted.sem, counted.at(1))
                    step(v.tensor_copy(place[:, :, 1:n + 1], logits_psum[:, :, 0:n]))
                    step(v.tensor_reduce(top[:], bank(2)[:, 0:n], AXX, ALU.max))
                    step(v.tensor_copy(largest[:], top[:]))

    with ExitStack() as L1:
        z = tmp(L1, "z", [P, HALVES, IN1_COLS])
        normed_T(x, g_mix, xT)
        product(xT, KT, IN1_COLS, copy_to=z, loads=small[3:])

        def zc(name, lo=0, width=None):
            a, w = IN1[name]
            return z[:, :, a + lo:a + (w if width is None else lo + width)]

        y_att = tmp(L1, "y_att", [P, HALVES, D])
        with ExitStack() as st:
            qn, kn = (zc(n).rearrange("p h (n d) -> p h n d", d=HD) for n in ("q", "k"))
            group_norms([(qn, qn, g_q[:], HD), (kn, kn, g_k[:], HD)])
            qr = tmp(st, "qr", [P, HALVES, ATT_HEADS, HD])
            kr = tmp(st, "kr", [P, HALVES, ATT_KV, HD])
            t1 = tmp(st, "t1", [P, ATT_HEADS, HD // 2])
            t2 = tmp(st, "t2", [P, ATT_HEADS, HD // 2])
            with stage() as block:
                sync_stage(block)

                @block.vector
                def _(e):
                    step = make_step(e)
                    for src, dst, nh in ((qn, qr, ATT_HEADS), (kn, kr, ATT_KV)):
                        for h in range(HALVES):
                            x0, x1 = (src[:, h, :, :].rearrange("p n (d two) -> p n d two", two=2)[:, :, :, i] for i in range(2))
                            o0, o1 = (dst[:, h, :, :].rearrange("p n (d two) -> p n d two", two=2)[:, :, :, i] for i in range(2))
                            cos = row_bc(const("cos")[:, h * 32:(h + 1) * 32], [nh])
                            sin = row_bc(const("sin")[:, h * 32:(h + 1) * 32], [nh])
                            step(v.tensor_tensor(t1[:, 0:nh, :], x0, cos, ALU.mult))
                            step(v.tensor_tensor(t2[:, 0:nh, :], x1, sin, ALU.mult))
                            step(v.tensor_tensor(o0, t1[:, 0:nh, :], t2[:, 0:nh, :], ALU.subtract))
                            step(v.tensor_tensor(t1[:, 0:nh, :], x0, sin, ALU.mult))
                            step(v.tensor_tensor(t2[:, 0:nh, :], x1, cos, ALU.mult))
                            step(v.tensor_tensor(o1, t1[:, 0:nh, :], t2[:, 0:nh, :], ALU.add))
            qT = tmp(st, "qT", [HD, ATT_HEADS, SEQ])
            kT = tmp(st, "kT", [HD, ATT_KV, SEQ])
            transposes([qr[:, h, n, :] for n in range(ATT_HEADS) for h in range(HALVES)], HD,
                       qT[:].rearrange("p n t -> p (n t)"))
            transposes([kr[:, h, n, :] for n in range(ATT_KV) for h in range(HALVES)], HD,
                       kT[:].rearrange("p n t -> p (n t)"))
            att = tmp(st, "att", [P, HALVES, ATT_HEADS, HD])
            attend([dict(heads=[(qT[:, n, h * P:(h + 1) * P], kT[:, g, :],
                                 [zc("v", g * HD, HD)[:, k, :] for k in range(HALVES)]) for n in range(4 * g, 4 * g + 4)],
                         keys=SEQ, dv=HD, dst=att[:, h, 4 * g:4 * g + 4, :])
                    for h in range(HALVES) for g in range(ATT_KV)], HD ** -0.5)
            attT = tmp_split(st, "attT", [P, 4, SEQ])
            att_rows = att[:].rearrange("p h n d -> p h (n d)")
            transposes([att_rows[:, h, k * P:(k + 1) * P] for k in range(4) for h in range(HALVES)], P,
                       flat(attT))
            product(attT, 4, D, copy_to=y_att)

        y_sgu = tmp(L1, "y_sgu", [P, HALVES, D])
        with ExitStack() as st:
            sgu_ln_g = tmp(st, "sgu_g", [P, SGU_W])
            sgu_ln_b = tmp(st, "sgu_b", [P, SGU_W])
            w_sT = tmp(st, "w_sT", [P, SGU_G, P])
            u = tmp(st, "u", [P, HALVES, SGU_W])
            vn = tmp(st, "vn", [P, HALVES, SGU_W])
            sq = tmp(st, "sgu_sq", [P, HALVES, SGU_W])
            mean, var, rt = (tmp(st, n, [P, HALVES]) for n in ("mean", "var", "rt"))
            gelu, var_ready, root = S("gelu_ready"), S("group_sums"), S("group_roots")
            with stage() as block:
                @block.sync
                def _(sp):
                    for dst, src in ((sgu_ln_g[:], A["sgu_ln_g"][0].partition_broadcast(P)),
                                     (sgu_ln_b[:], A["sgu_ln_b"][0].partition_broadcast(P)),
                                     (w_sT[:], A["w_s"][0].rearrange("g q p -> q g p"))):
                        params_loaded.inc(sp.dma_start(dst, src), 16)
                    issue_loads(sp)

                @block.scalar
                def _(e):
                    gelu.inc(sc.activation(vn[:], zc("sv"), ACT.Gelu_apprx_tanh))
                    gelu.inc(sc.activation(u[:], zc("su"), ACT.Gelu_apprx_tanh))
                    e.wait_ge(var_ready.sem, var_ready.at(1))
                    root.inc(sc.activation(rt[:], var[:], ACT.Sqrt, scale=1.0 / SGU_W, bias=eps))

                @block.vector
                def _(e):
                    step = make_step(e)
                    e.wait_ge(gelu.sem, gelu.at(1))
                    step(v.tensor_reduce(mean[:], vn[:], AXX, ALU.add))
                    step(v.tensor_scalar(mean[:], mean[:], 1.0 / SGU_W, None, ALU.mult))
                    step(v.tensor_tensor(vn[:], vn[:], last_bc(mean[:], SGU_W), ALU.subtract))
                    step(v.tensor_tensor(sq[:], vn[:], vn[:], ALU.mult))
                    step(v.tensor_reduce(var[:], sq[:], AXX, ALU.add), var_ready)
                    e.wait_ge(root.sem, root.at(1))
                    step(v.reciprocal(var[:], rt[:]))
                    step(v.tensor_tensor(vn[:], vn[:], last_bc(var[:], SGU_W), ALU.mult))
                    e.wait_ge(params_loaded.sem, params_loaded.at(48))
                    step(v.tensor_tensor(vn[:], vn[:], row_bc(sgu_ln_g[:], [HALVES]), ALU.mult))
                    step(v.tensor_tensor(vn[:], vn[:], row_bc(sgu_ln_b[:], [HALVES]), ALU.add))
            mixed, dve = S("tokens_mixed"), S("dve_chain")
            with stage() as block:
                sync_stage(block)

                @block.tensor
                def _(e):
                    for h in range(HALVES):
                        for g in range(SGU_G):
                            last = pe.matmul(bank(h)[:, g * P:(g + 1) * P], w_sT[:, g, :], vn[:, h, g * P:(g + 1) * P],
                                             start=True, stop=True)
                        mixed.inc(last)

                @block.vector
                def _(e):
                    for h in range(HALVES):
                        e.wait_ge(mixed.sem, mixed.at(h + 1))
                        for g in range(SGU_G):
                            uu = u[:, h, g * P:(g + 1) * P]
                            last = v.scalar_tensor_tensor(out=uu, in0=bank(h)[:, g * P:(g + 1) * P], scalar=b_s[:, g:g + 1],
                                                          in1=uu, op0=ALU.add, op1=ALU.mult)
                        dve.inc(last)
            uT = tmp_split(st, "uT", [P, 4, SEQ])
            transposes([u[:, h, k * P:(k + 1) * P] for k in range(4) for h in range(HALVES)], P,
                       flat(uT))
            product(uT, 4, D, copy_to=y_sgu)

        gates, dve = S("gates_ready"), S("dve_chain")
        with stage() as block:
            sync_stage(block)

            @block.scalar
            def _(e):
                for n in ("ga", "gb"):
                    gates.inc(sc.activation(zc(n), zc(n), ACT.Sigmoid))

            @block.vector
            def _(e):
                step = make_step(e)
                e.wait_ge(gates.sem, gates.at(1))
                step(v.tensor_tensor(y_att[:], y_att[:], zc("ga"), ALU.mult))
                e.wait_ge(gates.sem, gates.at(2))
                step(v.tensor_tensor(y_sgu[:], y_sgu[:], zc("gb"), ALU.mult))
                step(v.tensor_tensor(y_att[:], y_att[:], y_sgu[:], ALU.add))
        transposes([y_att[:, h, k * P:(k + 1) * P] for k in range(KT) for h in range(HALVES)], P,
                   flat(xT))
        product(xT, KT, D, add_to=x)

    with ExitStack() as st:
        mem = tmp(st, "mem", [P, HALVES, D])
        memT = tmp_split(st, "memT", [P, KT, SEQ])
        normed_T(x, g_cross, xT)
        cqT, ckT = tmp(st, "cqT", [P, X_HEADS, SEQ]), tmp(st, "ckT", [P, X_HEADS, SEQ])
        cv = tmp(st, "cv", [P, HALVES, X_HEADS * X_HD])
        product_T(xT, cqT, loads=[(mem[:], A["mem"][0].rearrange("(h p) d -> p h d", p=P))])
        normed_T(mem, g_mem, memT)
        product_T(memT, ckT)
        product(memT, KT, X_HEADS * X_HD, copy_to=cv)
        catt = tmp(st, "catt", [P, HALVES, X_HEADS, X_HD])
        attend([dict(heads=[(cqT[:, n, h * P:(h + 1) * P], ckT[:, n, :],
                             [cv[:, k, n * X_HD:(n + 1) * X_HD] for k in range(HALVES)]) for n in range(n0, n0 + 2)],
                     keys=SEQ, dv=X_HD, dst=catt[:, h, n0:n0 + 2, :])
                for h in range(HALVES) for n0 in (0, 2)], X_HD ** -0.5)
        cT = tmp_split(st, "cT", [P, 4, SEQ])
        transposes([catt[:, h, k, :] for k in range(4) for h in range(HALVES)], P, flat(cT))
        product(cT, 4, D, add_to=x)

    moe_x = ExitStack()
    xn = tmp(moe_x, "xn_moe", [P, HALVES, D])
    gain_row = tmp(moe_x, "gain_row", [P, D])
    clear_routing(gain_row, A["g_moe_row"][0])
    normed_T(x, g_moe, xT, xn)
    with ExitStack() as st:
        gl, goh = tmp(st, "gl", [P, HALVES, N_GROUPS]), tmp(st, "goh", [P, HALVES, N_GROUPS])
        ge = tmp(st, "ge", [P, HALVES, N_GROUPS])
        el = tmp(st, "el", [P, HALVES, N_EXP1])
        sel, c4, m4 = (tmp(st, n, [P, HALVES, PER_GROUP]) for n in ("sel", "c4", "m4"))
        gbest, gsum = tmp(st, "gbest", [P, HALVES]), tmp(st, "gsum", [P, HALVES])
        t = [tmp(st, n, [P, HALVES]) for n in ("best1", "best2", "idx")] + \
            [tmp(st, n, [P, HALVES, PER_GROUP]) for n in ("cand", "one1", "one2", "left")]
        t = [a[:] for a in t]

        def finish(block, done):
            gshift, gexp = S("group_logits_max_ready"), S("group_exp_ready")
            diff_ready, diff_exp = S("top_two_difference"), S("top_two_exp")

            @block.vector
            def _(e):
                step = make_step(e)
                scale_tokens(e, step, xn, gain_row)
                e.wait_ge(done.sem, done.at(1))
                step(v.tensor_tensor(gl[:], logits_psum[:, :, 0:N_GROUPS], row_bc(b_rg[:], [HALVES]), ALU.add))
                step(v.tensor_tensor(el[:], logits_psum[:, :, 16:16 + N_EXP1], row_bc(b_re[:], [HALVES]), ALU.add))
                pick(step, gl[:], N_GROUPS, gbest[:], t[3], t[2], goh[:])
                step(v.tensor_tensor(ge[:], gl[:], last_bc(gbest[:], N_GROUPS), ALU.subtract), gshift)
                by_group = el[:].rearrange("p h (g e) -> p h g e", g=N_GROUPS)
                step(v.tensor_tensor(by_group, by_group, last_bc(goh[:], PER_GROUP), ALU.mult))
                step(v.tensor_reduce(sel[:], el[:].rearrange("p h (g e) -> p h e g", g=N_GROUPS), AXX, ALU.add))
                e.wait_ge(gexp.sem, gexp.at(1))
                step(v.tensor_reduce(gsum[:], ge[:], AXX, ALU.add))
                step(v.reciprocal(gsum[:], gsum[:]))
                top_two_weights(e, step, sel[:], PER_GROUP, c4[:], m4[:], t, other=gsum[:])
                for out_, in_ in ((comb, c4), (chosen, m4)):
                    step(v.tensor_tensor(out_[:, :, 1:1 + N_EXP1].rearrange("p h (g e) -> p h g e", g=N_GROUPS),
                                         in_[:].unsqueeze(2).to_broadcast([P, HALVES, N_GROUPS, PER_GROUP]),
                                         last_bc(goh[:], PER_GROUP), ALU.mult))

            @block.scalar
            def _(e):
                e.wait_ge(gshift.sem, gshift.at(1))
                gexp.inc(sc.activation(ge[:], ge[:], ACT.Exp))
                e.wait_ge(diff_ready.sem, diff_ready.at(1))
                diff_exp.inc(sc.activation(t[1], t[1], ACT.Exp))

        route([(w_rg, 0, N_GROUPS), (w_re, 16, N_EXP1)], finish)
    routed_experts(xn)
    moe_x.close()

    with ExitStack() as st:
        g_final = tmp(st, "g_final", [P, D])
        junk = tmp(st, "junk", [P, HALVES, D])
        ss, rms, rinv = (tmp(st, n, [P, HALVES]) for n in ("ss", "rms", "rinv"))
        with stage() as block:
            @block.sync
            def _(sp):
                params_loaded.inc(sp.dma_start(g_final[:], A["g_final"].partition_broadcast(P)), 16)
                issue_loads(sp)
            row_rms(block, x, rinv, junk, ss[:], rms[:])
            rms_done = S("rms_done")

            @block.vector
            def _(e):
                step = make_step(e)
                e.wait_ge(rms_done.sem, rms_done.at(1))
                step(v.reciprocal(rinv[:], rms[:]))
                e.wait_ge(params_loaded.sem, params_loaded.at(16))
                for h in range(HALVES):
                    step(v.scalar_tensor_tensor(out=x[:, h, :], in0=x[:, h, :], scalar=rinv[:, h:h + 1],
                                                in1=g_final[:], op0=ALU.mult, op1=ALU.mult))

    for layer in range(LAYERS):
        with ExitStack() as L2:
            hybrid_mixers(layer, L2)

        moe_x = ExitStack()
        xn = tmp(moe_x, "xn_moe", [P, HALVES, D])
        if layer % 2:
            gain_row = tmp(moe_x, "gain_row", [P, D])
            clear_routing(gain_row, A["norm_ffn_2_row"][layer])
        normed_T(x, g_ffn2[layer], xT, xn)
        if layer % 2 == 0:
            all_tokens_experts(lambda h, ex: const("all_ones")[:, 0:1])
        else:
            with ExitStack() as st:
                lg = tmp(st, "lg", [P, HALVES, N_EXP2])
                t = [tmp(st, n, [P, HALVES]) for n in ("best1", "best2", "idx")] + \
                    [tmp(st, n, [P, HALVES, N_EXP2]) for n in ("cand", "one1", "one2", "left")]
                t = [a[:] for a in t]

                def finish(block, done):
                    diff_ready, diff_exp = S("top_two_difference"), S("top_two_exp")

                    @block.vector
                    def _(e):
                        step = make_step(e)
                        scale_tokens(e, step, xn, gain_row)
                        e.wait_ge(done.sem, done.at(1))
                        step(v.tensor_copy(lg[:], logits_psum[:, :, 0:N_EXP2]))
                        top_two_weights(e, step, lg[:], N_EXP2, comb[:, :, 1:1 + N_EXP2], chosen[:, :, 1:1 + N_EXP2], t)

                    @block.scalar
                    def _(e):
                        e.wait_ge(diff_ready.sem, diff_ready.at(1))
                        diff_exp.inc(sc.activation(t[1], t[1], ACT.Exp))

                route([(router2, 0, N_EXP2)], finish)
            routed_experts(xn)
        moe_x.close()

        with ExitStack() as st:
            pr = tmp(st, "pr", [P, HALVES, PLE])
            proj, gate = tmp(st, "proj", [P, HALVES, D]), tmp(st, "gate", [P, HALVES, D])
            normed_T(x, g_ple2[layer], xT)
            product(xT, KT, D, copy_to=gate,
                    loads=[(pr[:], A["p_2"][layer, 0].rearrange("(h p) d -> p h d", p=P))])
            pT = tmp_split(st, "pT", [P, PLE // P, SEQ])
            transposes([pr[:, h, k * P:(k + 1) * P] for k in range(PLE // P) for h in range(HALVES)], P,
                       flat(pT))
            product(pT, PLE // P, D, copy_to=proj)
            gates = S("gates_ready")
            with stage() as block:
                sync_stage(block)

                @block.scalar
                def _(e):
                    gates.inc(sc.activation(gate[:], gate[:], ACT.Sigmoid))

                @block.vector
                def _(e):
                    step = make_step(e)
                    e.wait_ge(gates.sem, gates.at(1))
                    step(v.tensor_tensor(gate[:], gate[:], proj[:], ALU.mult))
                    step(v.tensor_tensor(x[:], x[:], gate[:], ALU.add))

    stored = S("output_stored")
    with stage() as block:
        @block.sync
        def _(sp):
            stored.inc(sp.dma_start(out[0].rearrange("(h p) d -> p h d", p=P), x[:]), 16)
            sp.wait_ge(stored.sem, stored.total)


_INS = ["x", "mem", "g_mix", "w_in", "g_q", "g_k", "w_att_out", "sgu_ln_g", "sgu_ln_b", "w_s", "b_s",
        "w_sgu_out", "w_out", "g_cross", "g_mem", "w_cq", "w_ckv", "w_co", "g_moe", "w_rg", "b_rg", "w_re",
        "b_re", "w_gate", "w_up", "w_down", "g_final", "p_2", "norm_attn_2", "w_in_2", "w_out_2",
        "nsa_cmp_pos_2", "nsa_cmp_w1_2", "nsa_cmp_w2_2", "nsa_qk_gain_2", "diff_qk_gain_2", "diff_lambda_2",
        "diff_norm_2", "gla_w_gate2_2", "gla_b_gate_2", "gla_norm_2", "hgrn_lb_logits_2", "hgrn_norm_2",
        "norm_ffn_2", "ffn_w_gate_2", "ffn_w_up_2", "ffn_w_down_2", "moe_router_2", "moe_w_gate_2",
        "moe_w_up_2", "moe_w_down_2", "ple_norm_2", "ple_w_gate_2", "ple_w_proj_2"]

_TILED_GAINS = ("g_mix", "g_cross", "g_mem", "g_moe", "norm_attn_2", "norm_ffn_2", "ple_norm_2")
_LAST_TWO_SWAPPED = ("b_s", "w_s")


def kernel(**inputs):
    import numpy as _np
    import concourse.bacc as _bacc
    from concourse import mybir as _mybir
    from concourse.bass_utils import run_bass_kernel_spmd as _run

    nc = _bacc.Bacc("TRN2", target_bir_lowering=False, num_devices=1)
    arrays, aps = {}, {}
    for name in _INS:
        a = _np.asarray(inputs[name])
        if name in _TILED_GAINS:
            a = a.reshape(a.shape[0], KT, P).transpose(0, 2, 1)
        elif name == "nsa_cmp_pos_2":
            a = a.reshape(LAYERS, 2, CMP_LEN // 2, 2, HD).transpose(0, 3, 4, 1, 2).reshape(LAYERS, P, 2, CMP_LEN // 2)
        elif name in _LAST_TWO_SWAPPED:
            a = a.swapaxes(-1, -2)
        if name in ("g_moe", "norm_ffn_2"):
            row = _np.asarray(inputs[name])
            arrays[f"in_{name}_row_dram"] = row
            aps[name + "_row"] = nc.dram_tensor(f"in_{name}_row_dram", row.shape, _mybir.dt.from_np(row.dtype),
                                                kind="ExternalInput").ap()
        a = _np.ascontiguousarray(a)
        arrays[f"in_{name}_dram"] = a
        aps[name] = nc.dram_tensor(f"in_{name}_dram", a.shape, _mybir.dt.from_np(a.dtype), kind="ExternalInput").ap()
    cols, values = shape_constants()
    arrays["shape_constants"] = values
    consts = nc.dram_tensor("shape_constants", values.shape, _mybir.dt.float32, kind="ExternalInput").ap()
    out = nc.dram_tensor("out_dram", (1, SEQ, D), _mybir.dt.float32, kind="ExternalOutput").ap()
    fused_layers(nc, aps, consts, cols, out)
    r = _run(nc, [arrays], core_ids=[0])
    return r.results[0]["out_dram"]
```
